# Optimizing a Trainium2 kernel written in Bass

```python
import math
import jax, jax.numpy as jnp
from jax import lax
import numpy as np

D_MODEL = 1024
BATCH = 1
SEQ = 512
DEPTH = 2

MEM_LEN = 256
EPS = 1e-6
ROPE_THETA = 500000.0
Q_BLOCK = 128

DIFF_HEADS = 8
DIFF_HEAD_DIM = 64
DIFF_V_DIM = 2 * DIFF_HEAD_DIM
DIFF_ROT_DIM = DIFF_HEAD_DIM // 4
DIFF_QK_WIDTH = DIFF_HEADS * 2 * DIFF_HEAD_DIM
DIFF_V_WIDTH = DIFF_HEADS * DIFF_V_DIM
DIFF_LAMBDA_STD = 0.1

MLA_HEADS = 8
MLA_Q_LORA = 512
MLA_KV_LORA = 256
MLA_NOPE_DIM = 64
MLA_ROPE_DIM = 32
MLA_V_DIM = 64
MLA_QK_DIM = MLA_NOPE_DIM + MLA_ROPE_DIM
MLA_V_WIDTH = MLA_HEADS * MLA_V_DIM

CROSS_HEADS = 4
CROSS_HEAD_DIM = 128
CROSS_WIDTH = CROSS_HEADS * CROSS_HEAD_DIM

N_BRANCHES = 3
FFN_HIDDEN = -(-8 * D_MODEL // (3 * 256)) * 256

IN_SIZES = (DIFF_QK_WIDTH, DIFF_QK_WIDTH, DIFF_V_WIDTH, MLA_Q_LORA, MLA_KV_LORA, MLA_ROPE_DIM, CROSS_WIDTH, N_BRANCHES * D_MODEL)
IN_COLS = sum(IN_SIZES)
IN_SPLIT_POINTS = tuple(sum(IN_SIZES[:j + 1]) for j in range(len(IN_SIZES) - 1))

kernel_name = "hybrid_diffattn_mla_memxattn_gated_trunk"

def rms_norm(x, w):
    xf = x.astype(jnp.float32)
    y = xf * lax.rsqrt(jnp.mean(xf * xf, axis=-1, keepdims=True) + EPS)
    return (y * w.astype(jnp.float32)).astype(x.dtype)

def apply_rope(x, positions, rot_dim):
    half = rot_dim // 2
    inv_freq = ROPE_THETA ** (-jnp.arange(half, dtype=jnp.float32) * 2.0 / rot_dim)
    ang = positions.astype(jnp.float32)[..., None] * inv_freq
    cos = jnp.cos(ang)[:, :, None, :]
    sin = jnp.sin(ang)[:, :, None, :]
    xf = x.astype(jnp.float32)
    x1 = xf[..., :half]
    x2 = xf[..., half:rot_dim]
    out = jnp.concatenate([x1 * cos - x2 * sin, x2 * cos + x1 * sin, xf[..., rot_dim:]], axis=-1)
    return out.astype(x.dtype)

def causal_block_probs(q_blk, k_pre, q_start, scale):
    n_q = q_blk.shape[1]
    n_k = k_pre.shape[1]
    s = jnp.einsum('bqhd,bkhd->bhqk', q_blk, k_pre).astype(jnp.float32) * scale
    mask = (q_start + jnp.arange(n_q))[:, None] >= jnp.arange(n_k)[None, :]
    s = jnp.where(mask, s, -jnp.inf)
    return jax.nn.softmax(s, axis=-1)

def diff_attention(q, k, v, lam, scale):
    seq = q.shape[1]
    outs = []
    for start in range(0, seq, Q_BLOCK):
        end = start + Q_BLOCK
        p1 = causal_block_probs(q[:, start:end, :, 0], k[:, :end, :, 0], start, scale)
        p2 = causal_block_probs(q[:, start:end, :, 1], k[:, :end, :, 1], start, scale)
        p = (p1 - lam * p2).astype(v.dtype)
        outs.append(jnp.einsum('bhqk,bkhd->bqhd', p, v[:, :end]))
    return jnp.concatenate(outs, axis=1)

def causal_attention(q, k, v, scale):
    seq = q.shape[1]
    outs = []
    for start in range(0, seq, Q_BLOCK):
        end = start + Q_BLOCK
        p = causal_block_probs(q[:, start:end], k[:, :end], start, scale).astype(v.dtype)
        outs.append(jnp.einsum('bhqk,bkhd->bqhd', p, v[:, :end]))
    return jnp.concatenate(outs, axis=1)

def setup_inputs(seed: int = 0) -> dict:
    key = jax.random.key(seed)
    ks = iter(jax.random.split(key, 32))

    def w(shape):
        return jax.random.normal(next(ks), shape, jnp.float32) * (shape[-2] ** -0.5)

    def gain(shape):
        return 1.0 + 0.02 * jax.random.normal(next(ks), shape, jnp.float32)

    x = jax.random.normal(next(ks), (BATCH, SEQ, D_MODEL), jnp.float32)
    mem = jax.random.normal(next(ks), (BATCH, MEM_LEN, D_MODEL), jnp.float32)
    offsets = jax.random.randint(next(ks), (BATCH, 1), 0, 1024, dtype=jnp.int32)
    positions = offsets + jnp.arange(SEQ, dtype=jnp.int32)[None, :]
    return {
        "x": x,
        "mem": mem,
        "positions": positions,
        "attn_norm_w": gain((DEPTH, D_MODEL)),
        "w_in": w((DEPTH, D_MODEL, IN_COLS)),
        "diff_lambda": DIFF_LAMBDA_STD * jax.random.normal(next(ks), (DEPTH, 4, DIFF_HEAD_DIM), jnp.float32),
        "diff_subln_w": gain((DEPTH, DIFF_V_DIM)),
        "w_o_diff": w((DEPTH, DIFF_V_WIDTH, D_MODEL)),
        "mla_q_norm_w": gain((DEPTH, MLA_Q_LORA)),
        "mla_w_uq": w((DEPTH, MLA_Q_LORA, MLA_HEADS * MLA_QK_DIM)),
        "mla_kv_norm_w": gain((DEPTH, MLA_KV_LORA)),
        "mla_w_ukv": w((DEPTH, MLA_KV_LORA, MLA_HEADS * (MLA_NOPE_DIM + MLA_V_DIM))),
        "w_o_mla": w((DEPTH, MLA_V_WIDTH, D_MODEL)),
        "mem_norm_w": gain((DEPTH, D_MODEL)),
        "w_mem_kv": w((DEPTH, D_MODEL, 2 * CROSS_WIDTH)),
        "w_o_cross": w((DEPTH, CROSS_WIDTH, D_MODEL)),
        "w_out": w((DEPTH, D_MODEL, D_MODEL)),
        "ffn_norm_w": gain((DEPTH, D_MODEL)),
        "w_gate_up": w((DEPTH, D_MODEL, 2 * FFN_HIDDEN)),
        "w_down": w((DEPTH, FFN_HIDDEN, D_MODEL)),
        "final_norm_w": gain((D_MODEL,)),
    }

def reference(x, mem, positions, attn_norm_w, w_in, diff_lambda, diff_subln_w, w_o_diff,
              mla_q_norm_w, mla_w_uq, mla_kv_norm_w, mla_w_ukv, w_o_mla,
              mem_norm_w, w_mem_kv, w_o_cross, w_out, ffn_norm_w, w_gate_up, w_down,
              final_norm_w):
    b, s, _ = x.shape
    m_len = mem.shape[1]
    for i in range(DEPTH):
        h = rms_norm(x, attn_norm_w[i])
        proj = h @ w_in[i]
        dq, dk, dv, cq, ckv, krope, xq, gates = jnp.split(proj, IN_SPLIT_POINTS, axis=-1)

        dq = apply_rope(dq.reshape(b, s, 2 * DIFF_HEADS, DIFF_HEAD_DIM), positions, DIFF_ROT_DIM)
        dk = apply_rope(dk.reshape(b, s, 2 * DIFF_HEADS, DIFF_HEAD_DIM), positions, DIFF_ROT_DIM)
        dq = dq.reshape(b, s, DIFF_HEADS, 2, DIFF_HEAD_DIM)
        dk = dk.reshape(b, s, DIFF_HEADS, 2, DIFF_HEAD_DIM)
        dv = dv.reshape(b, s, DIFF_HEADS, DIFF_V_DIM)
        lam_init = 0.8 - 0.6 * math.exp(-0.3 * i)
        lv = diff_lambda[i].astype(jnp.float32)
        lam = jnp.exp(jnp.sum(lv[0] * lv[1])) - jnp.exp(jnp.sum(lv[2] * lv[3])) + lam_init
        a = diff_attention(dq, dk, dv, lam, DIFF_HEAD_DIM ** -0.5)
        a = rms_norm(a, diff_subln_w[i]) * (1.0 - lam_init)
        y_a = a.reshape(b, s, DIFF_V_WIDTH) @ w_o_diff[i]

        qm = (rms_norm(cq, mla_q_norm_w[i]) @ mla_w_uq[i]).reshape(b, s, MLA_HEADS, MLA_QK_DIM)
        q_nope = qm[..., :MLA_NOPE_DIM]
        q_pe = apply_rope(qm[..., MLA_NOPE_DIM:], positions, MLA_ROPE_DIM)
        kv = (rms_norm(ckv, mla_kv_norm_w[i]) @ mla_w_ukv[i]).reshape(b, s, MLA_HEADS, MLA_NOPE_DIM + MLA_V_DIM)
        k_nope = kv[..., :MLA_NOPE_DIM]
        v_m = kv[..., MLA_NOPE_DIM:]
        k_pe = apply_rope(krope[:, :, None, :], positions, MLA_ROPE_DIM)
        q_full = jnp.concatenate([q_nope, q_pe], axis=-1)
        k_full = jnp.concatenate([k_nope, jnp.broadcast_to(k_pe, (b, s, MLA_HEADS, MLA_ROPE_DIM))], axis=-1)
        mo = causal_attention(q_full, k_full, v_m, MLA_QK_DIM ** -0.5)
        y_b = mo.reshape(b, s, MLA_V_WIDTH) @ w_o_mla[i]

        mh = rms_norm(mem, mem_norm_w[i])
        mk, mv = jnp.split(mh @ w_mem_kv[i], 2, axis=-1)
        mk = mk.reshape(b, m_len, CROSS_HEADS, CROSS_HEAD_DIM)
        mv = mv.reshape(b, m_len, CROSS_HEADS, CROSS_HEAD_DIM)
        xq = xq.reshape(b, s, CROSS_HEADS, CROSS_HEAD_DIM)
        sc = jnp.einsum('bqhd,bkhd->bhqk', xq, mk).astype(jnp.float32) * (CROSS_HEAD_DIM ** -0.5)
        pc = jax.nn.softmax(sc, axis=-1).astype(mv.dtype)
        co = jnp.einsum('bhqk,bkhd->bqhd', pc, mv)
        y_c = co.reshape(b, s, CROSS_WIDTH) @ w_o_cross[i]

        g_a, g_b, g_c = jnp.split(jax.nn.sigmoid(gates), N_BRANCHES, axis=-1)
        x = x + (g_a * y_a + g_b * y_b + g_c * y_c) @ w_out[i]

        h2 = rms_norm(x, ffn_norm_w[i])
        f_gate, f_up = jnp.split(h2 @ w_gate_up[i], 2, axis=-1)
        x = x + (jax.nn.silu(f_gate) * f_up) @ w_down[i]
    return rms_norm(x, final_norm_w)


_drawn_inputs = setup_inputs


def setup_inputs(seed=0):
    import zlib

    import numpy as np

    out = dict(_drawn_inputs(seed))
    spreads = {}
    factors = {'attn_norm_w': 2.793,
     'diff_subln_w': 4.478,
     'mla_q_norm_w': 8.0,
     'mla_kv_norm_w': 8.0,
     'mem_norm_w': 8.0,
     'ffn_norm_w': 2.901,
     'final_norm_w': 2.949}
    for name, (base, spread) in spreads.items():
        noise = np.random.default_rng([zlib.crc32(name.encode()), seed]).standard_normal(out[name].shape)
        drawn = base * np.exp(spread * noise) if base else spread * noise
        out[name] = __import__('jax').numpy.asarray(drawn.astype(out[name].dtype))
    for name, factor in factors.items():
        out[name] = (out[name] * factor).astype(out[name].dtype)
    return out
```

```python
import math
from contextlib import ExitStack

import numpy as np
import concourse.bass as bass
from concourse import mybir

F32 = mybir.dt.float32
F32R = mybir.dt.float32r
BF16 = mybir.dt.bfloat16
I32 = mybir.dt.int32
ACT = mybir.ActivationFunctionType
ALU = mybir.AluOpType
AX = mybir.AxisListType

P = 128
D = 1024
SEQ = 512
MEM = 256
DEPTH = 2
EPS = 1e-6
THETA = 500000.0
KD = D // P
NT = SEQ // P
NM = MEM // P
HEADS = 8
CROSS = 4
ROT_D, ROT_M = 16, 32
Q_LORA, KV_LORA = 512, 256
QT, KVT = Q_LORA // P, KV_LORA // P
FFN = 2816
FT = FFN // P
DOWN = (6, 6, 5, 5)
DIFF_SCALE = 64 ** -0.5
MLA_SCALE = 96 ** -0.5
CROSS_SCALE = 128 ** -0.5
C_DQ, C_DK, C_DV, C_CQ, C_CKV, C_KR, C_XQ, C_GATE = 0, 1024, 2048, 3072, 3584, 3840, 3872, 4384
MASKED = -3.0e38
AHEAD = 3
CAUSAL = NT * (NT + 1) // 2 * P
G_ATTN, G_FFN, G_MEM, G_Q, G_KV, G_SUB, G_LAM, G_N = 0, 8, 16, 24, 28, 30, 31, 32


def q_off(t):
    return P * t * (t + 1) // 2


def k_off(j):
    return P * (NT * j - j * (j - 1) // 2)


class Tally:

    def __init__(self, sem, by, before=1, **stages):
        self.sem, self.by, self.start, total = sem, by, {}, 0
        for name, (per, steps) in stages.items():
            self.start[name] = (total, per)
            total += per * steps
        self.total, self.before = total, before

    def at(self, layer, stage, step=0, k=0):
        base, per = self.start[stage]
        return layer * self.total + step * per + (self.before + base + k)

    def index(self, layer, stage, step=0, k=0):
        base, per = self.start[stage]
        return layer * self.total + step * per + (base + k)

    def end(self, layers):
        return self.before + layers * self.total


def build_trunk(nc, x, mem, positions, attn_norm_w, w_in, diff_lambda, diff_subln_w, w_o_diff,
                mla_q_norm_w, mla_w_uq, mla_kv_norm_w, mla_w_ukv, w_o_mla, mem_norm_w, w_mem_kv,
                w_o_cross, w_out, ffn_norm_w, w_gate_up, w_down, final_norm_w, out, mem_scratch):
    ctx = ExitStack()
    with ctx:
        def sem(name):
            return ctx.enter_context(nc.semaphore(name))

        def bank(name):
            return ctx.enter_context(nc.psum_tensor(name, [P, 512], F32))

        cursor = [(nc.sbuf_base + 31) // 32 * 32]

        def here(name, shape, dt=F32):
            t = nc.alloc_sbuf_tensor_at(name, shape, dt, offset=cursor[0])
            size = int(np.prod(shape[1:])) * (2 if dt == BF16 else 4)
            cursor[0] += (size + 31) // 32 * 32
            return t

        xT = here("xT", [P, KD, SEQ])
        h_hi = here("h_hi", [P, KD, SEQ], F32R)
        h_lo = here("h_lo", [P, KD, SEQ], F32R)
        raw = [here(f"raw{s}", [P, KD * P]) for s in range(2)]
        w_hi = [here(f"w_hi{s}", [P, KD * P], F32R) for s in range(4)]
        w_lo = [here(f"w_lo{s}", [P, KD * P], F32R) for s in range(4)]
        cos_d, sin_d, cos_m, sin_m = (here(n, [P, SEQ]) for n in ("cos_d", "sin_d", "cos_m", "sin_m"))
        ident = here("ident", [P, P])
        ident_b = here("ident_b", [P, P], BF16)
        mask_b = here("mask_b", [P, P], BF16)
        ones = here("ones", [P, P])
        gains = here("gains", [P, P])
        gl = here("gl", [P, G_N])
        stat = {k: [here(f"{n}_{k}", [P, NT]) for n in ("top", "bias", "total", "inv")]
                for k in ("m", "d1", "d2")}
        lam_scale = here("lam_scale", [P, NT])
        warm = here("warm", [P, 1])
        eps = here("eps", [P, 1])
        pool_mark = here("pool_mark", [P, 4])
        x_sum = here("x_sum", [P, SEQ])
        square = here("square", [P, SEQ])
        rstd_at = cursor[0]
        rstd = here("rstd", [P, SEQ])

        base = cursor[0]

        def at(name, offset, shape, dt=F32):
            return nc.alloc_sbuf_tensor_at(name, shape, dt, offset=base + offset)

        KB = 1024
        outs = at("outs", 0, [P, 16, SEQ])
        outs_lo = at("outs_lo", 0, [P, 16, SEQ], F32R)
        mem_hi = at("mem_hi", 0, [P, KD, MEM], F32R)
        mem_lo = at("mem_lo", 8 * KB, [P, KD, MEM], F32R)
        ckv_raw = at("ckv_raw", 0, [P, KVT, SEQ])
        ckv_sq = at("ckv_sq", 4 * KB, [P, KVT, SEQ])
        cq_raw = at("cq_raw", 16 * KB, [P, QT, SEQ])
        q_sum = nc.alloc_sbuf_tensor_at("q_sum", [P, SEQ], F32, offset=rstd_at)
        mem_n = at("mem_n", 32 * KB, [P, KD, MEM])
        cq_hi = at("cq_hi", 32 * KB, [P, QT, SEQ], F32R)
        cq_lo = at("cq_lo", 40 * KB, [P, QT, SEQ], F32R)
        ckv_hi = at("ckv_hi", 48 * KB, [P, KVT, SEQ], F32R)
        ckv_lo = at("ckv_lo", 52 * KB, [P, KVT, SEQ], F32R)
        T = 56 * KB
        p_a = at("p_a", T, [P, CAUSAL])
        p_b = at("p_b", T + 5 * KB, [P, CAUSAL])
        pt_hi = at("pt_hi", T + 10 * KB, [P, CAUSAL], F32R)
        pt_lo = at("pt_lo", T + 15 * KB, [P, CAUSAL], F32R)
        v_hi = at("v_hi", T + 20 * KB, [P, NT, P], F32R)
        v_lo = at("v_lo", T + 22 * KB, [P, NT, P], F32R)
        mv_hi = at("mv_hi", T + 24 * KB, [P, NT, P], F32R)
        mv_lo = at("mv_lo", T + 26 * KB, [P, NT, P], F32R)
        qT = at("qT", T + 28 * KB, [P, SEQ])
        kT = at("kT", T + 30 * KB, [P, SEQ])
        mqT = at("mqT", T + 32 * KB, [P, SEQ])
        mkT = at("mkT", T + 34 * KB, [P, SEQ])
        vT = at("vT", T + 36 * KB, [P, SEQ])
        kvT = at("kvT", T + 38 * KB, [P, SEQ])
        a_sq = at("a_sq", T + 40 * KB, [P, SEQ])
        rot = at("rot", T + 42 * KB, [P, SEQ])
        mid = at("mid", T + 44 * KB, [P, SEQ])
        pair = at("pair", T + 42 * KB, [P, 2, SEQ])
        outs_hi = at("outs_hi", 32 * KB, [P, 16, SEQ], F32R)
        mix_hi = at("mix_hi", 64 * KB, [P, KD, SEQ], F32R)
        mix_lo = at("mix_lo", 80 * KB, [P, KD, SEQ], F32R)
        sig = at("sig", 96 * KB, [P, 3, SEQ])
        mix = nc.alloc_sbuf_tensor_at("mix", [P, SEQ], F32, offset=rstd_at)
        hid_hi = at("hid_hi", 0, [P, FT, SEQ], F32R)
        hid_lo = at("hid_lo", 44 * KB, [P, FT, SEQ], F32R)
        sig_f = at("sig_f", 88 * KB, [P, 2, SEQ])
        gated = at("gated", 92 * KB, [P, SEQ])
        hid = at("hid", 94 * KB, [P, 2, SEQ])
        x_in = at("x_in", 0, [P, NT, D])
        mem_in = at("mem_in", 16 * KB, [P, NM, D])
        mem_t = at("mem_t", 24 * KB, [P, KD, MEM])
        gain_rows = at("gain_rows", 32 * KB, [P, P])
        lam_in = at("lam_in", 33 * KB, [P, DEPTH, 4, 64])
        lam_prod = at("lam_prod", 35 * KB, [P, DEPTH * 2, 64])
        lam_sum = at("lam_sum", 36 * KB, [P, DEPTH * 2])
        lam_exp = at("lam_exp", 36 * KB + 64, [P, DEPTH * 2])
        mem_ss = at("mem_ss", 36 * KB + 128, [P, NM])
        mem_rstd = at("mem_rstd", 36 * KB + 192, [P, NM])
        pos_i = at("pos_i", 36 * KB + 256, [P, NT], I32)
        pos_f = at("pos_f", 36 * KB + 320, [P, NT])
        freq = at("freq", 36 * KB + 384, [P, 24])
        ang = at("ang", 37 * KB, [P, NT, 24])
        turns = at("turns", 38 * KB, [P, NT, 24])
        sin_t = at("sin_t", 39 * KB, [P, NT, 24])
        cos_t = at("cos_t", 40 * KB, [P, NT, 24])
        half_t = at("half_t", 41 * KB, [P, NT, 24])
        neg_t = at("neg_t", 42 * KB, [P, NT, 24])
        rope_t = at("rope_t", 44 * KB, [P, 4, NT, P])
        mem_sq = at("mem_sq", 52 * KB, [P, D])
        y_T = at("y_T", 16 * KB, [P, KD, SEQ])
        y_out = at("y_out", 0, [P, NT, D])
        assert base + 102 * KB <= nc.sbuf_usable_end, (base, nc.sbuf_usable_end)

        proj = [bank("proj0"), bank("proj1")]
        score = [bank("score0"), bank("score1"), bank("score2")]
        flip = [bank("flip0"), bank("flip1")]
        att = bank("att")
        ssq = score[2]

        raw_full = [sem("raw_full0"), sem("raw_full1")]
        SLOTS = dict(C=(4, CROSS), A=(4, 1), B=(4, HEADS), E=(20, 2), F=(4, 2), G=(4, FT // 2), H=(8, 4))
        slot_hi = Tally(sem("slot_hi"), "act", **SLOTS)
        slot_lo = Tally(sem("slot_lo"), "pool", 2, **SLOTS)
        slot_done = Tally(sem("slot_done"), "pe", **SLOTS)
        mq_done = Tally(sem("mq_done"), "pe", B=(1, HEADS))
        om_done = Tally(sem("om_done"), "pe", E=(4, 2))
        SETS = dict(C=(1, CROSS), B=(3, HEADS))
        score_full = Tally(sem("score_full"), "pe", C=(2, CROSS), B=(9, HEADS))
        bias_ready = Tally(sem("bias_ready"), "ve", **SETS)
        exp_done = Tally(sem("exp_done"), "act", C=(4, CROSS), B=(12, HEADS))
        prob_ready = Tally(sem("prob_ready"), "ve", C=(1, CROSS), B=(2, HEADS))
        FLIPS = dict(C=(4, CROSS), B=(8, HEADS))
        flip_full = Tally(sem("flip_full"), "pe", **FLIPS)
        flip_hi = Tally(sem("flip_hi"), "act", **FLIPS)
        flip_read = Tally(sem("flip_read"), "ve", **FLIPS)
        ATT = dict(C=(1, CROSS), B=(2, HEADS))
        att_full = Tally(sem("att_full"), "pe", **ATT)
        att_read = Tally(sem("att_read"), "ve", **ATT)
        kv_copied = Tally(sem("kv_copied"), "act", C=(3, CROSS), B=(2, HEADS))
        mla_ready = Tally(sem("mla_ready"), "ve", A=(1, 1), B=(2, HEADS))
        diff_ready = Tally(sem("diff_ready"), "ve", B=(2, HEADS))
        SSQ = dict(N1=(1, 1), A=(2, 1), B=(1, HEADS), N2=(1, 1))
        ssq_full = Tally(sem("ssq_full"), "pe", **SSQ)
        ssq_read = Tally(sem("ssq_read"), "act", **SSQ)
        rms_ready = Tally(sem("rms_ready"), "act", **SSQ)
        SQ = dict(C=(1, CROSS), F=(4, 2), H=(2, 4))
        tile_ready = Tally(sem("tile_ready"), "ve", **SQ)
        sq_done = Tally(sem("sq_done"), "act", KD + 1, **SQ)
        sq_added = Tally(sem("sq_added"), "ve", KD + 1, **SQ)
        ckv_copied = Tally(sem("ckv_copied"), "ve", A=(2, 1))
        ckv_squared = Tally(sem("ckv_squared"), "act", A=(2, 1))
        a_squared = Tally(sem("a_squared"), "act", B=(1, HEADS))
        NORM = dict(N1=(KD, 1), A=(QT + KVT, 1), N2=(KD, 1))
        pair_ready = Tally(sem("pair_ready"), "ve", **NORM)
        pair_hi = Tally(sem("pair_hi"), "act", **NORM)
        pair_lo = Tally(sem("pair_lo"), "ve", **NORM)
        gl_ready = Tally(sem("gl_ready"), "ve", N1=(1, 1))
        mem_loaded = Tally(sem("mem_loaded"), "dma", 0, N1=(16, 1))
        memh_hi = Tally(sem("memh_hi"), "act", N1=(KD, 1))
        memh_lo = Tally(sem("memh_lo"), "ve", N1=(KD, 1))
        outs_split_hi = Tally(sem("outs_split_hi"), "act", E=(16, 1))
        outs_split = Tally(sem("outs_split"), "ve", E=(16, 1))
        sig_ready = Tally(sem("sig_ready"), "act", E=(12, 2))
        od_used = Tally(sem("od_used"), "ve", E=(4, 2))
        om_used = Tally(sem("om_used"), "ve", E=(4, 2))
        oc_used = Tally(sem("oc_used"), "ve", E=(4, 2))
        mix_ready = Tally(sem("mix_ready"), "ve", E=(4, 2))
        mix_split_hi = Tally(sem("mix_split_hi"), "act", E=(4, 2))
        mix_split = Tally(sem("mix_split"), "ve", E=(4, 2))
        HID = dict(G=(2, FT // 2))
        silu_sig = Tally(sem("silu_sig"), "act", **HID)
        gate_used = Tally(sem("gate_used"), "ve", **HID)
        hid_ready = Tally(sem("hid_ready"), "ve", **HID)
        hid_split_hi = Tally(sem("hid_split_hi"), "act", **HID)
        hid_split = Tally(sem("hid_split"), "ve", **HID)
        const_step, const_ready = sem("const_step"), sem("const_ready")
        in_gain, in_x, in_mem, in_pos, in_lam = (sem(n) for n in ("in_gain", "in_x", "in_mem", "in_pos", "in_lam"))
        pre_full, pre_read, pre_act = sem("pre_full"), sem("pre_read"), sem("pre_act")
        pre_chain = sem("pre_chain")
        pre_vec, mem_stored, mem_scaled, rope_ready = (sem(n) for n in ("pre_vec", "mem_stored", "mem_scaled", "rope_ready"))
        y_ready, y_flipped, y_copied, stored = sem("y_ready"), sem("y_flipped"), sem("y_copied"), sem("stored")
        vec_step = Tally(sem("vec_step"), "ve", N1=(2, 1), C=(2, CROSS), A=(2, 1), P=(6, 1), B=(14, HEADS - 1), L=(8, 1),
                         E=(4, 2), N2=(1, 1))

        tallies = [
            sq_done, sq_added, slot_hi, slot_done, mq_done, om_done, score_full, bias_ready,
            exp_done, prob_ready, flip_full, flip_hi, flip_read, att_full, att_read, kv_copied,
            mla_ready, diff_ready, ssq_full, ssq_read, rms_ready, tile_ready, ckv_copied,
            ckv_squared, a_squared, pair_ready, pair_hi, pair_lo, gl_ready, memh_hi, memh_lo,
            outs_split_hi, outs_split, sig_ready, od_used, om_used, oc_used, mix_ready,
            mix_split_hi, mix_split, silu_sig, gate_used, hid_ready, hid_split_hi, hid_split,
            vec_step,
        ]

        def start_counts(engine, by):
            for t in tallies:
                if t.by == by:
                    engine.sem_inc(t.sem, 1)

        block = ctx.enter_context(nc.Block())

        @block.sync
        def _(sp):
            for t in range(NT):
                sp.dma_start(x_in[:, t, :], x[0, t * P:(t + 1) * P, :]).then_inc(in_x, 16)
            for t in range(NM):
                sp.dma_start(mem_in[:, t, :], mem[0, t * P:(t + 1) * P, :]).then_inc(in_mem, 16)
            sp.wait_ge(const_ready, 1)
            for l in range(DEPTH):
                for row, w, n in ((G_ATTN, attn_norm_w, KD), (G_FFN, ffn_norm_w, KD), (G_MEM, mem_norm_w, KD),
                                  (G_Q, mla_q_norm_w, QT), (G_KV, mla_kv_norm_w, KVT), (G_SUB, diff_subln_w, 1)):
                    sp.dma_start(gain_rows[l * G_N + row:l * G_N + row + n, :],
                                 w[l, :].rearrange("(k p) -> k p", p=P)).then_inc(in_gain, 16)
            sp.dma_start(gain_rows[DEPTH * G_N:DEPTH * G_N + KD, :],
                         final_norm_w.rearrange("(k p) -> k p", p=P)).then_inc(in_gain, 16)
            sp.dma_start(pos_i[:, :], positions[0, :].rearrange("(t p) -> p t", p=P),
                         allow_slow_non_contiguous=True).then_inc(in_pos, 16)
            sp.dma_start(lam_in[:, :, :, :].rearrange("p l a d -> p (l a d)"),
                         diff_lambda.rearrange("l a d -> (l a d)").partition_broadcast(P)).then_inc(in_lam, 16)

            def slot(l, stage, step, s, *parts):
                sp.wait_ge(slot_lo.sem, slot_lo.at(l, stage, step, s - 1))
                assert len(parts) == 2
                for col, src in parts:
                    n, width = src.shape[1], src.shape[2]
                    sp.dma_start(raw[s % 2][:, col:col + n * width].rearrange("p (k n) -> p k n", k=n),
                                 src).then_inc(raw_full[s % 2], 16)

            def tiles(w, l, k0, k1, col, width=P):
                v = w.rearrange("l (k p) n -> l p k n", p=P)
                v = v[l:l + 1] if isinstance(l, int) else v[bass.ds(l, 1)]
                v = v[:, :, k0:k1, bass.ds(col, width)]
                return v.rearrange("a p k n -> (a p) k n")

            def whole(w, l, col):
                return (0, tiles(w, l, 0, 4, col)), (4 * P, tiles(w, l, 4, 8, col))

            def cross_slots(l, i):
                slot(l, "C", i, 0, *whole(w_in, l, C_XQ + i * P))
                slot(l, "C", i, 1, *whole(w_mem_kv, l, i * P))
                slot(l, "C", i, 2, *whole(w_mem_kv, l, 512 + i * P))
                slot(l, "C", i, 3, *whole(w_in, l, C_CQ + i * P))

            def head_slots(l, h):
                slot(l, "B", h, 0, *whole(w_in, l, C_DV + h * P))
                slot(l, "B", h, 1, (0, tiles(mla_w_uq, l, 0, QT, h * 96, 96)),
                     (QT * 96, tiles(mla_w_ukv, l, 0, KVT, h * P)))
                slot(l, "B", h, 2, *whole(w_in, l, C_DQ + h * P))
                slot(l, "B", h, 3, *whole(w_in, l, C_DK + h * P))

            with sp.Fori(0, DEPTH) as l:
                with sp.Fori(0, CROSS) as i:
                    cross_slots(l, i)
                slot(l, "A", 0, 0, *whole(w_in, l, C_CKV))
                slot(l, "A", 0, 1, *whole(w_in, l, C_CKV + P))
                slot(l, "A", 0, 2, (0, tiles(w_in, l, 0, 2, C_KR - 64, 96)), (2 * 96, tiles(w_in, l, 2, 4, C_KR - 64, 96)))
                slot(l, "A", 0, 3, (0, tiles(w_in, l, 4, 6, C_KR - 64, 96)), (2 * 96, tiles(w_in, l, 6, 8, C_KR - 64, 96)))
                with sp.Fori(0, HEADS) as h:
                    head_slots(l, h)
                with sp.Fori(0, 2) as jj:
                    for e in range(4):
                        j = jj * (4 * P) + e * P
                        for g in range(3):
                            slot(l, "E", jj, 5 * e + g, *whole(w_in, l, j + (C_GATE + g * D)))
                        slot(l, "E", jj, 5 * e + 3, *whole(w_o_diff, l, j))
                        slot(l, "E", jj, 5 * e + 4, (0, tiles(w_o_mla, l, 0, 4, j)), (4 * P, tiles(w_o_cross, l, 0, 4, j)))
                with sp.Fori(0, 2) as jj:
                    for e in range(4):
                        slot(l, "F", jj, e, *whole(w_out, l, jj * (4 * P) + e * P))
                with sp.Fori(0, FT // 2) as t:
                    for e in range(2):
                        slot(l, "G", t, 2 * e, *whole(w_gate_up, l, t * (2 * P) + e * P))
                        slot(l, "G", t, 2 * e + 1, *whole(w_gate_up, l, t * (2 * P) + (e * P + FFN)))
                with sp.Fori(0, 4) as jj:
                    for e in range(2):
                        k = 0
                        for c, n in enumerate(DOWN):
                            slot(l, "H", jj, 4 * e + c, (0, tiles(w_down, l, k, k + 3, jj * (2 * P) + e * P)),
                                 (3 * P, tiles(w_down, l, k + 3, k + n, jj * (2 * P) + e * P)))
                            k += n
            for s in range(AHEAD + 1):
                sp.wait_ge(slot_lo.sem, slot_lo.end(DEPTH) + s - 1)
                for half in range(2):
                    sp.dma_start(raw[s % 2][:, half * 512:(half + 1) * 512], w_out[0, 0:P, 0:512]).then_inc(raw_full[s % 2], 16)
            for t in range(NT):
                sp.wait_ge(y_copied, 2 * (t + 1))
                sp.dma_start(out[0, t * P:(t + 1) * P, :], y_out[:, t, :]).then_inc(stored, 16)
            sp.wait_ge(stored, 16 * NT)
            sp.wait_ge(mem_stored, 16)

        @block.gpsimd
        def _(pool):
            g = nc.gpsimd
            n = [0]

            def step(ins):
                n[0] += 1
                ins.then_inc(const_step, 1)
                pool.wait_ge(const_step, n[0])

            step(g.memset(gain_rows[:, :], 0.0))
            g.memset(warm[:, :], 0.0).then_inc(const_ready, 1)
            g.memset(ones[:, :], 1.0)
            g.memset(eps[:, :], EPS)
            step(g.memset(ident[:, :], 0.0))
            step(g.affine_select(out=ident[:, :], in_=ident[:, :], compare_op=ALU.not_equal, fill=1.0,
                                 base=0, pattern=[[-1, P]], channel_multiplier=1))
            step(g.memset(ident_b[:, :], 0.0))
            step(g.affine_select(out=ident_b[:, :], in_=ident_b[:, :], compare_op=ALU.not_equal, fill=1.0,
                                 base=0, pattern=[[-1, P]], channel_multiplier=1))
            step(g.memset(mask_b[:, :], 0.0))
            step(g.affine_select(out=mask_b[:, :], in_=mask_b[:, :], compare_op=ALU.is_ge, fill=MASKED,
                                 base=0, pattern=[[-1, P]], channel_multiplier=1))
            g.memset(x_sum[:, :], 0.0)
            for r, rot_dim in ((0, ROT_D), (ROT_D // 2, ROT_M)):
                for i in range(rot_dim // 2):
                    f = np.float32(THETA) ** (-np.float32(i) * np.float32(2.0) / np.float32(rot_dim))
                    g.memset(freq[:, r + i:r + i + 1], float(f))
            for kind in range(4):
                step(g.memset(rope_t[:, kind, :, :], 1.0 - kind % 2))
            g.memset(pool_mark[:, 2:3], 0.0).then_inc(const_ready, 1)
            for b in range(2):
                g.memset(pool_mark[:, b:b + 1], 0.0).then_inc(slot_lo.sem, 1)
            total = slot_lo.total * DEPTH
            with pool.Fori(0, total // 4) as r:
                for s in range(4):
                    pool.wait_ge(slot_hi.sem, r * 4 + (slot_hi.before + s + 1))
                    g.tensor_tensor(w_lo[s][:, :], raw[s % 2][:, :], w_hi[s][:, :].bitcast(F32),
                                    ALU.subtract).then_inc(slot_lo.sem, 1)
            for s in range(AHEAD + 1):
                pool.wait_ge(slot_hi.sem, slot_hi.before + total + s + 1)
                g.tensor_tensor(w_lo[s][:, :], raw[s % 2][:, :], w_hi[s][:, :].bitcast(F32),
                                ALU.subtract).then_inc(slot_lo.sem, 1)

        @block.tensor
        def _(pe):
            mm = nc.tensor.matmul
            start_counts(pe, "pe")

            def product(pieces):
                last = len(pieces) - 1
                for n, (o, sh, sl, mh, ml) in enumerate(pieces):
                    mm(o, sh, mh, start=n == 0, stop=False)
                    mm(o, sh, ml, start=False, stop=False)
                    ins = mm(o, sl, mh, start=False, stop=n == last)
                return ins

            def unit(l, stage, step, s, b, free, n, rhs, width=P, cols=SEQ, first=0, before=None, start=True, stop=True):
                pe.wait_ge(slot_lo.sem, slot_lo.at(l, stage, step, s + 1))
                if free:
                    pe.wait_ge(free[0].sem, free[1])
                hi, lo = w_hi[s % 4], w_lo[s % 4]
                for k in range(n):
                    if before:
                        before(k)
                    c = first + k * width
                    rh, rl = rhs(k)
                    o = proj[b][0:width, 0:cols]
                    mm(o, hi[:, c:c + width], rh, start=start and k == 0, stop=False)
                    mm(o, hi[:, c:c + width], rl, start=False, stop=False)
                    ins = mm(o, lo[:, c:c + width], rh, start=False, stop=stop and k == n - 1)
                return ins

            def h_rhs(k):
                return h_hi[:, k, :], h_lo[:, k, :]

            def sum_squares(l, stage, k, *tiles):
                pe.wait_ge(ssq_read.sem, ssq_read.at(l, stage, 0, k))
                for n, t in enumerate(tiles):
                    ins = mm(ssq[:, :], ones[:, :], t, start=n == 0, stop=n == len(tiles) - 1)
                ins.then_inc(ssq_full.sem, 1)

            def flip_bank(l, stage, step, k):
                pe.wait_ge(flip_read.sem, flip_read.at(l, stage, step, k - 1) if stage == "B" or k else flip_read.at(l, stage, step, 0))
                return flip[k % 2]

            def causal_scores(l, h, n, q, k, rows):
                pe.wait_ge(exp_done.sem, exp_done.at(l, "B", h, 4 * n))
                for b, group in enumerate(((3,), (2, 0), (1,))):
                    for t in group:
                        o = score[b][:, 384 * (t == 0):384 * (t == 0) + (t + 1) * P]
                        mm(o, q[rows, t * P:(t + 1) * P], k[rows, 0:(t + 1) * P], start=True, stop=False)
                        ins = mm(o[:, t * P:(t + 1) * P], ident_b[:, :], mask_b[:, :], start=False, stop=True)
                    ins.then_inc(score_full.sem, 1)

            def causal_flip(l, h, n, part):
                p, k0 = (p_a, 2) if n == 0 else (p_b, 5)
                if part == 0:
                    pe.wait_ge(prob_ready.sem, prob_ready.at(l, "B", h, n + 1))
                fills = ((0,), (1,)) if part == 0 else ((2, 3),)
                for f, js in enumerate(fills):
                    k = k0 + 2 * part + f
                    b, col = flip_bank(l, "B", h, k), 0
                    for j in js:
                        for t in range(j, NT):
                            ins = nc.tensor.transpose(b[:, col:col + P], p[:, q_off(t) + j * P:q_off(t) + (j + 1) * P], ident[:, :])
                            col += P
                    ins.then_inc(flip_full.sem, 1)

            def causal_attend(l, h, n, vh, vl):
                pe.wait_ge(flip_read.sem, flip_read.at(l, "B", h, 5 + 3 * n))
                pe.wait_ge(att_read.sem, att_read.at(l, "B", h, n))
                product([(att[:, j * P:SEQ], vh[:, j, :], vl[:, j, :], pt_hi[:, k_off(j):k_off(j) + SEQ - j * P],
                          pt_lo[:, k_off(j):k_off(j) + SEQ - j * P]) for j in range(NT)]).then_inc(att_full.sem, 1)

            def flip_values(l, h):
                for k, (src, copied) in enumerate(((vT, 1), (kvT, 2))):
                    pe.wait_ge(kv_copied.sem, kv_copied.at(l, "B", h, copied))
                    b = flip_bank(l, "B", h, k)
                    for j in range(NT):
                        ins = nc.tensor.transpose(b[:, j * P:(j + 1) * P], src[:, j * P:(j + 1) * P], ident[:, :])
                    ins.then_inc(flip_full.sem, 1)

            def project_v(l, h):
                unit(l, "B", h, 0, 0, (diff_ready, diff_ready.at(l, "B", h)), KD, h_rhs).then_inc(slot_done.sem, 1)

            def project_latent(l, h, wait_norm=False):
                if wait_norm:
                    pe.wait_ge(pair_lo.sem, pair_lo.at(l, "A", 0, QT + KVT))
                unit(l, "B", h, 1, 1, (diff_ready, diff_ready.at(l, "B", h)), QT, lambda k: (cq_hi[:, k, :], cq_lo[:, k, :]), width=96).then_inc(mq_done.sem, 1)
                unit(l, "B", h, 1, 0, (kv_copied, kv_copied.at(l, "B", h, 1)), KVT, lambda k: (ckv_hi[:, k, :], ckv_lo[:, k, :]), first=QT * 96).then_inc(slot_done.sem, 1)

            def project_q(l, h):
                unit(l, "B", h, 2, 1, (mla_ready, mla_ready.at(l, "B", h, 1)), KD, h_rhs).then_inc(slot_done.sem, 1)

            def project_k(l, h):
                unit(l, "B", h, 3, 0, (kv_copied, kv_copied.at(l, "B", h, 2)), KD, h_rhs).then_inc(slot_done.sem, 1)

            def head(l, h, n):
                pe.wait_ge(mla_ready.sem, mla_ready.at(l, "B", h, 2))
                pe.wait_ge(ssq_read.sem, ssq_read.at(l, "B", h))
                causal_scores(l, h, 0, mqT, mkT, slice(0, 96))
                if n is not None:
                    project_v(l, n)
                pe.wait_ge(diff_ready.sem, diff_ready.at(l, "B", h, 2))
                causal_scores(l, h, 1, qT, kT, slice(0, 64))
                causal_flip(l, h, 0, 0)
                if n is not None:
                    project_latent(l, n)
                causal_flip(l, h, 0, 1)
                causal_scores(l, h, 2, qT, kT, slice(64, 128))
                if n is not None:
                    project_q(l, n)
                causal_attend(l, h, 0, mv_hi, mv_lo)
                causal_flip(l, h, 1, 0)
                if n is not None:
                    project_k(l, n)
                causal_flip(l, h, 1, 1)
                causal_attend(l, h, 1, v_hi, v_lo)
                if n is not None:
                    flip_values(l, n)
                pe.wait_ge(a_squared.sem, a_squared.at(l, "B", h, 1))
                mm(ssq[:, :], ones[:, :], a_sq[:, :], start=True, stop=True).then_inc(ssq_full.sem, 1)

            def cross_scores(l, i):
                pe.wait_ge(kv_copied.sem, kv_copied.at(l, "C", i, 3))
                pe.wait_ge(exp_done.sem, exp_done.at(l, "C", i))
                for b in range(2):
                    for t in (2 * b, 2 * b + 1):
                        ins = mm(score[b][:, (t % 2) * MEM:(t % 2 + 1) * MEM], qT[:, t * P:(t + 1) * P], kT[:, 0:MEM], start=True, stop=True)
                    ins.then_inc(score_full.sem, 1)

            def cross_flip(l, i):
                pe.wait_ge(prob_ready.sem, prob_ready.at(l, "C", i, 1))
                for j in range(NM):
                    b = flip_bank(l, "C", i, 2 + j)
                    for t in range(NT):
                        ins = nc.tensor.transpose(b[:, t * P:(t + 1) * P], p_a[:, t * MEM + j * P:t * MEM + (j + 1) * P], ident[:, :])
                    ins.then_inc(flip_full.sem, 1)

            def cross_attend(l, i):
                pe.wait_ge(flip_read.sem, flip_read.at(l, "C", i, 4))
                pe.wait_ge(att_read.sem, att_read.at(l, "C", i))
                product([(att[:, :], v_hi[:, j, :], v_lo[:, j, :], pt_hi[:, j * SEQ:(j + 1) * SEQ], pt_lo[:, j * SEQ:(j + 1) * SEQ])
                         for j in range(NM)]).then_inc(att_full.sem, 1)

            def flip_memory(l, i):
                pe.wait_ge(kv_copied.sem, kv_copied.at(l, "C", i, 3))
                for j in range(NM):
                    b = flip_bank(l, "C", i, j)
                    nc.tensor.transpose(b[:, 0:P], vT[:, j * P:(j + 1) * P], ident[:, :]).then_inc(flip_full.sem, 1)

            def project_xq(l, i, before=None):
                unit(l, "C", i, 0, 0, (kv_copied, kv_copied.at(l, "C", i)), KD, h_rhs, before=before).then_inc(slot_done.sem, 1)

            def project_mem(l, i, s, b, free):
                unit(l, "C", i, s, b, free, KD, lambda k: (mem_hi[:, k, :], mem_lo[:, k, :]), cols=MEM).then_inc(slot_done.sem, 1)

            def project_cq(l, i):
                unit(l, "C", i, 3, 1, (kv_copied, kv_copied.at(l, "C", i, 2)), KD, h_rhs).then_inc(slot_done.sem, 1)

            fills = []
            fills.append((lambda: pe.wait_ge(in_gain, 16 * (6 * DEPTH + 1)), [(0, gain_rows[:, :])]))
            for k in range(KD):
                fills.append((lambda: pe.wait_ge(in_x, 16 * NT), [(t, x_in[:, t, k * P:(k + 1) * P]) for t in range(NT)]))
            for f in range(KD // 2):
                fills.append((lambda: pe.wait_ge(mem_scaled, NM),
                              [(2 * e + t, mem_in[:, t, (2 * f + e) * P:(2 * f + e + 1) * P]) for e in range(2) for t in range(NM)]))
            for kind in range(4):
                fills.append((lambda: pe.wait_ge(rope_ready, 1), [(t, rope_t[:, kind, t, :]) for t in range(NT)]))
            pe.wait_ge(const_ready, 2)
            for n, (wait, blocks) in enumerate(fills):
                wait()
                if n >= 2:
                    pe.wait_ge(pre_read, n - 1)
                for c, src in blocks:
                    ins = nc.tensor.transpose(flip[n % 2][:, c * P:(c + 1) * P], src, ident[:, :])
                ins.then_inc(pre_full, 1)
            pe.wait_ge(pre_read, len(fills))

            with pe.Fori(0, DEPTH) as l:
                pe.wait_ge(sq_added.sem, sq_added.at(l, "C"))
                sum_squares(l, "N1", 0, x_sum[:, :])
                project_xq(l, 0, before=lambda k: pe.wait_ge(pair_lo.sem, pair_lo.at(l, "N1", 0, k + 1)))
                pe.wait_ge(memh_lo.sem, memh_lo.at(l, "N1", 0, KD))
                project_mem(l, 0, 1, 1, (tile_ready, tile_ready.at(l, "C")))
                project_mem(l, 0, 2, 0, (kv_copied, kv_copied.at(l, "C", 0, 1)))
                project_cq(l, 0)
                flip_memory(l, 0)
                with pe.Fori(0, CROSS - 1) as i:
                    cross_scores(l, i)
                    project_xq(l, i + 1)
                    cross_flip(l, i)
                    project_mem(l, i + 1, 1, 1, (tile_ready, tile_ready.at(l, "C", i + 1)))
                    cross_attend(l, i)
                    project_mem(l, i + 1, 2, 0, (kv_copied, kv_copied.at(l, "C", i + 1, 1)))
                    project_cq(l, i + 1)
                    flip_memory(l, i + 1)
                i = CROSS - 1
                cross_scores(l, i)
                unit(l, "A", 0, 0, 0, (kv_copied, kv_copied.at(l, "C", CROSS)), KD, h_rhs).then_inc(slot_done.sem, 1)
                pe.wait_ge(sq_added.sem, sq_added.at(l, "F"))
                sum_squares(l, "A", 0, q_sum[:, :])
                cross_flip(l, i)
                unit(l, "A", 0, 1, 1, (tile_ready, tile_ready.at(l, "C", CROSS)), KD, h_rhs).then_inc(slot_done.sem, 1)
                cross_attend(l, i)
                unit(l, "A", 0, 2, 0, (ckv_copied, ckv_copied.at(l, "A", 0, 1)), 4, h_rhs, width=96, stop=False).then_inc(slot_done.sem, 1)
                unit(l, "A", 0, 3, 0, None, 4, lambda k: h_rhs(k + 4), width=96, start=False).then_inc(slot_done.sem, 1)
                pe.wait_ge(ckv_squared.sem, ckv_squared.at(l, "A", 0, 2))
                sum_squares(l, "A", 1, ckv_sq[:, 0, :], ckv_sq[:, 1, :])
                pe.wait_ge(mla_ready.sem, mla_ready.at(l, "B", 0))
                project_v(l, 0)
                project_latent(l, 0, wait_norm=True)
                project_q(l, 0)
                project_k(l, 0)
                flip_values(l, 0)
                with pe.Fori(0, HEADS // 2 - 1) as hp:
                    for e in range(2):
                        head(l, hp * 2 + e, hp * 2 + (e + 1))
                head(l, HEADS - 2, HEADS - 1)
                head(l, HEADS - 1, None)
                with pe.Fori(0, 2) as jj:
                    for e in range(4):
                        s = 5 * e
                        unit(l, "E", jj, s, 0, (om_used, om_used.at(l, "E", jj, e)), KD, h_rhs).then_inc(slot_done.sem, 1)
                        unit(l, "E", jj, s + 1, 1, (oc_used, oc_used.at(l, "E", jj, e)), KD, h_rhs).then_inc(slot_done.sem, 1)
                        unit(l, "E", jj, s + 2, 0, (sig_ready, sig_ready.at(l, "E", jj, 3 * e + 1)), KD, h_rhs).then_inc(slot_done.sem, 1)

                        def split(k):
                            if e == 0:
                                pe.wait_ge(outs_split.sem, outs_split.at(l, "E", 0, k + 1))
                        unit(l, "E", jj, s + 3, 1, (sig_ready, sig_ready.at(l, "E", jj, 3 * e + 2)), KD,
                             lambda k: (outs_hi[:, k, :], outs_lo[:, k, :]), before=split).then_inc(slot_done.sem, 1)
                        unit(l, "E", jj, s + 4, 0, (sig_ready, sig_ready.at(l, "E", jj, 3 * e + 3)), 4,
                             lambda k: (outs_hi[:, 8 + k, :], outs_lo[:, 8 + k, :]), before=lambda k: split(8 + k)).then_inc(om_done.sem, 1)
                        unit(l, "E", jj, s + 4, 1, (od_used, od_used.at(l, "E", jj, e + 1)), 4,
                             lambda k: (outs_hi[:, 12 + k, :], outs_lo[:, 12 + k, :]), first=4 * P,
                             before=lambda k: split(12 + k)).then_inc(slot_done.sem, 1)
                with pe.Fori(0, 2) as jj:
                    for e in range(4):
                        def mixed(k):
                            if e == 0 and k == 0:
                                pe.wait_ge(om_used.sem, om_used.at(l, "E", 2))
                            if e == 0:
                                pe.wait_ge(mix_split.sem, mix_split.at(l, "E", 0, k + 1))
                        unit(l, "F", jj, e, e % 2, (tile_ready, tile_ready.at(l, "F", jj, e - 1)), KD,
                             lambda k: (mix_hi[:, k, :], mix_lo[:, k, :]), before=mixed).then_inc(slot_done.sem, 1)
                pe.wait_ge(sq_added.sem, sq_added.at(l, "H"))
                sum_squares(l, "N2", 0, x_sum[:, :])
                with pe.Fori(0, FT // 2) as t:
                    for e in range(2):
                        def normed(k):
                            if e == 0:
                                pe.wait_ge(pair_lo.sem, pair_lo.at(l, "N2", 0, k + 1))
                        unit(l, "G", t, 2 * e, 0, (gate_used, gate_used.at(l, "G", t, e)), KD, h_rhs, before=normed).then_inc(slot_done.sem, 1)
                        unit(l, "G", t, 2 * e + 1, 1, (hid_ready, hid_ready.at(l, "G", t, e)), KD, h_rhs).then_inc(slot_done.sem, 1)
                with pe.Fori(0, 4) as jj:
                    for e in range(2):
                        k = 0
                        for c, n in enumerate(DOWN):
                            if e == 0 and c == 0:
                                pe.wait_ge(gate_used.sem, gate_used.at(l, "G", FT // 2))
                            if e == 0:
                                pe.wait_ge(hid_split.sem, hid_split.at(l, "G", 0, k + n))
                            unit(l, "H", jj, 4 * e + c, e, (tile_ready, tile_ready.at(l, "H", jj, e - 1)) if c == 0 else None, n, lambda q, k=k: (hid_hi[:, k + q, :], hid_lo[:, k + q, :]),
                                 start=c == 0, stop=c == 3).then_inc(slot_done.sem, 1)
                            k += n
            pe.wait_ge(sq_added.sem, sq_added.end(DEPTH))
            pe.wait_ge(ssq_read.sem, ssq_read.end(DEPTH))
            mm(ssq[:, :], ones[:, :], x_sum[:, :], start=True, stop=True).then_inc(ssq_full.sem, 1)
            pe.wait_ge(y_ready, KD)
            for t in range(NT):
                for half in range(2):
                    n = 2 * t + half
                    if n >= 2:
                        pe.wait_ge(y_copied, n - 1)
                    for k in range(4):
                        ins = nc.tensor.transpose(flip[n % 2][:, k * P:(k + 1) * P], y_T[:, 4 * half + k, t * P:(t + 1) * P], ident[:, :])
                    ins.then_inc(y_flipped, 1)

        @block.scalar
        def _(act):
            sc = nc.scalar
            start_counts(act, "act")

            def copy(out, in_):
                return sc.activation(out, in_, ACT.Copy)

            def split_ahead(l, stage, step, s):
                n = slot_hi.index(l, stage, step, s)
                act.wait_ge(slot_done.sem, slot_done.at(l, stage, step, s))
                q = s + AHEAD
                act.wait_ge(raw_full[q % 2], n * 16 + (AHEAD * 16 + (16 if q % 2 else 32)))
                copy(w_hi[q % 4][:, :], raw[q % 2][:, :]).then_inc(slot_hi.sem, 1)

            def exps(l, stage, step, n, k, p, scale):
                _, bias, total, _ = stat[k]
                act.wait_ge(bias_ready.sem, bias_ready.at(l, stage, step, n + 1))
                for t in range(NT):
                    if stage == "C":
                        src, dst = score[t // 2][:, (t % 2) * MEM:(t % 2 + 1) * MEM], p[:, t * MEM:(t + 1) * MEM]
                    else:
                        b, c = {3: (0, 0), 2: (1, 0), 0: (1, 384), 1: (2, 0)}[t]
                        src, dst = score[b][:, c:c + (t + 1) * P], p[:, q_off(t):q_off(t) + (t + 1) * P]
                    sc.activation(dst, src, ACT.Exp, bias=bias[:, t:t + 1], scale=scale,
                                  accum_out=total[:, t:t + 1]).then_inc(exp_done.sem, 1)

            def flip_high(l, stage, step, k, dst, src):
                act.wait_ge(flip_full.sem, flip_full.at(l, stage, step, k + 1))
                copy(dst, src).then_inc(flip_hi.sem, 1)

            def causal_high(l, h, n, part):
                if part == 0:
                    act.wait_ge(att_full.sem, att_full.at(l, "B", h, n))
                    flip_high(l, "B", h, 2 + 3 * n, pt_hi[:, 0:512], flip[n][:, :])
                    flip_high(l, "B", h, 3 + 3 * n, pt_hi[:, 512:896], flip[1 - n][:, 0:384])
                else:
                    flip_high(l, "B", h, 4 + 3 * n, pt_hi[:, 896:1280], flip[n][:, 0:384])

            def values_high(l, h):
                act.wait_ge(att_full.sem, att_full.at(l, "B", h))
                flip_high(l, "B", h, 0, v_hi[:, :, :].rearrange("p j d -> p (j d)"), flip[0][:, :])
                flip_high(l, "B", h, 1, mv_hi[:, :, :].rearrange("p j d -> p (j d)"), flip[1][:, :])

            def out_v(l, h):
                act.wait_ge(slot_done.sem, slot_done.at(l, "B", h, 1))
                copy(vT[:, :], proj[0][:, :]).then_inc(kv_copied.sem, 1)

            def out_kv(l, h):
                act.wait_ge(slot_done.sem, slot_done.at(l, "B", h, 2))
                copy(kvT[:, :], proj[0][:, :]).then_inc(kv_copied.sem, 1)

            def squares(l, stage, step, k, src):
                act.wait_ge(tile_ready.sem, tile_ready.at(l, stage, step, k + 1))
                act.wait_ge(sq_added.sem, sq_added.at(l, stage, step, k))
                scale = (Q_LORA if stage == "C" else D) ** -0.5
                sc.activation(square[:, :], src, ACT.Square, scale=scale).then_inc(sq_done.sem, 1)

            def rms(l, stage, step, k):
                act.wait_ge(ssq_full.sem, ssq_full.at(l, stage, step, k + 1))
                sc.activation(rstd[:, :], ssq[:, :], ACT.Ln, bias=eps[:, 0:1]).then_inc(ssq_read.sem, 1)
                act.wait_ge(ssq_read.sem, ssq_read.at(l, stage, step, k + 1))
                sc.activation(rstd[:, :], rstd[:, :], ACT.Exp, scale=-0.5).then_inc(rms_ready.sem, 1)

            def pair_high(l, stage, k, dst):
                act.wait_ge(pair_ready.sem, pair_ready.at(l, stage, 0, k + 1))
                copy(dst, pair[:, k % 2, :]).then_inc(pair_hi.sem, 1)

            def head(l, h, n, e):
                exps(l, "B", h, 0, "m", p_a, MLA_SCALE)
                if n is not None:
                    split_ahead(l, "B", n, 0)
                    out_v(l, n)
                act.wait_ge(flip_full.sem, flip_full.at(l, "B", h))
                exps(l, "B", h, 1, "d1", p_b, DIFF_SCALE)
                causal_high(l, h, 0, 0)
                if n is not None:
                    split_ahead(l, "B", n, 1)
                causal_high(l, h, 0, 1)
                if n is not None:
                    out_kv(l, n)
                act.wait_ge(flip_full.sem, flip_full.at(l, "B", h, 5))
                exps(l, "B", h, 2, "d2", p_a, DIFF_SCALE)
                if n is not None:
                    split_ahead(l, "B", n, 2)
                act.wait_ge(att_full.sem, att_full.at(l, "B", h, 1))
                o = outs[64 * e:64 * e + 64, 8 + h // 2, :] if isinstance(h, int) else \
                    outs[64 * e:64 * e + 64, bass.ds(n_pair(h) + 8, 1), :].rearrange("p a n -> p (a n)")
                copy(o, att[64:128, :]).then_inc(att_read.sem, 1)
                causal_high(l, h, 1, 0)
                if n is not None:
                    split_ahead(l, "B", n, 3)
                causal_high(l, h, 1, 1)
                act.wait_ge(att_full.sem, att_full.at(l, "B", h, 2))
                act.wait_ge(ssq_full.sem, ssq_full.at(l, "B", h))
                sc.activation(a_sq[:, :], att[:, :], ACT.Square, scale=float(P) ** -0.5).then_inc(a_squared.sem, 1)
                if n is not None:
                    values_high(l, n)
                act.wait_ge(att_read.sem, att_read.at(l, "B", h))
                rms(l, "B", h, 0)

            pair_of = [None]

            def n_pair(h):
                return pair_of[0]

            def cross_step(l, i):
                exps(l, "C", i, 0, "m", p_a, CROSS_SCALE)

            def cross_high(l, i):
                act.wait_ge(att_full.sem, att_full.at(l, "C", i))
                for j in range(NM):
                    flip_high(l, "C", i, 2 + j, pt_hi[:, j * SEQ:(j + 1) * SEQ], flip[j][:, :])

            def memory_high(l, i):
                act.wait_ge(att_full.sem, att_full.at(l, "C", i))
                for j in range(NM):
                    flip_high(l, "C", i, j, v_hi[:, j, :], flip[j][:, 0:P])

            def out_cross(l, i, s, b, dst, cols):
                act.wait_ge(slot_done.sem, slot_done.at(l, "C", i, s + 1))
                copy(dst, proj[b][:, 0:cols]).then_inc(kv_copied.sem, 1)

            act.wait_ge(const_ready, 2)
            act.wait_ge(in_mem, 16 * NM)
            for t in range(NM):
                if t:
                    act.wait_ge(pre_act, t)
                sc.activation(mem_sq[:, :], mem_in[:, t, :], ACT.Square, scale=float(D) ** -0.5,
                              accum_out=mem_ss[:, t:t + 1]).then_inc(pre_act, 1)
            act.wait_ge(pre_vec, 1)
            sc.activation(sin_t[:, :, :], ang[:, :, :], ACT.Sin)
            sc.activation(half_t[:, :, :], ang[:, :, :], ACT.Sin, scale=0.5).then_inc(pre_act, 1)
            act.wait_ge(pre_vec, 2)
            sc.activation(lam_exp[:, :], lam_sum[:, :], ACT.Exp).then_inc(pre_act, 1)
            for k in range(KD):
                act.wait_ge(pre_read, k + 2)
                act.wait_ge(sq_added.sem, k + 1)
                sc.activation(square[:, :], xT[:, k, :], ACT.Square, scale=float(D) ** -0.5).then_inc(sq_done.sem, 1)

            act.wait_ge(pre_act, NM + 2)
            sc.activation(mem_rstd[:, :], mem_ss[:, :], ACT.Ln, bias=eps[:, 0:1]).then_inc(pre_act, 1)
            act.wait_ge(pre_act, NM + 3)
            sc.activation(mem_rstd[:, :], mem_rstd[:, :], ACT.Exp, scale=-0.5).then_inc(pre_act, 1)
            for s in range(AHEAD + 1):
                act.wait_ge(raw_full[s % 2], 32 * (s // 2 + 1))
                copy(w_hi[s][:, :], raw[s % 2][:, :]).then_inc(slot_hi.sem, 1)
            act.wait_ge(pre_read, 1 + KD + KD // 2)
            act.dma_start(mem_scratch[:, :, :], mem_t[:, :, :]).then_inc(mem_stored, 16)
            act.wait_ge(pre_read, 1 + KD + KD // 2 + 4)

            with act.Fori(0, DEPTH) as l:
                act.wait_ge(mem_stored, 16)
                act.wait_ge(slot_done.sem, slot_done.at(l, "C"))
                act.dma_start(mem_n[:, :, :], mem_scratch[:, :, :]).then_inc(mem_loaded.sem, 16)
                sc.activation(warm[:, :], eps[:, :], ACT.Ln)
                rms(l, "N1", 0, 0)
                for k in range(KD):
                    pair_high(l, "N1", k, h_hi[:, k, :])
                act.wait_ge(gl_ready.sem, gl_ready.at(l, "N1", 0, 1))
                act.wait_ge(mem_loaded.sem, mem_loaded.at(l, "N1", 0, 16))
                for k in range(KD):
                    sc.activation(mem_hi[:, k, :], mem_n[:, k, :], ACT.Copy, scale=gl[:, G_MEM + k:G_MEM + k + 1]).then_inc(memh_hi.sem, 1)
                out_cross(l, 0, 0, 0, qT[:, :], SEQ)
                split_ahead(l, "C", 0, 1)
                out_cross(l, 0, 1, 1, kT[:, 0:MEM], MEM)
                split_ahead(l, "C", 0, 2)
                out_cross(l, 0, 2, 0, vT[:, 0:MEM], MEM)
                split_ahead(l, "C", 0, 3)
                squares(l, "C", 0, 0, cq_raw[:, 0, :])
                memory_high(l, 0)
                with act.Fori(0, CROSS - 1) as i:
                    cross_step(l, i)
                    split_ahead(l, "C", i + 1, 0)
                    out_cross(l, i + 1, 0, 0, qT[:, :], SEQ)
                    cross_high(l, i)
                    split_ahead(l, "C", i + 1, 1)
                    out_cross(l, i + 1, 1, 1, kT[:, 0:MEM], MEM)
                    split_ahead(l, "C", i + 1, 2)
                    out_cross(l, i + 1, 2, 0, vT[:, 0:MEM], MEM)
                    split_ahead(l, "C", i + 1, 3)
                    squares(l, "C", i + 1, 0, cq_raw[:, bass.ds(i + 1, 1), :].rearrange("p a n -> p (a n)"))
                    memory_high(l, i + 1)
                i = CROSS - 1
                cross_step(l, i)
                split_ahead(l, "A", 0, 0)
                for j in range(KVT):
                    act.wait_ge(ckv_copied.sem, ckv_copied.at(l, "A", 0, j + 1))
                    sc.activation(ckv_sq[:, j, :], ckv_raw[:, j, :], ACT.Square, scale=float(KV_LORA) ** -0.5).then_inc(ckv_squared.sem, 1)
                    if j == 0:
                        cross_high(l, i)
                        rms(l, "A", 0, 0)
                        split_ahead(l, "A", 0, 1)
                        for k in range(QT):
                            pair_high(l, "A", k, cq_hi[:, k, :])
                        split_ahead(l, "A", 0, 2)
                split_ahead(l, "A", 0, 3)
                rms(l, "A", 0, 1)
                for k in range(KVT):
                    pair_high(l, "A", QT + k, ckv_hi[:, k, :])
                split_ahead(l, "B", 0, 0)
                out_v(l, 0)
                split_ahead(l, "B", 0, 1)
                out_kv(l, 0)
                split_ahead(l, "B", 0, 2)
                split_ahead(l, "B", 0, 3)
                values_high(l, 0)
                with act.Fori(0, HEADS // 2 - 1) as hp:
                    pair_of[0] = hp
                    for e in range(2):
                        head(l, hp * 2 + e, hp * 2 + (e + 1), e)
                head(l, HEADS - 2, HEADS - 1, 0)
                head(l, HEADS - 1, None, 1)
                sc.activation(warm[:, :], eps[:, :], ACT.Sigmoid)
                act.wait_ge(att_read.sem, att_read.at(l, "B", HEADS))
                split_ahead(l, "E", 0, 0)
                for k in range(16):
                    copy(outs_hi[:, k, :], outs[:, k, :]).then_inc(outs_split_hi.sem, 1)
                with act.Fori(0, 2) as jj:
                    for e in range(4):
                        for g in range(3):
                            s = 5 * e + g
                            if s:
                                split_ahead(l, "E", jj, s)
                            act.wait_ge(slot_done.sem, slot_done.at(l, "E", jj, s + 1))
                            act.wait_ge(mix_ready.sem, mix_ready.at(l, "E", jj, e))
                            sc.activation(sig[:, g, :], proj[g % 2][:, :], ACT.Sigmoid).then_inc(sig_ready.sem, 1)
                        split_ahead(l, "E", jj, 5 * e + 3)
                        split_ahead(l, "E", jj, 5 * e + 4)
                        if e == 3:
                            split_ahead(l, "E", jj, 20)
                        act.wait_ge(mix_ready.sem, mix_ready.at(l, "E", jj, e + 1))
                        copy(mix_hi[:, bass.ds(jj * 4 + e, 1), :].rearrange("p a n -> p (a n)"), mix[:, :]).then_inc(mix_split_hi.sem, 1)
                with act.Fori(0, 2) as jj:
                    for e in range(4):
                        if e:
                            split_ahead(l, "F", jj, e)
                        if e == 3:
                            split_ahead(l, "F", jj, 4)
                        squares(l, "F", jj, e, xT[:, bass.ds(jj * 4 + e, 1), :].rearrange("p a n -> p (a n)"))
                rms(l, "N2", 0, 0)
                sc.activation(warm[:, :], eps[:, :], ACT.Sigmoid)
                for k in range(KD):
                    pair_high(l, "N2", k, h_hi[:, k, :])
                with act.Fori(0, FT // 2) as t:
                    for e in range(2):
                        if e:
                            split_ahead(l, "G", t, 2)
                        act.wait_ge(slot_done.sem, slot_done.at(l, "G", t, 2 * e + 1))
                        act.wait_ge(gate_used.sem, gate_used.at(l, "G", t))
                        sc.activation(sig_f[:, e, :], proj[0][:, :], ACT.Sigmoid).then_inc(silu_sig.sem, 1)
                        split_ahead(l, "G", t, 2 * e + 1)
                        act.wait_ge(hid_ready.sem, hid_ready.at(l, "G", t, e + 1))
                        copy(hid_hi[:, bass.ds(t * 2 + e, 1), :].rearrange("p a n -> p (a n)"), hid[:, e, :]).then_inc(hid_split_hi.sem, 1)
                    split_ahead(l, "G", t, 4)
                with act.Fori(0, 4) as jj:
                    for e in range(2):
                        for c in range(4):
                            if e or c:
                                split_ahead(l, "H", jj, 4 * e + c)
                        if e:
                            split_ahead(l, "H", jj, 8)
                        squares(l, "H", jj, e, xT[:, bass.ds(jj * 2 + e, 1), :].rearrange("p a n -> p (a n)"))
            act.wait_ge(ssq_full.sem, ssq_full.end(DEPTH) + 1)
            sc.activation(rstd[:, :], ssq[:, :], ACT.Ln, bias=eps[:, 0:1]).then_inc(ssq_read.sem, 1)
            act.wait_ge(ssq_read.sem, ssq_read.end(DEPTH) + 1)
            sc.activation(rstd[:, :], rstd[:, :], ACT.Exp, scale=-0.5).then_inc(rms_ready.sem, 1)
            for n in range(1, 2 * NT, 2):
                act.wait_ge(y_flipped, n + 1)
                act.wait_ge(y_copied, n)
                copy(y_out[:, n // 2, 512:1024], flip[1][:, :]).then_inc(y_copied, 1)

        @block.vector
        def _(ve):
            v = nc.vector
            start_counts(ve, "ve")
            state = {"origin": 0, "n": 0}

            def begin(l, stage, step=0):
                state["origin"], state["n"] = vec_step.at(l, stage, step), 0

            def end(stage):
                assert state["n"] == vec_step.start[stage][1], (stage, state["n"])

            def chain(ins):
                state["n"] += 1
                ins.then_inc(vec_step.sem, 1)
                ve.wait_ge(vec_step.sem, state["origin"] + state["n"])

            def one(t, i):
                return t[:, bass.ds(i, 1), :].rearrange("p a n -> p (a n)") if not isinstance(i, int) else t[:, i, :]

            SHUF_D = [(i + 8) % 16 if i < 16 else i for i in range(32)]
            SHUF_M = [(i + 16) % 32 for i in range(32)]

            def rope(dst, src, rows, cos, sin, mask, last):
                ve.wait_ge(last[0].sem, last[1])
                v.tensor_tensor(mid[rows, :], src[rows, :], cos[rows, :], ALU.mult)
                chain(v.stream_shuffle(rot[rows, :], src[rows, :], mask))
                chain(v.tensor_tensor(rot[rows, :], rot[rows, :], sin[rows, :], ALU.mult))
                return v.tensor_tensor(dst[rows, :], mid[rows, :], rot[rows, :], ALU.add)

            def maxima(l, stage, step, n, k, scale):
                top, bias, _, _ = stat[k]
                for t in (range(NT) if stage == "C" else (3, 2, 0, 1)):
                    if stage == "C":
                        full, src = t // 2 + 1, score[t // 2][:, (t % 2) * MEM:(t % 2 + 1) * MEM]
                    else:
                        b, c = {3: (0, 0), 2: (1, 0), 0: (1, 384), 1: (2, 0)}[t]
                        full, src = b + 1, score[b][:, c:c + (t + 1) * P]
                    if stage == "C" and t % 2 == 0 or stage == "B" and t != 0:
                        ve.wait_ge(score_full.sem, score_full.at(l, stage, step, 3 * n + full))
                    ins = v.tensor_reduce(top[:, t:t + 1], src, AX.X, ALU.max)
                chain(ins)
                v.tensor_scalar(bias[:, :], top[:, :], -scale, None, ALU.mult).then_inc(bias_ready.sem, 1)

            def invert(l, stage, step, n, k):
                _, _, total, inv = stat[k]
                ve.wait_ge(exp_done.sem, exp_done.at(l, stage, step, 4 * (n + 1)))
                chain(v.reciprocal(inv[:, :], total[:, :]))

            def normalise(p, inv, off, size):
                for t in range(NT):
                    s = p[:, off(t):off(t) + size(t)]
                    ins = v.tensor_scalar(s, s, inv[:, t:t + 1], None, ALU.mult)
                return ins

            def flip_low(l, stage, step, k, dst, src, hi):
                ve.wait_ge(flip_hi.sem, flip_hi.at(l, stage, step, k + 1))
                v.tensor_tensor(dst, src, hi.bitcast(F32), ALU.subtract).then_inc(flip_read.sem, 1)

            def causal_low(l, h, n, part):
                if part == 0:
                    flip_low(l, "B", h, 2 + 3 * n, pt_lo[:, 0:512], flip[n][:, :], pt_hi[:, 0:512])
                    flip_low(l, "B", h, 3 + 3 * n, pt_lo[:, 512:896], flip[1 - n][:, 0:384], pt_hi[:, 512:896])
                else:
                    flip_low(l, "B", h, 4 + 3 * n, pt_lo[:, 896:1280], flip[n][:, 0:384], pt_hi[:, 896:1280])

            def values_low(l, h):
                for k, (lo, hi) in enumerate(((v_lo, v_hi), (mv_lo, mv_hi))):
                    flip_low(l, "B", h, k, lo[:, :, :].rearrange("p j d -> p (j d)"), flip[k][:, :],
                             hi[:, :, :].rearrange("p j d -> p (j d)"))

            def out_latent(l, h, last=None):
                ve.wait_ge(mq_done.sem, mq_done.at(l, "B", h, 1))
                last = last or (diff_ready, diff_ready.at(l, "B", h))
                rope(mqT, proj[1], slice(0, 96), cos_m, sin_m, SHUF_M, last).then_inc(mla_ready.sem, 1)
                ve.wait_ge(kv_copied.sem, kv_copied.at(l, "B", h, 2))
                v.tensor_copy(mkT[0:64, :], kvT[0:64, :]).then_inc(mla_ready.sem, 1)

            def out_qk(l, h, s, b, dst):
                ve.wait_ge(slot_done.sem, slot_done.at(l, "B", h, s + 1))
                last = (mla_ready, mla_ready.at(l, "B", h, 1)) if s == 2 else (diff_ready, diff_ready.at(l, "B", h, 1))
                rope(dst, proj[b], slice(0, P), cos_d, sin_d, SHUF_D, last).then_inc(diff_ready.sem, 1)

            def rms(l, stage, k):
                ve.wait_ge(rms_ready.sem, rms_ready.at(l, stage, 0, k + 1))

            def norm(l, stage, k0, src, gain, n, hi, lo):
                def low(k):
                    ve.wait_ge(pair_hi.sem, pair_hi.at(l, stage, 0, k0 + k + 1))
                    v.tensor_tensor(lo[:, k, :], pair[:, (k0 + k) % 2, :], hi[:, k, :].bitcast(F32), ALU.subtract).then_inc(pair_lo.sem, 1)
                for k in range(n):
                    if k >= 2:
                        ve.wait_ge(pair_lo.sem, pair_lo.at(l, stage, 0, k0 + k - 1))
                    v.scalar_tensor_tensor(pair[:, (k0 + k) % 2, :], src[:, k, :], gl[:, gain + k:gain + k + 1], rstd[:, :],
                                           ALU.mult, ALU.mult).then_inc(pair_ready.sem, 1)
                    if k:
                        low(k - 1)
                low(n - 1)

            def add_square(l, stage, step, k, acc):
                ve.wait_ge(sq_done.sem, sq_done.at(l, stage, step, k + 1))
                v.tensor_tensor(acc[:, :], acc[:, :], square[:, :], ALU.add).then_inc(sq_added.sem, 1)
                ve.wait_ge(sq_added.sem, sq_added.at(l, stage, step, k + 1))

            def head(l, h, n):
                begin(l, "B" if n is not None else "L", h if n is not None else 0)
                maxima(l, "B", h, 0, "m", MLA_SCALE)
                invert(l, "B", h, 0, "m")
                normalise(p_a, stat["m"][3], q_off, lambda t: (t + 1) * P).then_inc(prob_ready.sem, 1)
                maxima(l, "B", h, 1, "d1", DIFF_SCALE)
                causal_low(l, h, 0, 0)
                if n is not None:
                    out_latent(l, n)
                causal_low(l, h, 0, 1)
                invert(l, "B", h, 1, "d1")
                chain(normalise(p_b, stat["d1"][3], q_off, lambda t: (t + 1) * P))
                maxima(l, "B", h, 2, "d2", DIFF_SCALE)
                invert(l, "B", h, 2, "d2")
                chain(v.tensor_scalar(lam_scale[:, :], stat["d2"][3][:, :], gl[:, G_LAM:G_LAM + 1], None, ALU.mult))
                for t in range(NT):
                    s = slice(q_off(t), q_off(t) + (t + 1) * P)
                    ins = v.scalar_tensor_tensor(p_b[:, s], p_a[:, s], lam_scale[:, t:t + 1], p_b[:, s], ALU.mult, ALU.add)
                ins.then_inc(prob_ready.sem, 1)
                if n is not None:
                    out_qk(l, n, 2, 1, qT)
                causal_low(l, h, 1, 0)
                if n is not None:
                    out_qk(l, n, 3, 0, kT)
                causal_low(l, h, 1, 1)
                if n is not None:
                    values_low(l, n)
                ve.wait_ge(rms_ready.sem, rms_ready.at(l, "B", h, 1))
                v.scalar_tensor_tensor(one(outs, h), att[:, :], gl[:, G_SUB:G_SUB + 1], rstd[:, :], ALU.mult, ALU.mult).then_inc(att_read.sem, 1)

                end("B" if n is not None else "L")

            def cross_prob(l, i):
                maxima(l, "C", i, 0, "m", CROSS_SCALE)
                invert(l, "C", i, 0, "m")
                normalise(p_a, stat["m"][3], lambda t: t * MEM, lambda t: MEM).then_inc(prob_ready.sem, 1)

            def cross_low(l, i):
                for j in range(NM):
                    s = slice(j * SEQ, (j + 1) * SEQ)
                    flip_low(l, "C", i, 2 + j, pt_lo[:, s], flip[j][:, :], pt_hi[:, s])

            def memory_low(l, i):
                for j in range(NM):
                    flip_low(l, "C", i, j, v_lo[:, j, :], flip[j][:, 0:P], v_hi[:, j, :])

            def cross_out(l, i):
                ve.wait_ge(att_full.sem, att_full.at(l, "C", i, 1))
                v.tensor_copy(one(outs, i + 12), att[:, :]).then_inc(att_read.sem, 1)

            def out_cq(l, i):
                ve.wait_ge(slot_done.sem, slot_done.at(l, "C", i, 4))
                v.tensor_copy(one(cq_raw, i), proj[1][:, :]).then_inc(tile_ready.sem, 1)
                add_square(l, "C", i, 0, q_sum)

            def out_residual(l, stage, step, k, s, b, tile):
                ve.wait_ge(slot_done.sem, slot_done.at(l, stage, step, s))
                v.tensor_tensor(one(xT, tile), one(xT, tile), proj[b][:, :], ALU.add).then_inc(tile_ready.sem, 1)
                add_square(l, stage, step, k, x_sum)

            pre = [0]

            def now(ins):
                pre[0] += 1
                ins.then_inc(pre_chain, 1)
                ve.wait_ge(pre_chain, pre[0])

            def fill(n, dst, cols=512):
                ve.wait_ge(pre_full, n + 1)
                v.tensor_copy(dst, flip[n % 2][:, 0:cols]).then_inc(pre_read, 1)

            ve.wait_ge(const_ready, 2)
            ve.wait_ge(in_pos, 16)
            now(v.tensor_copy(pos_f[:, :], pos_i[:, :]))
            for t in range(NT):
                ins = v.tensor_scalar(ang[:, t, :], freq[:, :], pos_f[:, t:t + 1], None, ALU.mult)
            now(ins)
            magic = 1.5 * 2 ** 23
            now(v.tensor_scalar(turns[:, :, :], ang[:, :, :], 1 / (2 * math.pi), magic, ALU.mult, ALU.add))
            now(v.tensor_scalar(turns[:, :, :], turns[:, :, :], -magic, None, ALU.add))
            c1 = 6.28125
            c2 = float(np.float32(math.floor((2 * math.pi - c1) * 2 ** 20) / 2 ** 20))
            c3 = 2 * math.pi - c1 - c2
            for c in (c1, c2, c3):
                now(v.scalar_tensor_tensor(ang[:, :, :], turns[:, :, :], -c, ang[:, :, :], ALU.mult, ALU.add))
            v.tensor_scalar(ang[:, :, :], ang[:, :, :], 3.1415925, -3.1415925, ALU.min, ALU.max).then_inc(pre_vec, 1)
            ve.wait_ge(in_lam, 16)
            pairs = lam_in[:, :, :, :].rearrange("p l (a b) d -> p (l a) b d", b=2)
            now(v.tensor_tensor(lam_prod[:, :, :], pairs[:, :, 0, :], pairs[:, :, 1, :], ALU.mult))
            v.tensor_reduce(lam_sum[:, :], lam_prod[:, :, :], AX.X, ALU.add).then_inc(pre_vec, 1)
            ve.wait_ge(pre_full, 1)
            v.tensor_copy(gains[:, :], flip[0][:, 0:P]).then_inc(pre_read, 1)
            for k in range(KD):
                fill(1 + k, xT[:, k, :])
                if k:
                    ve.wait_ge(sq_done.sem, k + 1)
                    v.tensor_tensor(x_sum[:, :], x_sum[:, :], square[:, :], ALU.add).then_inc(sq_added.sem, 1)
                    ve.wait_ge(sq_added.sem, k + 1)
            ve.wait_ge(sq_done.sem, KD + 1)
            v.tensor_tensor(x_sum[:, :], x_sum[:, :], square[:, :], ALU.add).then_inc(sq_added.sem, 1)
            ve.wait_ge(pre_act, NM + 4)
            for t in range(NM):
                v.tensor_scalar(mem_in[:, t, :], mem_in[:, t, :], mem_rstd[:, t:t + 1], None, ALU.mult).then_inc(mem_scaled, 1)
            for f in range(KD // 2):
                fill(1 + KD + f, mem_t[:, 2 * f:2 * f + 2, :].rearrange("p k n -> p (k n)"))
            ve.wait_ge(pre_act, NM + 1)
            now(v.tensor_tensor(cos_t[:, :, :], half_t[:, :, :], half_t[:, :, :], ALU.mult))
            v.tensor_scalar(neg_t[:, :, :], sin_t[:, :, :], -1.0, None, ALU.mult)
            now(v.tensor_scalar(cos_t[:, :, :], cos_t[:, :, :], -2.0, 1.0, ALU.mult, ALU.add))
            for c0, half, f0, kind in ((0, 8, 0, 0), (64, 8, 0, 0), (64, 16, 8, 2)):
                f = slice(f0, f0 + half)
                a, b = slice(c0, c0 + half), slice(c0 + half, c0 + 2 * half)
                v.tensor_copy(rope_t[:, kind, :, a], cos_t[:, :, f])
                v.tensor_copy(rope_t[:, kind, :, b], cos_t[:, :, f])
                v.tensor_copy(rope_t[:, kind + 1, :, a], neg_t[:, :, f])
                ins = v.tensor_copy(rope_t[:, kind + 1, :, b], sin_t[:, :, f])
            ins.then_inc(rope_ready, 1)
            ve.wait_ge(pre_act, NM + 2)
            ve.wait_ge(pre_read, 1)
            for l in range(DEPTH):
                lam_init = 0.8 - 0.6 * math.exp(-0.3 * l)
                sub = gains[:, l * G_N + G_SUB:l * G_N + G_SUB + 1]
                lam = gains[:, l * G_N + G_LAM:l * G_N + G_LAM + 1]
                now(v.tensor_tensor(lam, lam_exp[:, 2 * l + 1:2 * l + 2], lam_exp[:, 2 * l:2 * l + 1], ALU.subtract))
                v.tensor_scalar(lam, lam, -lam_init, None, ALU.add)
                now(v.tensor_scalar(sub, sub, 1.0 - lam_init, None, ALU.mult))
            for kind, t in enumerate((cos_d, sin_d, cos_m, sin_m)):
                fill(1 + KD + KD // 2 + kind, t[:, :])

            with ve.Fori(0, DEPTH) as l:
                begin(l, "N1")
                v.tensor_copy(gl[:, :], gains[:, bass.ds(l * G_N, G_N)]).then_inc(gl_ready.sem, 1)
                ve.wait_ge(gl_ready.sem, gl_ready.at(l, "N1", 0, 1))
                rms(l, "N1", 0)
                chain(v.memset(x_sum[:, :], 0.0))
                norm(l, "N1", 0, xT, G_ATTN, KD, h_hi, h_lo)
                for k in range(KD):
                    ve.wait_ge(memh_hi.sem, memh_hi.at(l, "N1", 0, k + 1))
                    v.scalar_tensor_tensor(mem_lo[:, k, :], mem_n[:, k, :], gl[:, G_MEM + k:G_MEM + k + 1],
                                           mem_hi[:, k, :].bitcast(F32), ALU.mult, ALU.subtract).then_inc(memh_lo.sem, 1)
                chain(v.memset(q_sum[:, :], 0.0))
                end("N1")
                out_cq(l, 0)
                memory_low(l, 0)
                with ve.Fori(0, CROSS - 1) as i:
                    begin(l, "C", i)
                    cross_prob(l, i)
                    cross_low(l, i)
                    cross_out(l, i)
                    out_cq(l, i + 1)
                    memory_low(l, i + 1)
                    end("C")
                i = CROSS - 1
                begin(l, "C", i)
                cross_prob(l, i)
                end("C")
                begin(l, "A")

                def out_ckv(j):
                    ve.wait_ge(slot_done.sem, slot_done.at(l, "A", 0, j + 1))
                    v.tensor_copy(ckv_raw[:, j, :], proj[j][:, :]).then_inc(ckv_copied.sem, 1)
                out_ckv(0)
                cross_low(l, i)
                rms(l, "A", 0)
                out_ckv(1)
                norm(l, "A", 0, cq_raw, G_Q, QT, cq_hi, cq_lo)
                cross_out(l, i)
                ve.wait_ge(slot_done.sem, slot_done.at(l, "A", 0, 4))
                rope(mkT, proj[0], slice(64, 96), cos_m, sin_m, SHUF_M, (pair_lo, pair_lo.at(l, "A", 0, QT))).then_inc(mla_ready.sem, 1)
                ve.wait_ge(mla_ready.sem, mla_ready.at(l, "A", 0, 1))
                rms(l, "A", 1)
                ve.wait_ge(ckv_squared.sem, ckv_squared.at(l, "A", 0, 2))
                norm(l, "A", QT, ckv_raw, G_KV, KVT, ckv_hi, ckv_lo)
                end("A")
                begin(l, "P")
                out_latent(l, 0, (pair_lo, pair_lo.at(l, "A", 0, QT + KVT)))
                out_qk(l, 0, 2, 1, qT)
                out_qk(l, 0, 3, 0, kT)
                values_low(l, 0)
                end("P")
                with ve.Fori(0, HEADS // 2 - 1) as hp:
                    for e in range(2):
                        head(l, hp * 2 + e, hp * 2 + (e + 1))
                head(l, HEADS - 2, HEADS - 1)
                head(l, HEADS - 1, None)
                for k in range(16):
                    ve.wait_ge(outs_split_hi.sem, outs_split_hi.at(l, "E", 0, k + 1))
                    v.tensor_tensor(outs_lo[:, k, :], outs[:, k, :], outs_hi[:, k, :].bitcast(F32), ALU.subtract).then_inc(outs_split.sem, 1)
                with ve.Fori(0, 2) as jj:
                    begin(l, "E", jj)
                    for e in range(4):
                        ve.wait_ge(sig_ready.sem, sig_ready.at(l, "E", jj, 3 * e + 3))
                        ve.wait_ge(slot_done.sem, slot_done.at(l, "E", jj, 5 * e + 4))
                        ve.wait_ge(mix_split.sem, mix_split.at(l, "E", jj, e))
                        v.tensor_tensor(mix[:, :], proj[1][:, :], sig[:, 0, :], ALU.mult).then_inc(od_used.sem, 1)
                        ve.wait_ge(om_done.sem, om_done.at(l, "E", jj, e + 1))
                        v.tensor_tensor(sig[:, 1, :], proj[0][:, :], sig[:, 1, :], ALU.mult).then_inc(om_used.sem, 1)
                        ve.wait_ge(om_used.sem, om_used.at(l, "E", jj, e + 1))
                        chain(v.tensor_tensor(mix[:, :], mix[:, :], sig[:, 1, :], ALU.add))
                        ve.wait_ge(slot_done.sem, slot_done.at(l, "E", jj, 5 * e + 5))
                        v.tensor_tensor(sig[:, 2, :], proj[1][:, :], sig[:, 2, :], ALU.mult).then_inc(oc_used.sem, 1)
                        ve.wait_ge(oc_used.sem, oc_used.at(l, "E", jj, e + 1))
                        v.tensor_tensor(mix[:, :], mix[:, :], sig[:, 2, :], ALU.add).then_inc(mix_ready.sem, 1)
                        ve.wait_ge(mix_split_hi.sem, mix_split_hi.at(l, "E", jj, e + 1))
                        tile = jj * 4 + e
                        v.tensor_tensor(one(mix_lo, tile), mix[:, :], one(mix_hi, tile).bitcast(F32), ALU.subtract).then_inc(mix_split.sem, 1)
                    end("E")
                with ve.Fori(0, 2) as jj:
                    for e in range(4):
                        out_residual(l, "F", jj, e, e + 1, e % 2, jj * 4 + e)
                begin(l, "N2")
                rms(l, "N2", 0)
                chain(v.memset(x_sum[:, :], 0.0))
                end("N2")
                norm(l, "N2", 0, xT, G_FFN, KD, h_hi, h_lo)
                with ve.Fori(0, FT // 2) as t:
                    for e in range(2):
                        ve.wait_ge(silu_sig.sem, silu_sig.at(l, "G", t, e + 1))
                        ve.wait_ge(hid_split.sem, hid_split.at(l, "G", t, e))
                        v.tensor_tensor(gated[:, :], proj[0][:, :], sig_f[:, e, :], ALU.mult).then_inc(gate_used.sem, 1)
                        ve.wait_ge(gate_used.sem, gate_used.at(l, "G", t, e + 1))
                        ve.wait_ge(slot_done.sem, slot_done.at(l, "G", t, 2 * e + 2))
                        v.tensor_tensor(hid[:, e, :], proj[1][:, :], gated[:, :], ALU.mult).then_inc(hid_ready.sem, 1)
                        ve.wait_ge(hid_split_hi.sem, hid_split_hi.at(l, "G", t, e + 1))
                        tile = t * 2 + e
                        v.tensor_tensor(one(hid_lo, tile), hid[:, e, :], one(hid_hi, tile).bitcast(F32), ALU.subtract).then_inc(hid_split.sem, 1)
                with ve.Fori(0, 4) as jj:
                    for e in range(2):
                        out_residual(l, "H", jj, e, 4 * e + 4, e, jj * 2 + e)
            ve.wait_ge(rms_ready.sem, rms_ready.end(DEPTH) + 1)
            for k in range(KD):
                c = DEPTH * G_N + k
                v.scalar_tensor_tensor(y_T[:, k, :], xT[:, k, :], gains[:, c:c + 1], rstd[:, :], ALU.mult, ALU.mult).then_inc(y_ready, 1)
            for n in range(0, 2 * NT, 2):
                ve.wait_ge(y_flipped, n + 1)
                ve.wait_ge(y_copied, n)
                v.tensor_copy(y_out[:, n // 2, 0:512], flip[0][:, :]).then_inc(y_copied, 1)


def kernel(**inputs):
    import concourse.bacc as bacc
    from concourse.bass_utils import run_bass_kernel_spmd

    names = ["x", "mem", "positions", "attn_norm_w", "w_in", "diff_lambda", "diff_subln_w", "w_o_diff", "mla_q_norm_w",
             "mla_w_uq", "mla_kv_norm_w", "mla_w_ukv", "w_o_mla", "mem_norm_w", "w_mem_kv", "w_o_cross", "w_out",
             "ffn_norm_w", "w_gate_up", "w_down", "final_norm_w"]
    nc = bacc.Bacc("TRN2", target_bir_lowering=False, num_devices=1)
    arrays, args = {}, []
    for name in names:
        a = np.ascontiguousarray(inputs[name])
        arrays[f"in_{name}"] = a
        args.append(nc.dram_tensor(f"in_{name}", a.shape, mybir.dt.from_np(a.dtype), kind="ExternalInput").ap())
    args.append(nc.dram_tensor("out", (1, SEQ, D), F32, kind="ExternalOutput").ap())
    args.append(nc.dram_tensor("mem_scratch", (P, KD, MEM), F32, kind="Internal").ap())
    build_trunk(nc, *args)
    r = run_bass_kernel_spmd(nc, [arrays], core_ids=[0])
    return r.results[0]["out"]
```

```python
import math
from contextlib import ExitStack

import numpy as np
import concourse.bass as bass
from concourse import mybir

F32 = mybir.dt.float32
F32R = mybir.dt.float32r
BF16 = mybir.dt.bfloat16
I32 = mybir.dt.int32
ACT = mybir.ActivationFunctionType
ALU = mybir.AluOpType
AX = mybir.AxisListType

P = 128
D = 1024
SEQ = 512
MEM = 256
DEPTH = 2
EPS = 1e-6
THETA = 500000.0
KD = D // P
NT = SEQ // P
NM = MEM // P
HEADS = 8
CROSS = 4
ROT_D, ROT_M = 16, 32
Q_LORA, KV_LORA = 512, 256
QT, KVT = Q_LORA // P, KV_LORA // P
FFN = 2816
FT = FFN // P
DOWN = (6, 6, 5, 5)
DIFF_SCALE = 64 ** -0.5
MLA_SCALE = 96 ** -0.5
CROSS_SCALE = 128 ** -0.5
C_DQ, C_DK, C_DV, C_CQ, C_CKV, C_KR, C_XQ, C_GATE = 0, 1024, 2048, 3072, 3584, 3840, 3872, 4384
MASKED = -3.0e38
LN_EXP = "natural_log_exp_and_others"
AHEAD = 3
CAUSAL = NT * (NT + 1) // 2 * P
G_ATTN, G_FFN, G_MEM, G_Q, G_KV, G_SUB, G_LAM, G_N = 0, 8, 16, 24, 28, 30, 31, 32


def q_off(t):
    return P * t * (t + 1) // 2


def k_off(j):
    return P * (NT * j - j * (j - 1) // 2)


class Tally:

    def __init__(self, sem, by, before=1, **stages):
        self.sem, self.by, self.start, total = sem, by, {}, 0
        for name, (per, steps) in stages.items():
            self.start[name] = (total, per)
            total += per * steps
        self.total, self.before = total, before

    def at(self, layer, stage, step=0, k=0):
        base, per = self.start[stage]
        return layer * self.total + step * per + (self.before + base + k)

    def index(self, layer, stage, step=0, k=0):
        base, per = self.start[stage]
        return layer * self.total + step * per + (base + k)

    def end(self, layers):
        return self.before + layers * self.total


def build_trunk(nc, x, mem, positions, attn_norm_w, w_in, diff_lambda, diff_subln_w, w_o_diff,
                mla_q_norm_w, mla_w_uq, mla_kv_norm_w, mla_w_ukv, w_o_mla, mem_norm_w, w_mem_kv,
                w_o_cross, w_out, ffn_norm_w, w_gate_up, w_down, final_norm_w, out, mem_scratch, table_scratch):
    ctx = ExitStack()
    with ctx:
        def sem(name):
            return ctx.enter_context(nc.semaphore(name))

        def bank(name):
            return ctx.enter_context(nc.psum_tensor(name, [P, 512], F32))

        cursor = [(nc.sbuf_base + 31) // 32 * 32]

        def here(name, shape, dt=F32):
            t = nc.alloc_sbuf_tensor_at(name, shape, dt, offset=cursor[0])
            size = int(np.prod(shape[1:])) * (2 if dt == BF16 else 4)
            cursor[0] += (size + 31) // 32 * 32
            return t

        xT = here("xT", [P, KD, SEQ])
        h_hi = here("h_hi", [P, KD, SEQ], F32R)
        h_lo = here("h_lo", [P, KD, SEQ], F32R)
        raw = [here(f"raw{s}", [P, KD * P]) for s in range(2)]
        w_hi = [here(f"w_hi{s}", [P, KD * P], F32R) for s in range(4)]
        w_lo = [here(f"w_lo{s}", [P, KD * P], F32R) for s in range(4)]
        tables_d = here("tables_d", [P, 2, SEQ])
        cos_d, sin_d = tables_d[:, 0, :], tables_d[:, 1, :]
        cos_m, sin_m = (here(n, [P, SEQ]) for n in ("cos_m", "sin_m"))
        ident = here("ident", [P, P])
        ident_b = here("ident_b", [P, P], BF16)
        mask_b = here("mask_b", [P, P], BF16)
        ones = here("ones", [P, P])
        gains = here("gains", [P, P])
        gl = here("gl", [P, G_N])
        stat = {k: [here(f"{n}_{k}", [P, NT]) for n in ("top", "bias", "total", "inv")]
                for k in ("m", "d1", "d2")}
        lam_scale = here("lam_scale", [P, NT])
        warm = here("warm", [P, 1])
        eps = here("eps", [P, 1])
        pool_mark = here("pool_mark", [P, 4])
        x_sum_at = cursor[0]
        x_sum = here("x_sum", [P, SEQ])
        rstd_x = nc.alloc_sbuf_tensor_at("rstd_x", [P, SEQ], F32, offset=x_sum_at)
        square = here("square", [P, SEQ])
        rstd_at = cursor[0]
        rstd = here("rstd", [P, SEQ])

        base = cursor[0]

        def at(name, offset, shape, dt=F32):
            return nc.alloc_sbuf_tensor_at(name, shape, dt, offset=base + offset)

        KB = 1024
        outs = at("outs", 0, [P, 16, SEQ])
        outs_lo = at("outs_lo", 0, [P, 16, SEQ], F32R)
        mem_hi = at("mem_hi", 0, [P, KD, MEM], F32R)
        mem_lo = at("mem_lo", 8 * KB, [P, KD, MEM], F32R)
        ckv_raw = at("ckv_raw", 0, [P, KVT, SEQ])
        ckv_sq = at("ckv_sq", 4 * KB, [P, KVT, SEQ])
        cq_raw = at("cq_raw", 16 * KB, [P, QT, SEQ])
        q_sum = nc.alloc_sbuf_tensor_at("q_sum", [P, SEQ], F32, offset=rstd_at)
        mem_n = at("mem_n", 88 * KB, [P, KD, MEM])
        cq_hi = at("cq_hi", 32 * KB, [P, QT, SEQ], F32R)
        cq_lo = at("cq_lo", 40 * KB, [P, QT, SEQ], F32R)
        ckv_hi = at("ckv_hi", 48 * KB, [P, KVT, SEQ], F32R)
        ckv_lo = at("ckv_lo", 52 * KB, [P, KVT, SEQ], F32R)
        T = 56 * KB
        p_a = at("p_a", T, [P, CAUSAL])
        p_b = at("p_b", T + 5 * KB, [P, CAUSAL])
        pt_hi = at("pt_hi", T + 10 * KB, [P, CAUSAL], F32R)
        pt_lo = at("pt_lo", T + 15 * KB, [P, CAUSAL], F32R)
        v_hi = at("v_hi", T + 20 * KB, [P, NT, P], F32R)
        v_lo = at("v_lo", T + 22 * KB, [P, NT, P], F32R)
        mv_hi = at("mv_hi", T + 24 * KB, [P, NT, P], F32R)
        mv_lo = at("mv_lo", T + 26 * KB, [P, NT, P], F32R)
        qT = at("qT", T + 28 * KB, [P, SEQ])
        kT = at("kT", T + 30 * KB, [P, SEQ])
        mqT = at("mqT", T + 32 * KB, [P, SEQ])
        mkT = at("mkT", T + 34 * KB, [P, SEQ])
        vT = at("vT", T + 36 * KB, [P, SEQ])
        kvT = at("kvT", T + 38 * KB, [P, SEQ])
        a_sq = at("a_sq", T + 40 * KB, [P, SEQ])
        rot = at("rot", T + 42 * KB, [P, SEQ])
        mid = at("mid", T + 44 * KB, [P, SEQ])
        pair = at("pair", T + 42 * KB, [P, 2, SEQ])
        outs_hi = at("outs_hi", 32 * KB, [P, 16, SEQ], F32R)
        mix_hi = at("mix_hi", 64 * KB, [P, KD, SEQ], F32R)
        mix_lo = at("mix_lo", 80 * KB, [P, KD, SEQ], F32R)
        sig = at("sig", 96 * KB, [P, 3, SEQ])
        mix = nc.alloc_sbuf_tensor_at("mix", [P, SEQ], F32, offset=rstd_at)
        hid_hi = at("hid_hi", 0, [P, FT, SEQ], F32R)
        hid_lo = at("hid_lo", 44 * KB, [P, FT, SEQ], F32R)
        sig_f = at("sig_f", 88 * KB, [P, 2, SEQ])
        gated = at("gated", 92 * KB, [P, SEQ])
        hid = at("hid", 94 * KB, [P, 2, SEQ])
        gate_n = at("gate_n", 98 * KB, [P, SEQ])
        x_in = at("x_in", 0, [P, NT, D])
        mem_in = at("mem_in", 16 * KB, [P, NM, D])
        gain_rows = at("gain_rows", 32 * KB, [P, P])
        lam_in = at("lam_in", 33 * KB, [P, DEPTH, 4, 64])
        lam_prod = at("lam_prod", 35 * KB, [P, DEPTH * 2, 64])
        lam_sum = at("lam_sum", 36 * KB, [P, DEPTH * 2])
        lam_exp = at("lam_exp", 36 * KB + 64, [P, DEPTH * 2])
        mem_ss = at("mem_ss", 36 * KB + 128, [P, NM])
        mem_rstd = at("mem_rstd", 36 * KB + 192, [P, NM])
        pos_i = at("pos_i", 36 * KB + 256, [P, NT], I32)
        pos_f = at("pos_f", 36 * KB + 320, [P, NT])
        freq = at("freq", 36 * KB + 384, [P, 24])
        ang = at("ang", 37 * KB, [P, NT, 24])
        turns = at("turns", 38 * KB, [P, NT, 24])
        sin_t = at("sin_t", 39 * KB, [P, NT, 24])
        cos_t = at("cos_t", 40 * KB, [P, NT, 24])
        half_t = at("half_t", 41 * KB, [P, NT, 24])
        neg_t = at("neg_t", 42 * KB, [P, NT, 24])
        rope_t = at("rope_t", 44 * KB, [P, 4, NT, P])
        mem_sq = at("mem_sq", 52 * KB, [P, D])
        x_sq = at("x_sq", 56 * KB, [P, 2, SEQ])
        y_T = at("y_T", 16 * KB, [P, KD, SEQ])
        y_out = at("y_out", 0, [P, NT, D])
        assert base + 102 * KB <= nc.sbuf_usable_end, (base, nc.sbuf_usable_end)

        proj = [bank("proj0"), bank("proj1")]
        score = [bank("score0"), bank("score1"), bank("score2")]
        flip = [bank("flip0"), bank("flip1")]
        att = bank("att")
        ssq = score[2]

        raw_full = [sem("raw_full0"), sem("raw_full1")]
        SLOTS = dict(C=(4, CROSS), A=(4, 1), B=(4, HEADS), E=(20, 2), F=(4, 2), G=(4, FT // 2), H=(8, 4))
        slot_hi = Tally(sem("slot_hi"), "act", **SLOTS)
        slot_lo = Tally(sem("slot_lo"), "pool", 2, **SLOTS)
        slot_done = Tally(sem("slot_done"), "pe", **SLOTS)
        mq_done = Tally(sem("mq_done"), "pe", B=(1, HEADS))
        om_done = Tally(sem("om_done"), "pe", E=(4, 2))
        SETS = dict(C=(1, CROSS), B=(3, HEADS))
        score_full = Tally(sem("score_full"), "pe", C=(2, CROSS), B=(9, HEADS))
        bias_ready = Tally(sem("bias_ready"), "ve", **SETS)
        exp_done = Tally(sem("exp_done"), "act", C=(4, CROSS), B=(12, HEADS))
        prob_ready = Tally(sem("prob_ready"), "ve", C=(1, CROSS), B=(2, HEADS))
        FLIPS = dict(C=(4, CROSS), B=(8, HEADS))
        flip_full = Tally(sem("flip_full"), "pe", **FLIPS)
        flip_hi = Tally(sem("flip_hi"), "act", **FLIPS)
        flip_read = Tally(sem("flip_read"), "ve", **FLIPS)
        ATT = dict(C=(1, CROSS), B=(2, HEADS))
        att_full = Tally(sem("att_full"), "pe", **ATT)
        att_read = Tally(sem("att_read"), "ve", **ATT)
        kv_copied = Tally(sem("kv_copied"), "act", C=(2, CROSS), B=(1, HEADS))
        xq_copied = Tally(sem("xq_copied"), "ve", C=(1, CROSS))
        v_copied = Tally(sem("v_copied"), "ve", B=(1, HEADS))
        gate_out = Tally(sem("gate_out"), "ve", E=(12, 2))
        mla_ready = Tally(sem("mla_ready"), "ve", A=(1, 1), B=(2, HEADS))
        diff_ready = Tally(sem("diff_ready"), "ve", B=(2, HEADS))
        SSQ = dict(N1=(1, 1), A=(2, 1), B=(1, HEADS), N2=(1, 1))
        ssq_full = Tally(sem("ssq_full"), "pe", **SSQ)
        ssq_read = Tally(sem("ssq_read"), "act", **SSQ)
        rms_ready = Tally(sem("rms_ready"), "act", **SSQ)
        SQ = dict(C=(1, CROSS), F=(4, 2), H=(2, 4))
        tile_ready = Tally(sem("tile_ready"), "ve", **SQ)
        sq_done = Tally(sem("sq_done"), "act", KD + 1, **SQ)
        sq_added = Tally(sem("sq_added"), "ve", KD + 1, **SQ)
        ckv_copied = Tally(sem("ckv_copied"), "ve", A=(2, 1))
        ckv_squared = Tally(sem("ckv_squared"), "act", A=(2, 1))
        a_squared = Tally(sem("a_squared"), "act", B=(1, HEADS))
        NORM = dict(A=(QT + KVT, 1), F=(4, 2), H=(2, 4))
        pair_ready = Tally(sem("pair_ready"), "ve", KD + 1, **NORM)
        pair_hi = Tally(sem("pair_hi"), "act", KD + 1, **NORM)
        pair_lo = Tally(sem("pair_lo"), "ve", KD + 1, **NORM)
        gl_ready = Tally(sem("gl_ready"), "ve", N1=(1, 1))
        mem_loaded = Tally(sem("mem_loaded"), "act", H=(32, 1))
        memh_hi = Tally(sem("memh_hi"), "act", N1=(KD, 1))
        memh_lo = Tally(sem("memh_lo"), "ve", N1=(KD, 1))
        outs_split_hi = Tally(sem("outs_split_hi"), "act", E=(16, 1))
        outs_split = Tally(sem("outs_split"), "ve", E=(16, 1))
        sig_ready = Tally(sem("sig_ready"), "act", E=(12, 2))
        od_used = Tally(sem("od_used"), "ve", E=(4, 2))
        om_used = Tally(sem("om_used"), "ve", E=(4, 2))
        oc_used = Tally(sem("oc_used"), "ve", E=(4, 2))
        mix_ready = Tally(sem("mix_ready"), "ve", E=(4, 2))
        mix_split_hi = Tally(sem("mix_split_hi"), "act", E=(4, 2))
        mix_split = Tally(sem("mix_split"), "ve", E=(4, 2))
        HID = dict(G=(2, FT // 2))
        gate_read = Tally(sem("gate_read"), "ve", **HID)
        silu_sig = Tally(sem("silu_sig"), "act", **HID)
        gate_used = Tally(sem("gate_used"), "ve", **HID)
        hid_ready = Tally(sem("hid_ready"), "ve", **HID)
        hid_split_hi = Tally(sem("hid_split_hi"), "act", **HID)
        hid_split = Tally(sem("hid_split"), "ve", **HID)
        const_step, const_ready = sem("const_step"), sem("const_ready")
        in_gain, in_mem, in_pos, in_lam = (sem(n) for n in ("in_gain", "in_mem", "in_pos", "in_lam"))
        in_x = [sem("in_x0"), sem("in_x1")]
        pre_full, pre_read, pre_act = sem("pre_full"), sem("pre_read"), sem("pre_act")
        pre_chain = sem("pre_chain")
        pre_vec, mem_stored, mem_scaled, rope_ready, x_copied = (sem(n) for n in ("pre_vec", "mem_stored", "mem_scaled", "rope_ready", "x_copied"))
        y_ready, y_flipped, y_copied, stored = sem("y_ready"), sem("y_flipped"), sem("y_copied"), sem("stored")
        vec_step = Tally(sem("vec_step"), "ve", N1=(5, 1), C=(2, CROSS), A=(3, 1), P=(7, 1), B=(14, HEADS - 1), L=(7, 1),
                         E=(4, 2), N2=(4, 1), G=(2, FT // 2))

        tallies = [
            sq_done, sq_added, slot_hi, slot_done, mq_done, om_done, score_full, bias_ready,
            exp_done, prob_ready, flip_full, flip_hi, flip_read, att_full, att_read, kv_copied,
            mla_ready, diff_ready, mem_loaded, xq_copied, v_copied, gate_out, ssq_full, ssq_read, rms_ready, tile_ready, ckv_copied,
            ckv_squared, a_squared, pair_ready, pair_hi, pair_lo, gl_ready, memh_hi, memh_lo,
            outs_split_hi, outs_split, sig_ready, od_used, om_used, oc_used, mix_ready,
            mix_split_hi, mix_split, gate_read, silu_sig, gate_used, hid_ready, hid_split_hi, hid_split,
            vec_step,
        ]

        def start_counts(engine, by):
            for t in tallies:
                if t.by == by:
                    engine.sem_inc(t.sem, 1)

        def load_gains(engine, l):
            for row, w, n in ((G_ATTN, attn_norm_w, KD), (G_FFN, ffn_norm_w, KD), (G_MEM, mem_norm_w, KD),
                              (G_Q, mla_q_norm_w, QT), (G_KV, mla_kv_norm_w, KVT), (G_SUB, diff_subln_w, 1)):
                engine.dma_start(gain_rows[l * G_N + row:l * G_N + row + n, :],
                                 w[l, :].rearrange("(k p) -> k p", p=P)).then_inc(in_gain, 16)

        block = ctx.enter_context(nc.Block())

        @block.sync
        def _(sp):
            sp.wait_ge(const_ready, 1)
            load_gains(sp, 0)
            sp.dma_start(gain_rows[DEPTH * G_N:DEPTH * G_N + KD, :],
                         final_norm_w.rearrange("(k p) -> k p", p=P)).then_inc(in_gain, 16)
            xv = x[0, :, :].rearrange("(t p) d -> p t d", p=P)
            for half in range(2):
                c = slice(half * (D // 2), (half + 1) * (D // 2))
                sp.dma_start(x_in[:, :, c], xv[:, :, c]).then_inc(in_x[half], 16)
            sp.dma_start(mem_in[:, :, :], mem[0, :, :].rearrange("(t p) d -> p t d", p=P)).then_inc(in_mem, 16)

            def slot(l, stage, step, s, *parts):
                sp.wait_ge(slot_lo.sem, slot_lo.at(l, stage, step, s - 1))
                assert len(parts) == 2
                for col, src in parts:
                    n, width = src.shape[1], src.shape[2]
                    sp.dma_start(raw[s % 2][:, col:col + n * width].rearrange("p (k n) -> p k n", k=n),
                                 src).then_inc(raw_full[s % 2], 16)

            def tiles(w, l, k0, k1, col, width=P):
                v = w.rearrange("l (k p) n -> l p k n", p=P)
                v = v[l:l + 1] if isinstance(l, int) else v[bass.ds(l, 1)]
                v = v[:, :, k0:k1, bass.ds(col, width)]
                return v.rearrange("a p k n -> (a p) k n")

            def whole(w, l, col):
                return (0, tiles(w, l, 0, 4, col)), (4 * P, tiles(w, l, 4, 8, col))

            def cross_slots(l, i):
                slot(l, "C", i, 0, *whole(w_in, l, C_XQ + i * P))
                slot(l, "C", i, 1, *whole(w_mem_kv, l, i * P))
                slot(l, "C", i, 2, *whole(w_mem_kv, l, 512 + i * P))
                slot(l, "C", i, 3, *whole(w_in, l, C_CQ + i * P))

            def head_slots(l, h):
                slot(l, "B", h, 0, *whole(w_in, l, C_DV + h * P))
                slot(l, "B", h, 1, (0, tiles(mla_w_uq, l, 0, QT, h * 96, 96)),
                     (QT * 96, tiles(mla_w_ukv, l, 0, KVT, h * P)))
                slot(l, "B", h, 2, *whole(w_in, l, C_DQ + h * P))
                slot(l, "B", h, 3, *whole(w_in, l, C_DK + h * P))

            with sp.Fori(0, DEPTH) as l:
                with sp.Fori(0, CROSS) as i:
                    cross_slots(l, i)
                slot(l, "A", 0, 0, *whole(w_in, l, C_CKV))
                slot(l, "A", 0, 1, *whole(w_in, l, C_CKV + P))
                slot(l, "A", 0, 2, (0, tiles(w_in, l, 0, 2, C_KR - 64, 96)), (2 * 96, tiles(w_in, l, 2, 4, C_KR - 64, 96)))
                slot(l, "A", 0, 3, (0, tiles(w_in, l, 4, 6, C_KR - 64, 96)), (2 * 96, tiles(w_in, l, 6, 8, C_KR - 64, 96)))
                with sp.Fori(0, HEADS) as h:
                    head_slots(l, h)
                with sp.Fori(0, 2) as jj:
                    for e in range(4):
                        j = jj * (4 * P) + e * P
                        for g in range(3):
                            slot(l, "E", jj, 5 * e + g, *whole(w_in, l, j + (C_GATE + g * D)))
                        slot(l, "E", jj, 5 * e + 3, *whole(w_o_diff, l, j))
                        slot(l, "E", jj, 5 * e + 4, (0, tiles(w_o_mla, l, 0, 4, j)), (4 * P, tiles(w_o_cross, l, 0, 4, j)))
                with sp.Fori(0, 2) as jj:
                    for e in range(4):
                        slot(l, "F", jj, e, *whole(w_out, l, jj * (4 * P) + e * P))
                with sp.Fori(0, FT // 2) as t:
                    for e in range(2):
                        slot(l, "G", t, 2 * e, *whole(w_gate_up, l, t * (2 * P) + e * P))
                        slot(l, "G", t, 2 * e + 1, *whole(w_gate_up, l, t * (2 * P) + (e * P + FFN)))
                with sp.Fori(0, 4) as jj:
                    for e in range(2):
                        k = 0
                        for c, n in enumerate(DOWN):
                            slot(l, "H", jj, 4 * e + c, (0, tiles(w_down, l, k, k + 3, jj * (2 * P) + e * P)),
                                 (3 * P, tiles(w_down, l, k + 3, k + n, jj * (2 * P) + e * P)))
                            k += n
            for s in range(AHEAD + 1):
                sp.wait_ge(slot_lo.sem, slot_lo.end(DEPTH) + s - 1)
                for half in range(2):
                    sp.dma_start(raw[s % 2][:, half * 512:(half + 1) * 512], w_out[0, 0:P, 0:512]).then_inc(raw_full[s % 2], 16)
            for t in range(NT):
                sp.wait_ge(y_copied, 2 * (t + 1))
                sp.dma_start(out[0, t * P:(t + 1) * P, :], y_out[:, t, :]).then_inc(stored, 16)
            sp.wait_ge(stored, 16 * NT)
            sp.wait_ge(mem_stored, 32)

        @block.gpsimd
        def _(pool):
            g = nc.gpsimd
            n = [0]

            def step(ins):
                n[0] += 1
                ins.then_inc(const_step, 1)
                pool.wait_ge(const_step, n[0])

            step(g.memset(gain_rows[:, :], 0.0))
            g.memset(warm[:, :], 0.0).then_inc(const_ready, 1)
            g.memset(ones[:, :], 1.0)
            g.memset(eps[:, :], EPS)
            step(g.memset(ident[:, :], 0.0))
            step(g.affine_select(out=ident[:, :], in_=ident[:, :], compare_op=ALU.not_equal, fill=1.0,
                                 base=0, pattern=[[-1, P]], channel_multiplier=1))
            step(g.memset(ident_b[:, :], 0.0))
            step(g.affine_select(out=ident_b[:, :], in_=ident_b[:, :], compare_op=ALU.not_equal, fill=1.0,
                                 base=0, pattern=[[-1, P]], channel_multiplier=1))
            step(g.memset(mask_b[:, :], 0.0))
            step(g.affine_select(out=mask_b[:, :], in_=mask_b[:, :], compare_op=ALU.is_ge, fill=MASKED,
                                 base=0, pattern=[[-1, P]], channel_multiplier=1))
            g.memset(x_sum[:, :], 0.0)
            for r, rot_dim in ((0, ROT_D), (ROT_D // 2, ROT_M)):
                for i in range(rot_dim // 2):
                    f = np.float32(THETA) ** (-np.float32(i) * np.float32(2.0) / np.float32(rot_dim))
                    g.memset(freq[:, r + i:r + i + 1], float(f))
            for kind in range(4):
                step(g.memset(rope_t[:, kind, :, :], 1.0 - kind % 2))
            g.memset(pool_mark[:, 2:3], 0.0).then_inc(const_ready, 1)
            for b in range(2):
                g.memset(pool_mark[:, b:b + 1], 0.0).then_inc(slot_lo.sem, 1)
            total = slot_lo.total * DEPTH
            with pool.Fori(0, total // 4) as r:
                for s in range(4):
                    pool.wait_ge(slot_hi.sem, r * 4 + (slot_hi.before + s + 1))
                    g.tensor_tensor(w_lo[s][:, :], raw[s % 2][:, :], w_hi[s][:, :].bitcast(F32),
                                    ALU.subtract).then_inc(slot_lo.sem, 1)
            for s in range(AHEAD + 1):
                pool.wait_ge(slot_hi.sem, slot_hi.before + total + s + 1)
                g.tensor_tensor(w_lo[s][:, :], raw[s % 2][:, :], w_hi[s][:, :].bitcast(F32),
                                ALU.subtract).then_inc(slot_lo.sem, 1)

        @block.tensor
        def _(pe):
            mm = nc.tensor.matmul
            start_counts(pe, "pe")

            def product(pieces):
                last = len(pieces) - 1
                for n, (o, sh, sl, mh, ml) in enumerate(pieces):
                    mm(o, sh, mh, start=n == 0, stop=False)
                    mm(o, sh, ml, start=False, stop=False)
                    ins = mm(o, sl, mh, start=False, stop=n == last)
                return ins

            def unit(l, stage, step, s, b, free, n, rhs, width=P, cols=SEQ, first=0, before=None, start=True, stop=True):
                pe.wait_ge(slot_lo.sem, slot_lo.at(l, stage, step, s + 1))
                if free:
                    pe.wait_ge(free[0].sem, free[1])
                hi, lo = w_hi[s % 4], w_lo[s % 4]
                for k in range(n):
                    if before:
                        before(k)
                    c = first + k * width
                    rh, rl = rhs(k)
                    o = proj[b][0:width, 0:cols]
                    mm(o, hi[:, c:c + width], rh, start=start and k == 0, stop=False)
                    mm(o, hi[:, c:c + width], rl, start=False, stop=False)
                    ins = mm(o, lo[:, c:c + width], rh, start=False, stop=stop and k == n - 1)
                return ins

            def h_rhs(k):
                return h_hi[:, k, :], h_lo[:, k, :]

            def sum_squares(l, stage, k, *tiles):
                pe.wait_ge(ssq_read.sem, ssq_read.at(l, stage, 0, k))
                for n, t in enumerate(tiles):
                    ins = mm(ssq[:, :], ones[:, :], t, start=n == 0, stop=n == len(tiles) - 1)
                ins.then_inc(ssq_full.sem, 1)

            def flip_bank(l, stage, step, k):
                pe.wait_ge(flip_read.sem, flip_read.at(l, stage, step, k - 1) if stage == "B" or k else flip_read.at(l, stage, step, 0))
                return flip[k % 2]

            def causal_scores(l, h, n, q, k, rows):
                pe.wait_ge(exp_done.sem, exp_done.at(l, "B", h, 4 * n))
                for b, group in enumerate(((3,), (2, 0), (1,))):
                    for t in group:
                        o = score[b][:, 384 * (t == 0):384 * (t == 0) + (t + 1) * P]
                        mm(o, q[rows, t * P:(t + 1) * P], k[rows, 0:(t + 1) * P], start=True, stop=False)
                        ins = mm(o[:, t * P:(t + 1) * P], ident_b[:, :], mask_b[:, :], start=False, stop=True)
                    ins.then_inc(score_full.sem, 1)

            def causal_flip(l, h, n, part):
                p, k0 = (p_a, 2) if n == 0 else (p_b, 5)
                if part == 0:
                    pe.wait_ge(prob_ready.sem, prob_ready.at(l, "B", h, n + 1))
                fills = ((0,), (1,)) if part == 0 else ((2, 3),)
                for f, js in enumerate(fills):
                    k = k0 + 2 * part + f
                    b, col = flip_bank(l, "B", h, k), 0
                    for j in js:
                        for t in range(j, NT):
                            ins = nc.tensor.transpose(b[:, col:col + P], p[:, q_off(t) + j * P:q_off(t) + (j + 1) * P], ident[:, :])
                            col += P
                    ins.then_inc(flip_full.sem, 1)

            def causal_attend(l, h, n, vh, vl):
                pe.wait_ge(flip_read.sem, flip_read.at(l, "B", h, 5 + 3 * n))
                pe.wait_ge(att_read.sem, att_read.at(l, "B", h, n))
                product([(att[:, j * P:SEQ], vh[:, j, :], vl[:, j, :], pt_hi[:, k_off(j):k_off(j) + SEQ - j * P],
                          pt_lo[:, k_off(j):k_off(j) + SEQ - j * P]) for j in range(NT)]).then_inc(att_full.sem, 1)

            def flip_values(l, h):
                for k, (src, copied) in enumerate(((vT, v_copied), (kvT, kv_copied))):
                    pe.wait_ge(copied.sem, copied.at(l, "B", h, 1))
                    b = flip_bank(l, "B", h, k)
                    for j in range(NT):
                        ins = nc.tensor.transpose(b[:, j * P:(j + 1) * P], src[:, j * P:(j + 1) * P], ident[:, :])
                    ins.then_inc(flip_full.sem, 1)

            def project_v(l, h):
                unit(l, "B", h, 0, 0, (diff_ready, diff_ready.at(l, "B", h)), KD, h_rhs).then_inc(slot_done.sem, 1)

            def project_latent(l, h, wait_norm=False):
                if wait_norm:
                    pe.wait_ge(pair_lo.sem, pair_lo.at(l, "A", 0, QT + KVT))
                unit(l, "B", h, 1, 1, (diff_ready, diff_ready.at(l, "B", h)), QT, lambda k: (cq_hi[:, k, :], cq_lo[:, k, :]), width=96).then_inc(mq_done.sem, 1)
                unit(l, "B", h, 1, 0, (v_copied, v_copied.at(l, "B", h, 1)), KVT, lambda k: (ckv_hi[:, k, :], ckv_lo[:, k, :]), first=QT * 96).then_inc(slot_done.sem, 1)

            def project_q(l, h):
                unit(l, "B", h, 2, 1, (mla_ready, mla_ready.at(l, "B", h, 1)), KD, h_rhs).then_inc(slot_done.sem, 1)

            def project_k(l, h):
                unit(l, "B", h, 3, 0, (kv_copied, kv_copied.at(l, "B", h, 1)), KD, h_rhs).then_inc(slot_done.sem, 1)

            def latent_scores(l, h):
                pe.wait_ge(mla_ready.sem, mla_ready.at(l, "B", h, 2))
                causal_scores(l, h, 0, mqT, mkT, slice(0, 96))

            def head(l, h, n):
                if n is not None:
                    project_v(l, n)
                pe.wait_ge(diff_ready.sem, diff_ready.at(l, "B", h, 2))
                causal_scores(l, h, 1, qT, kT, slice(0, 64))
                causal_flip(l, h, 0, 0)
                if n is not None:
                    pe.wait_ge(ssq_read.sem, ssq_read.at(l, "B", h))
                    project_latent(l, n)
                causal_flip(l, h, 0, 1)
                causal_scores(l, h, 2, qT, kT, slice(64, 128))
                if n is not None:
                    project_q(l, n)
                causal_attend(l, h, 0, mv_hi, mv_lo)
                if n is not None:
                    project_k(l, n)
                causal_flip(l, h, 1, 0)
                causal_flip(l, h, 1, 1)
                if n is not None:
                    latent_scores(l, n)
                causal_attend(l, h, 1, v_hi, v_lo)
                if n is not None:
                    flip_values(l, n)
                pe.wait_ge(a_squared.sem, a_squared.at(l, "B", h, 1))
                pe.wait_ge(diff_ready.sem, diff_ready.at(l, "B", h + 1 if n is None else n, 0 if n is None else 1))
                mm(proj[1][:, :], ones[:, :], a_sq[:, :], start=True, stop=True).then_inc(ssq_full.sem, 1)

            def cross_scores(l, i):
                pe.wait_ge(kv_copied.sem, kv_copied.at(l, "C", i, 2))
                pe.wait_ge(xq_copied.sem, xq_copied.at(l, "C", i, 1))
                pe.wait_ge(exp_done.sem, exp_done.at(l, "C", i))
                for b in range(2):
                    for t in (2 * b, 2 * b + 1):
                        ins = mm(score[b][:, (t % 2) * MEM:(t % 2 + 1) * MEM], qT[:, t * P:(t + 1) * P], kT[:, 0:MEM], start=True, stop=True)
                    ins.then_inc(score_full.sem, 1)

            def cross_flip(l, i):
                pe.wait_ge(prob_ready.sem, prob_ready.at(l, "C", i, 1))
                for j in range(NM):
                    b = flip_bank(l, "C", i, 2 + j)
                    for t in range(NT):
                        ins = nc.tensor.transpose(b[:, t * P:(t + 1) * P], p_a[:, t * MEM + j * P:t * MEM + (j + 1) * P], ident[:, :])
                    ins.then_inc(flip_full.sem, 1)

            def cross_attend(l, i):
                pe.wait_ge(flip_read.sem, flip_read.at(l, "C", i, 4))
                pe.wait_ge(att_read.sem, att_read.at(l, "C", i))
                product([(att[:, :], v_hi[:, j, :], v_lo[:, j, :], pt_hi[:, j * SEQ:(j + 1) * SEQ], pt_lo[:, j * SEQ:(j + 1) * SEQ])
                         for j in range(NM)]).then_inc(att_full.sem, 1)

            def flip_memory(l, i):
                pe.wait_ge(kv_copied.sem, kv_copied.at(l, "C", i, 2))
                for j in range(NM):
                    b = flip_bank(l, "C", i, j)
                    nc.tensor.transpose(b[:, 0:P], vT[:, j * P:(j + 1) * P], ident[:, :]).then_inc(flip_full.sem, 1)

            def project_xq(l, i, before=None):
                unit(l, "C", i, 0, 0, (kv_copied, kv_copied.at(l, "C", i)), KD, h_rhs, before=before).then_inc(slot_done.sem, 1)

            def project_mem(l, i, s, b, free):
                unit(l, "C", i, s, b, free, KD, lambda k: (mem_hi[:, k, :], mem_lo[:, k, :]), cols=MEM).then_inc(slot_done.sem, 1)

            def project_cq(l, i):
                unit(l, "C", i, 3, 1, (kv_copied, kv_copied.at(l, "C", i, 1)), KD, h_rhs).then_inc(slot_done.sem, 1)

            fills = []
            fills.append(((in_gain, 16 * (6 * DEPTH + 1)), [(0, gain_rows[:, :])], [(pre_read, 1)]))
            for k in range(KD):
                fills.append(((in_x[k // (KD // 2)], 16), [(t, x_in[:, t, k * P:(k + 1) * P]) for t in range(NT)],
                              [(x_copied, k + 1)]))
            for kind in range(4):
                fills.append(((rope_ready, 1), [(t, rope_t[:, kind, t, :]) for t in range(NT)], [(pre_read, 2 + kind)]))
            for f in range(KD // 2):
                fills.append(((mem_scaled, NM),
                              [(2 * e + t, mem_in[:, t, (2 * f + e) * P:(2 * f + e + 1) * P]) for e in range(2) for t in range(NM)],
                              [(pre_read, 6 + f)]))
            pe.wait_ge(const_ready, 2)
            for n, ((loaded, count), blocks, _) in enumerate(fills):
                pe.wait_ge(loaded, count)
                if n >= 2:
                    for reader, reads in fills[n - 2][2]:
                        pe.wait_ge(reader, reads)
                for c, src in blocks:
                    ins = nc.tensor.transpose(flip[n % 2][:, c * P:(c + 1) * P], src, ident[:, :])
                ins.then_inc(pre_full, 1)
            pe.wait_ge(pre_read, 5 + KD // 2)

            with pe.Fori(0, DEPTH) as l:
                project_xq(l, 0, before=lambda k: pe.wait_ge(pair_lo.sem, pair_lo.at(l, "A", 0, k + 1 - KD)))
                pe.wait_ge(sq_added.sem, sq_added.at(l, "C"))
                sum_squares(l, "N1", 0, x_sum[:, :])
                pe.wait_ge(memh_lo.sem, memh_lo.at(l, "N1", 0, KD))
                project_mem(l, 0, 1, 1, (tile_ready, tile_ready.at(l, "C")))
                project_mem(l, 0, 2, 0, (xq_copied, xq_copied.at(l, "C", 0, 1)))
                project_cq(l, 0)
                flip_memory(l, 0)
                with pe.Fori(0, CROSS - 1) as i:
                    cross_scores(l, i)
                    project_xq(l, i + 1)
                    cross_flip(l, i)
                    project_mem(l, i + 1, 1, 1, (tile_ready, tile_ready.at(l, "C", i + 1)))
                    cross_attend(l, i)
                    project_mem(l, i + 1, 2, 0, (xq_copied, xq_copied.at(l, "C", i + 1, 1)))
                    project_cq(l, i + 1)
                    flip_memory(l, i + 1)
                i = CROSS - 1
                cross_scores(l, i)
                unit(l, "A", 0, 0, 0, (kv_copied, kv_copied.at(l, "C", CROSS)), KD, h_rhs).then_inc(slot_done.sem, 1)
                pe.wait_ge(sq_added.sem, sq_added.at(l, "F"))
                sum_squares(l, "A", 0, q_sum[:, :])
                cross_flip(l, i)
                unit(l, "A", 0, 1, 1, (tile_ready, tile_ready.at(l, "C", CROSS)), KD, h_rhs).then_inc(slot_done.sem, 1)
                cross_attend(l, i)
                unit(l, "A", 0, 2, 0, (ckv_copied, ckv_copied.at(l, "A", 0, 1)), 4, h_rhs, width=96, stop=False).then_inc(slot_done.sem, 1)
                unit(l, "A", 0, 3, 0, None, 4, lambda k: h_rhs(k + 4), width=96, start=False).then_inc(slot_done.sem, 1)
                pe.wait_ge(ckv_squared.sem, ckv_squared.at(l, "A", 0, 2))
                sum_squares(l, "A", 1, ckv_sq[:, 0, :], ckv_sq[:, 1, :])
                pe.wait_ge(mla_ready.sem, mla_ready.at(l, "B", 0))
                project_v(l, 0)
                project_latent(l, 0, wait_norm=True)
                project_q(l, 0)
                project_k(l, 0)
                pe.wait_ge(ssq_read.sem, ssq_read.at(l, "B", 0))
                latent_scores(l, 0)
                flip_values(l, 0)
                with pe.Fori(0, HEADS // 2 - 1) as hp:
                    for e in range(2):
                        head(l, hp * 2 + e, hp * 2 + (e + 1))
                head(l, HEADS - 2, HEADS - 1)
                head(l, HEADS - 1, None)
                with pe.Fori(0, 2) as jj:
                    for e in range(4):
                        s = 5 * e
                        unit(l, "E", jj, s, 0, (om_used, om_used.at(l, "E", jj, e)), KD, h_rhs).then_inc(slot_done.sem, 1)
                        if e == 0:
                            pe.wait_ge(ssq_read.sem, ssq_read.at(l, "B", HEADS))
                        unit(l, "E", jj, s + 1, 1, (oc_used, oc_used.at(l, "E", jj, e)), KD, h_rhs).then_inc(slot_done.sem, 1)
                        unit(l, "E", jj, s + 2, 0, (gate_out, gate_out.at(l, "E", jj, 3 * e + 1)), KD, h_rhs).then_inc(slot_done.sem, 1)

                        def split(k):
                            if e == 0:
                                pe.wait_ge(outs_split.sem, outs_split.at(l, "E", 0, k + 1))
                        unit(l, "E", jj, s + 3, 1, (gate_out, gate_out.at(l, "E", jj, 3 * e + 2)), KD,
                             lambda k: (outs_hi[:, k, :], outs_lo[:, k, :]), before=split).then_inc(slot_done.sem, 1)
                        unit(l, "E", jj, s + 4, 0, (gate_out, gate_out.at(l, "E", jj, 3 * e + 3)), 4,
                             lambda k: (outs_hi[:, 8 + k, :], outs_lo[:, 8 + k, :]), before=lambda k: split(8 + k)).then_inc(om_done.sem, 1)
                        unit(l, "E", jj, s + 4, 1, (od_used, od_used.at(l, "E", jj, e + 1)), 4,
                             lambda k: (outs_hi[:, 12 + k, :], outs_lo[:, 12 + k, :]), first=4 * P,
                             before=lambda k: split(12 + k)).then_inc(slot_done.sem, 1)
                with pe.Fori(0, 2) as jj:
                    for e in range(4):
                        def mixed(k):
                            if e == 0 and k == 0:
                                pe.wait_ge(om_used.sem, om_used.at(l, "E", 2))
                            if e == 0:
                                pe.wait_ge(mix_split.sem, mix_split.at(l, "E", 0, k + 1))
                        unit(l, "F", jj, e, e % 2, (tile_ready, tile_ready.at(l, "F", jj, e - 1)), KD,
                             lambda k: (mix_hi[:, k, :], mix_lo[:, k, :]), before=mixed).then_inc(slot_done.sem, 1)
                unit(l, "G", 0, 0, 0, (tile_ready, tile_ready.at(l, "F", 1, 3)), KD, h_rhs,
                     before=lambda k: pe.wait_ge(pair_lo.sem, pair_lo.at(l, "F", 0, k + 1))).then_inc(slot_done.sem, 1)
                pe.wait_ge(sq_added.sem, sq_added.at(l, "H"))
                sum_squares(l, "N2", 0, x_sum[:, :])
                unit(l, "G", 0, 1, 1, (tile_ready, tile_ready.at(l, "H")), KD, h_rhs).then_inc(slot_done.sem, 1)

                def gate_up(t, e):
                    unit(l, "G", t, 2 * e, 0, (gate_read, gate_read.at(l, "G", t, e)), KD, h_rhs).then_inc(slot_done.sem, 1)
                    unit(l, "G", t, 2 * e + 1, 1, (hid_ready, hid_ready.at(l, "G", t, e)), KD, h_rhs).then_inc(slot_done.sem, 1)
                gate_up(0, 1)
                with pe.Fori(0, FT // 2 - 1) as t:
                    gate_up(t + 1, 0)
                    gate_up(t + 1, 1)
                with pe.Fori(0, 4) as jj:
                    for e in range(2):
                        k = 0
                        for c, n in enumerate(DOWN):
                            if e == 0 and c == 0:
                                pe.wait_ge(gate_read.sem, gate_read.at(l, "G", FT // 2))
                            if e == 0:
                                pe.wait_ge(hid_split.sem, hid_split.at(l, "G", 0, k + n))
                            unit(l, "H", jj, 4 * e + c, e, (tile_ready, tile_ready.at(l, "H", jj, e - 1)) if c == 0 else None, n, lambda q, k=k: (hid_hi[:, k + q, :], hid_lo[:, k + q, :]),
                                 start=c == 0, stop=c == 3).then_inc(slot_done.sem, 1)
                            k += n
            pe.wait_ge(sq_added.sem, sq_added.end(DEPTH))
            pe.wait_ge(ssq_read.sem, ssq_read.end(DEPTH))
            mm(ssq[:, :], ones[:, :], x_sum[:, :], start=True, stop=True).then_inc(ssq_full.sem, 1)
            pe.wait_ge(y_ready, KD)
            for t in range(NT):
                for half in range(2):
                    n = 2 * t + half
                    if n >= 2:
                        pe.wait_ge(y_copied, n - 1)
                    for k in range(4):
                        ins = nc.tensor.transpose(flip[n % 2][:, k * P:(k + 1) * P], y_T[:, 4 * half + k, t * P:(t + 1) * P], ident[:, :])
                    ins.then_inc(y_flipped, 1)

        @block.scalar
        def _(act):
            sc = nc.scalar
            start_counts(act, "act")

            def copy(out, in_):
                return sc.activation(out, in_, ACT.Copy)

            def split_ahead(l, stage, step, s):
                n = slot_hi.index(l, stage, step, s)
                act.wait_ge(slot_done.sem, slot_done.at(l, stage, step, s))
                q = s + AHEAD
                act.wait_ge(raw_full[q % 2], n * 16 + (AHEAD * 16 + (16 if q % 2 else 32)))
                copy(w_hi[q % 4][:, :], raw[q % 2][:, :]).then_inc(slot_hi.sem, 1)

            def exps(l, stage, step, n, k, p, scale):
                _, bias, total, _ = stat[k]
                act.wait_ge(bias_ready.sem, bias_ready.at(l, stage, step, n + 1))
                for t in range(NT):
                    if stage == "C":
                        src, dst = score[t // 2][:, (t % 2) * MEM:(t % 2 + 1) * MEM], p[:, t * MEM:(t + 1) * MEM]
                    else:
                        b, c = {3: (0, 0), 2: (1, 0), 0: (1, 384), 1: (2, 0)}[t]
                        src, dst = score[b][:, c:c + (t + 1) * P], p[:, q_off(t):q_off(t) + (t + 1) * P]
                    sc.activation(dst, src, ACT.Exp, bias=bias[:, t:t + 1], scale=scale,
                                  accum_out=total[:, t:t + 1]).then_inc(exp_done.sem, 1)

            def flip_high(l, stage, step, k, dst, src):
                act.wait_ge(flip_full.sem, flip_full.at(l, stage, step, k + 1))
                copy(dst, src).then_inc(flip_hi.sem, 1)

            def causal_high(l, h, n, part):
                if part == 0:
                    act.wait_ge(att_full.sem, att_full.at(l, "B", h, n))
                    flip_high(l, "B", h, 2 + 3 * n, pt_hi[:, 0:512], flip[n][:, :])
                    flip_high(l, "B", h, 3 + 3 * n, pt_hi[:, 512:896], flip[1 - n][:, 0:384])
                else:
                    flip_high(l, "B", h, 4 + 3 * n, pt_hi[:, 896:1280], flip[n][:, 0:384])

            def values_high(l, h):
                act.wait_ge(att_full.sem, att_full.at(l, "B", h))
                flip_high(l, "B", h, 0, v_hi[:, :, :].rearrange("p j d -> p (j d)"), flip[0][:, :])
                flip_high(l, "B", h, 1, mv_hi[:, :, :].rearrange("p j d -> p (j d)"), flip[1][:, :])

            def out_kv(l, h):
                act.wait_ge(slot_done.sem, slot_done.at(l, "B", h, 2))
                copy(kvT[:, :], proj[0][:, :]).then_inc(kv_copied.sem, 1)

            def squares(l, stage, step, k, src):
                act.wait_ge(tile_ready.sem, tile_ready.at(l, stage, step, k + 1))
                act.wait_ge(sq_added.sem, sq_added.at(l, stage, step, k))
                scale = (Q_LORA if stage == "C" else D) ** -0.5
                sc.activation(square[:, :], src, ACT.Square, scale=scale).then_inc(sq_done.sem, 1)

            def rms(l, stage, step, k, sums=ssq, r=rstd):
                act.wait_ge(ssq_full.sem, ssq_full.at(l, stage, step, k + 1))
                sc.activation(r[:, :], sums[:, :], ACT.Ln, bias=eps[:, 0:1]).then_inc(ssq_read.sem, 1)
                act.wait_ge(ssq_read.sem, ssq_read.at(l, stage, step, k + 1))
                sc.activation(r[:, :], r[:, :], ACT.Exp, scale=-0.5).then_inc(rms_ready.sem, 1)

            def pair_high(l, stage, k, dst, step=0):
                act.wait_ge(pair_ready.sem, pair_ready.at(l, stage, step, k + 1))
                copy(dst, pair[:, k % 2, :]).then_inc(pair_hi.sem, 1)

            def head(l, h, n, e):
                exps(l, "B", h, 0, "m", p_a, MLA_SCALE)
                if n is not None:
                    split_ahead(l, "B", n, 0)
                act.wait_ge(flip_full.sem, flip_full.at(l, "B", h))
                exps(l, "B", h, 1, "d1", p_b, DIFF_SCALE)
                causal_high(l, h, 0, 0)
                if n is not None:
                    split_ahead(l, "B", n, 1)
                causal_high(l, h, 0, 1)
                if n is not None:
                    out_kv(l, n)
                act.wait_ge(flip_full.sem, flip_full.at(l, "B", h, 5))
                exps(l, "B", h, 2, "d2", p_a, DIFF_SCALE)
                if n is not None:
                    split_ahead(l, "B", n, 2)
                act.wait_ge(att_full.sem, att_full.at(l, "B", h, 1))
                o = outs[64 * e:64 * e + 64, 8 + h // 2, :] if isinstance(h, int) else \
                    outs[64 * e:64 * e + 64, bass.ds(n_pair(h) + 8, 1), :].rearrange("p a n -> p (a n)")
                copy(o, att[64:128, :]).then_inc(att_read.sem, 1)
                causal_high(l, h, 1, 0)
                if n is not None:
                    split_ahead(l, "B", n, 3)
                causal_high(l, h, 1, 1)
                act.wait_ge(att_full.sem, att_full.at(l, "B", h, 2))
                act.wait_ge(ssq_full.sem, ssq_full.at(l, "B", h))
                sc.activation(a_sq[:, :], att[:, :], ACT.Square, scale=float(P) ** -0.5).then_inc(a_squared.sem, 1)
                if n is not None:
                    values_high(l, n)
                act.wait_ge(att_read.sem, att_read.at(l, "B", h))
                rms(l, "B", h, 0, proj[1])

            pair_of = [None]

            def n_pair(h):
                return pair_of[0]

            def cross_step(l, i):
                exps(l, "C", i, 0, "m", p_a, CROSS_SCALE)

            def cross_high(l, i):
                act.wait_ge(att_full.sem, att_full.at(l, "C", i))
                for j in range(NM):
                    flip_high(l, "C", i, 2 + j, pt_hi[:, j * SEQ:(j + 1) * SEQ], flip[j][:, :])

            def memory_high(l, i):
                act.wait_ge(att_full.sem, att_full.at(l, "C", i))
                for j in range(NM):
                    flip_high(l, "C", i, j, v_hi[:, j, :], flip[j][:, 0:P])

            def out_cross(l, i, s, b, dst, cols):
                act.wait_ge(slot_done.sem, slot_done.at(l, "C", i, s + 1))
                copy(dst, proj[b][:, 0:cols]).then_inc(kv_copied.sem, 1)

            act.dma_start(pos_i[:, :], positions[0, :].rearrange("(t p) -> p t", p=P),
                          allow_slow_non_contiguous=True).then_inc(in_pos, 16)
            act.dma_start(lam_in[:, :, :, :].rearrange("p l a d -> p (l a d)"),
                          diff_lambda.rearrange("l a d -> (l a d)").partition_broadcast(P)).then_inc(in_lam, 16)
            act.wait_ge(const_ready, 1)
            for l in range(1, DEPTH):
                load_gains(act, l)
            act.wait_ge(const_ready, 2)
            act.wait_ge(pre_vec, 1)
            sc.activation(sin_t[:, :, :], ang[:, :, :], ACT.Sin)
            sc.activation(half_t[:, :, :], ang[:, :, :], ACT.Sin, scale=0.5).then_inc(pre_act, 1)
            act.wait_ge(pre_vec, 2)
            sc.preload_act_table_set(LN_EXP)
            sc.activation(lam_exp[:, :], lam_sum[:, :], ACT.Exp).then_inc(pre_act, 1)

            def first_slot(s):
                act.wait_ge(raw_full[s % 2], 32 * (s // 2 + 1))
                copy(w_hi[s][:, :], raw[s % 2][:, :]).then_inc(slot_hi.sem, 1)
            for k in range(KD):
                act.wait_ge(pre_full, k + 2)
                copy(xT[:, k, :], flip[(1 + k) % 2][:, :]).then_inc(x_copied, 1)
                act.wait_ge(x_copied, k + 1)
                if k >= 2:
                    act.wait_ge(sq_added.sem, k)
                sc.activation(x_sq[:, k % 2, :], xT[:, k, :], ACT.Square, scale=float(D) ** -0.5).then_inc(sq_done.sem, 1)
                act.wait_ge(pair_ready.sem, k + 2)
                copy(h_hi[:, k, :], pair[:, k % 2, :]).then_inc(pair_hi.sem, 1)
            act.wait_ge(in_mem, 16)
            for t in range(NM):
                act.wait_ge(pre_act, 2 + t)
                sc.activation(mem_sq[:, :], mem_in[:, t, :], ACT.Square, scale=float(D) ** -0.5,
                              accum_out=mem_ss[:, t:t + 1]).then_inc(pre_act, 1)
            act.wait_ge(pre_act, NM + 2)
            sc.activation(mem_rstd[:, :], mem_ss[:, :], ACT.Ln, bias=eps[:, 0:1]).then_inc(pre_act, 1)
            act.wait_ge(pre_act, NM + 3)
            sc.activation(mem_rstd[:, :], mem_rstd[:, :], ACT.Exp, scale=-0.5).then_inc(pre_act, 1)
            for s in range(AHEAD + 1):
                first_slot(s)
            act.wait_ge(pre_read, 5 + KD // 2)
            act.dma_start(mem_scratch[:, :, :], mem_n[:, :, :]).then_inc(mem_stored, 16)
            act.dma_start(table_scratch[:, :, :], tables_d[:, :, :]).then_inc(mem_stored, 16)

            with act.Fori(0, DEPTH) as l:
                act.wait_ge(slot_done.sem, slot_done.at(l, "C"))
                act.wait_ge(gl_ready.sem, gl_ready.at(l, "N1", 0, 1))
                act.wait_ge(mem_loaded.sem, mem_loaded.at(l, "H"))
                for k in range(KD):
                    sc.activation(mem_hi[:, k, :], mem_n[:, k, :], ACT.Copy, scale=gl[:, G_MEM + k:G_MEM + k + 1]).then_inc(memh_hi.sem, 1)
                rms(l, "N1", 0, 0, r=rstd_x)
                split_ahead(l, "C", 0, 1)
                out_cross(l, 0, 1, 1, kT[:, 0:MEM], MEM)
                split_ahead(l, "C", 0, 2)
                act.wait_ge(mem_stored, 32)
                out_cross(l, 0, 2, 0, vT[:, 0:MEM], MEM)
                split_ahead(l, "C", 0, 3)
                squares(l, "C", 0, 0, cq_raw[:, 0, :])
                memory_high(l, 0)
                with act.Fori(0, CROSS - 1) as i:
                    cross_step(l, i)
                    split_ahead(l, "C", i + 1, 0)
                    cross_high(l, i)
                    split_ahead(l, "C", i + 1, 1)
                    out_cross(l, i + 1, 1, 1, kT[:, 0:MEM], MEM)
                    split_ahead(l, "C", i + 1, 2)
                    out_cross(l, i + 1, 2, 0, vT[:, 0:MEM], MEM)
                    split_ahead(l, "C", i + 1, 3)
                    squares(l, "C", i + 1, 0, cq_raw[:, bass.ds(i + 1, 1), :].rearrange("p a n -> p (a n)"))
                    memory_high(l, i + 1)
                i = CROSS - 1
                cross_step(l, i)
                split_ahead(l, "A", 0, 0)
                for j in range(KVT):
                    act.wait_ge(ckv_copied.sem, ckv_copied.at(l, "A", 0, j + 1))
                    sc.activation(ckv_sq[:, j, :], ckv_raw[:, j, :], ACT.Square, scale=float(KV_LORA) ** -0.5).then_inc(ckv_squared.sem, 1)
                    if j == 0:
                        cross_high(l, i)
                        rms(l, "A", 0, 0)
                        split_ahead(l, "A", 0, 1)
                        for k in range(QT):
                            pair_high(l, "A", k, cq_hi[:, k, :])
                        split_ahead(l, "A", 0, 2)
                split_ahead(l, "A", 0, 3)
                rms(l, "A", 0, 1)
                for k in range(KVT):
                    pair_high(l, "A", QT + k, ckv_hi[:, k, :])
                split_ahead(l, "B", 0, 0)
                split_ahead(l, "B", 0, 1)
                out_kv(l, 0)
                split_ahead(l, "B", 0, 2)
                split_ahead(l, "B", 0, 3)
                values_high(l, 0)
                with act.Fori(0, HEADS // 2 - 1) as hp:
                    pair_of[0] = hp
                    for e in range(2):
                        head(l, hp * 2 + e, hp * 2 + (e + 1), e)
                head(l, HEADS - 2, HEADS - 1, 0)
                head(l, HEADS - 1, None, 1)
                sc.activation(warm[:, :], eps[:, :], ACT.Sigmoid)
                act.wait_ge(att_read.sem, att_read.at(l, "B", HEADS))
                split_ahead(l, "E", 0, 0)
                for k in range(16):
                    copy(outs_hi[:, k, :], outs[:, k, :]).then_inc(outs_split_hi.sem, 1)
                with act.Fori(0, 2) as jj:
                    for e in range(4):
                        for g in range(3):
                            s = 5 * e + g
                            if s:
                                split_ahead(l, "E", jj, s)
                            act.wait_ge(gate_out.sem, gate_out.at(l, "E", jj, 3 * e + g + 1))
                            sc.activation(sig[:, g, :], sig[:, g, :], ACT.Sigmoid).then_inc(sig_ready.sem, 1)
                        split_ahead(l, "E", jj, 5 * e + 3)
                        split_ahead(l, "E", jj, 5 * e + 4)
                        if e == 3:
                            split_ahead(l, "E", jj, 20)
                        act.wait_ge(mix_ready.sem, mix_ready.at(l, "E", jj, e + 1))
                        copy(mix_hi[:, bass.ds(jj * 4 + e, 1), :].rearrange("p a n -> p (a n)"), mix[:, :]).then_inc(mix_split_hi.sem, 1)
                sc.preload_act_table_set(LN_EXP)
                with act.Fori(0, 2) as jj:
                    for e in range(4):
                        if e:
                            split_ahead(l, "F", jj, e)
                        pair_high(l, "F", e, h_hi[:, bass.ds(jj * 4 + e, 1), :].rearrange("p a n -> p (a n)"), jj)
                        if e == 3:
                            split_ahead(l, "F", jj, 4)
                        squares(l, "F", jj, e, xT[:, bass.ds(jj * 4 + e, 1), :].rearrange("p a n -> p (a n)"))
                rms(l, "N2", 0, 0)
                sc.activation(warm[:, :], eps[:, :], ACT.Sigmoid)
                def gate_up(t):
                    for e in range(2):
                        if e:
                            split_ahead(l, "G", t, 2)
                        act.wait_ge(gate_read.sem, gate_read.at(l, "G", t, e + 1))
                        act.wait_ge(gate_used.sem, gate_used.at(l, "G", t))
                        sc.activation(sig_f[:, e, :], gate_n[:, :], ACT.Sigmoid).then_inc(silu_sig.sem, 1)
                        split_ahead(l, "G", t, 2 * e + 1)
                        act.wait_ge(hid_ready.sem, hid_ready.at(l, "G", t, e + 1))
                        copy(hid_hi[:, bass.ds(t * 2 + e, 1), :].rearrange("p a n -> p (a n)"), hid[:, e, :]).then_inc(hid_split_hi.sem, 1)
                    split_ahead(l, "G", t, 4)
                gate_up(0)
                with act.Fori(0, FT // 2 - 1) as t:
                    gate_up(t + 1)
                sc.preload_act_table_set(LN_EXP)
                act.wait_ge(hid_split.sem, hid_split.at(l, "G", FT // 2))
                act.dma_start(mem_n[:, :, :], mem_scratch[:, :, :]).then_inc(mem_loaded.sem, 16)
                act.dma_start(tables_d[:, :, :], table_scratch[:, :, :]).then_inc(mem_loaded.sem, 16)
                with act.Fori(0, 4) as jj:
                    for e in range(2):
                        for c in range(4):
                            if e or c:
                                split_ahead(l, "H", jj, 4 * e + c)
                        squares(l, "H", jj, e, xT[:, bass.ds(jj * 2 + e, 1), :].rearrange("p a n -> p (a n)"))
                        pair_high(l, "H", e, h_hi[:, bass.ds(jj * 2 + e, 1), :].rearrange("p a n -> p (a n)"), jj)
                        if e:
                            split_ahead(l, "H", jj, 8)
            act.wait_ge(mem_loaded.sem, mem_loaded.end(DEPTH))
            act.wait_ge(ssq_full.sem, ssq_full.end(DEPTH) + 1)
            sc.activation(rstd[:, :], ssq[:, :], ACT.Ln, bias=eps[:, 0:1]).then_inc(ssq_read.sem, 1)
            act.wait_ge(ssq_read.sem, ssq_read.end(DEPTH) + 1)
            sc.activation(rstd[:, :], rstd[:, :], ACT.Exp, scale=-0.5).then_inc(rms_ready.sem, 1)
            for n in range(1, 2 * NT, 2):
                act.wait_ge(y_flipped, n + 1)
                act.wait_ge(y_copied, n)
                copy(y_out[:, n // 2, 512:1024], flip[1][:, :]).then_inc(y_copied, 1)

        @block.vector
        def _(ve):
            v = nc.vector
            start_counts(ve, "ve")
            state = {"origin": 0, "n": 0}

            def begin(l, stage, step=0):
                state["origin"], state["n"] = vec_step.at(l, stage, step), 0

            def end(stage):
                assert state["n"] == vec_step.start[stage][1], (stage, state["n"])

            def chain(ins):
                state["n"] += 1
                ins.then_inc(vec_step.sem, 1)
                ve.wait_ge(vec_step.sem, state["origin"] + state["n"])

            def one(t, i):
                return t[:, bass.ds(i, 1), :].rearrange("p a n -> p (a n)") if not isinstance(i, int) else t[:, i, :]

            SHUF_D = [(i + 8) % 16 if i < 16 else i for i in range(32)]
            SHUF_M = [(i + 16) % 32 for i in range(32)]

            def rope(dst, src, rows, cos, sin, mask, last):
                ve.wait_ge(last[0].sem, last[1])
                v.tensor_tensor(mid[rows, :], src[rows, :], cos[rows, :], ALU.mult)
                chain(v.stream_shuffle(rot[rows, :], src[rows, :], mask))
                chain(v.tensor_tensor(rot[rows, :], rot[rows, :], sin[rows, :], ALU.mult))
                return v.tensor_tensor(dst[rows, :], mid[rows, :], rot[rows, :], ALU.add)

            def maxima(l, stage, step, n, k, scale):
                top, bias, _, _ = stat[k]
                for t in (range(NT) if stage == "C" else (3, 2, 0, 1)):
                    if stage == "C":
                        full, src = t // 2 + 1, score[t // 2][:, (t % 2) * MEM:(t % 2 + 1) * MEM]
                    else:
                        b, c = {3: (0, 0), 2: (1, 0), 0: (1, 384), 1: (2, 0)}[t]
                        full, src = b + 1, score[b][:, c:c + (t + 1) * P]
                    if stage == "C" and t % 2 == 0 or stage == "B" and t != 0:
                        ve.wait_ge(score_full.sem, score_full.at(l, stage, step, 3 * n + full))
                    ins = v.tensor_reduce(top[:, t:t + 1], src, AX.X, ALU.max)
                chain(ins)
                v.tensor_scalar(bias[:, :], top[:, :], -scale, None, ALU.mult).then_inc(bias_ready.sem, 1)

            def invert(l, stage, step, n, k):
                _, _, total, inv = stat[k]
                ve.wait_ge(exp_done.sem, exp_done.at(l, stage, step, 4 * (n + 1)))
                chain(v.reciprocal(inv[:, :], total[:, :]))

            def normalise(p, inv, off, size):
                for t in range(NT):
                    s = p[:, off(t):off(t) + size(t)]
                    ins = v.tensor_scalar(s, s, inv[:, t:t + 1], None, ALU.mult)
                return ins

            def flip_low(l, stage, step, k, dst, src, hi):
                ve.wait_ge(flip_hi.sem, flip_hi.at(l, stage, step, k + 1))
                v.tensor_tensor(dst, src, hi.bitcast(F32), ALU.subtract).then_inc(flip_read.sem, 1)

            def causal_low(l, h, n, part):
                if part == 0:
                    flip_low(l, "B", h, 2 + 3 * n, pt_lo[:, 0:512], flip[n][:, :], pt_hi[:, 0:512])
                    flip_low(l, "B", h, 3 + 3 * n, pt_lo[:, 512:896], flip[1 - n][:, 0:384], pt_hi[:, 512:896])
                else:
                    flip_low(l, "B", h, 4 + 3 * n, pt_lo[:, 896:1280], flip[n][:, 0:384], pt_hi[:, 896:1280])

            def values_low(l, h):
                for k, (lo, hi) in enumerate(((v_lo, v_hi), (mv_lo, mv_hi))):
                    flip_low(l, "B", h, k, lo[:, :, :].rearrange("p j d -> p (j d)"), flip[k][:, :],
                             hi[:, :, :].rearrange("p j d -> p (j d)"))

            def out_latent(l, h, last=None):
                ve.wait_ge(mq_done.sem, mq_done.at(l, "B", h, 1))
                last = last or (diff_ready, diff_ready.at(l, "B", h))
                rope(mqT, proj[1], slice(0, 96), cos_m, sin_m, SHUF_M, last).then_inc(mla_ready.sem, 1)
                ve.wait_ge(kv_copied.sem, kv_copied.at(l, "B", h, 1))
                v.tensor_copy(mkT[0:64, :], kvT[0:64, :]).then_inc(mla_ready.sem, 1)

            def out_qk(l, h, s, b, dst):
                ve.wait_ge(slot_done.sem, slot_done.at(l, "B", h, s + 1))
                last = (mla_ready, mla_ready.at(l, "B", h, 1)) if s == 2 else (diff_ready, diff_ready.at(l, "B", h, 1))
                rope(dst, proj[b], slice(0, P), cos_d, sin_d, SHUF_D, last).then_inc(diff_ready.sem, 1)

            def rms(l, stage, k):
                ve.wait_ge(rms_ready.sem, rms_ready.at(l, stage, 0, k + 1))

            def newton(r):
                chain(v.tensor_tensor(square[:, :], r[:, :], r[:, :], ALU.mult))
                chain(v.scalar_tensor_tensor(square[:, :], ssq[:, :], EPS, square[:, :], ALU.add, ALU.mult))
                chain(v.tensor_scalar(square[:, :], square[:, :], -0.5, 1.5, ALU.mult, ALU.add))
                chain(v.tensor_tensor(r[:, :], r[:, :], square[:, :], ALU.mult))

            def norm(l, stage, k0, src, gain, n, hi, lo):
                def low(k):
                    ve.wait_ge(pair_hi.sem, pair_hi.at(l, stage, 0, k0 + k + 1))
                    v.tensor_tensor(lo[:, k, :], pair[:, (k0 + k) % 2, :], hi[:, k, :].bitcast(F32), ALU.subtract).then_inc(pair_lo.sem, 1)
                for k in range(n):
                    if k >= 2:
                        ve.wait_ge(pair_lo.sem, pair_lo.at(l, stage, 0, k0 + k - 1))
                    v.scalar_tensor_tensor(pair[:, (k0 + k) % 2, :], src[:, k, :], gl[:, gain + k:gain + k + 1], rstd[:, :],
                                           ALU.mult, ALU.mult).then_inc(pair_ready.sem, 1)
                    if k:
                        low(k - 1)
                low(n - 1)

            def add_square(l, stage, step, k, acc):
                ve.wait_ge(sq_done.sem, sq_done.at(l, stage, step, k + 1))
                v.tensor_tensor(acc[:, :], acc[:, :], square[:, :], ALU.add).then_inc(sq_added.sem, 1)
                ve.wait_ge(sq_added.sem, sq_added.at(l, stage, step, k + 1))

            def head(l, h, n):
                begin(l, "B" if n is not None else "L", h if n is not None else 0)
                invert(l, "B", h, 0, "m")
                normalise(p_a, stat["m"][3], q_off, lambda t: (t + 1) * P).then_inc(prob_ready.sem, 1)
                if n is not None:
                    out_v(l, n)
                maxima(l, "B", h, 1, "d1", DIFF_SCALE)
                causal_low(l, h, 0, 0)
                if n is not None:
                    out_latent(l, n)
                causal_low(l, h, 0, 1)
                invert(l, "B", h, 1, "d1")
                chain(normalise(p_b, stat["d1"][3], q_off, lambda t: (t + 1) * P))
                maxima(l, "B", h, 2, "d2", DIFF_SCALE)
                invert(l, "B", h, 2, "d2")
                chain(v.tensor_scalar(lam_scale[:, :], stat["d2"][3][:, :], gl[:, G_LAM:G_LAM + 1], None, ALU.mult))
                for t in range(NT):
                    s = slice(q_off(t), q_off(t) + (t + 1) * P)
                    ins = v.scalar_tensor_tensor(p_b[:, s], p_a[:, s], lam_scale[:, t:t + 1], p_b[:, s], ALU.mult, ALU.add)
                ins.then_inc(prob_ready.sem, 1)
                if n is not None:
                    out_qk(l, n, 2, 1, qT)
                causal_low(l, h, 1, 0)
                causal_low(l, h, 1, 1)
                if n is not None:
                    out_qk(l, n, 3, 0, kT)
                    maxima(l, "B", n, 0, "m", MLA_SCALE)
                    values_low(l, n)
                ve.wait_ge(rms_ready.sem, rms_ready.at(l, "B", h, 1))
                v.scalar_tensor_tensor(one(outs, h), att[:, :], gl[:, G_SUB:G_SUB + 1], rstd[:, :], ALU.mult, ALU.mult).then_inc(att_read.sem, 1)

                end("B" if n is not None else "L")

            def cross_prob(l, i):
                maxima(l, "C", i, 0, "m", CROSS_SCALE)
                invert(l, "C", i, 0, "m")
                normalise(p_a, stat["m"][3], lambda t: t * MEM, lambda t: MEM).then_inc(prob_ready.sem, 1)

            def cross_low(l, i):
                for j in range(NM):
                    s = slice(j * SEQ, (j + 1) * SEQ)
                    flip_low(l, "C", i, 2 + j, pt_lo[:, s], flip[j][:, :], pt_hi[:, s])

            def memory_low(l, i):
                for j in range(NM):
                    flip_low(l, "C", i, j, v_lo[:, j, :], flip[j][:, 0:P], v_hi[:, j, :])

            def cross_out(l, i):
                ve.wait_ge(att_full.sem, att_full.at(l, "C", i, 1))
                v.tensor_copy(one(outs, i + 12), att[:, :]).then_inc(att_read.sem, 1)

            def out_xq(l, i):
                ve.wait_ge(slot_done.sem, slot_done.at(l, "C", i, 1))
                v.tensor_tensor(qT[:, :], proj[0][:, :], rstd_x[:, :], ALU.mult).then_inc(xq_copied.sem, 1)

            def out_v(l, h):
                ve.wait_ge(slot_done.sem, slot_done.at(l, "B", h, 1))
                v.tensor_tensor(vT[:, :], proj[0][:, :], rstd_x[:, :], ALU.mult).then_inc(v_copied.sem, 1)

            def out_cq(l, i):
                ve.wait_ge(slot_done.sem, slot_done.at(l, "C", i, 4))
                v.tensor_tensor(one(cq_raw, i), proj[1][:, :], rstd_x[:, :], ALU.mult).then_inc(tile_ready.sem, 1)
                add_square(l, "C", i, 0, q_sum)

            def out_residual(l, stage, step, k, s, b, tile, gain=None):
                ve.wait_ge(slot_done.sem, slot_done.at(l, stage, step, s))
                v.tensor_tensor(one(xT, tile), one(xT, tile), proj[b][:, :], ALU.add).then_inc(tile_ready.sem, 1)
                if gain is not None:
                    ve.wait_ge(tile_ready.sem, tile_ready.at(l, stage, step, k + 1))
                    ve.wait_ge(pair_lo.sem, pair_lo.at(l, stage, step, k - 1))
                    v.tensor_scalar(pair[:, k % 2, :], one(xT, tile), gains[:, bass.ds(tile + gain, 1)], None, ALU.mult).then_inc(pair_ready.sem, 1)
                add_square(l, stage, step, k, x_sum)
                if gain is not None:
                    ve.wait_ge(pair_hi.sem, pair_hi.at(l, stage, step, k + 1))
                    v.tensor_tensor(one(h_lo, tile), pair[:, k % 2, :], one(h_hi, tile).bitcast(F32), ALU.subtract).then_inc(pair_lo.sem, 1)

            pre = [0]

            def now(ins):
                pre[0] += 1
                ins.then_inc(pre_chain, 1)
                ve.wait_ge(pre_chain, pre[0])

            def fill(n, dst, cols=512):
                ve.wait_ge(pre_full, n + 1)
                v.tensor_copy(dst, flip[n % 2][:, 0:cols]).then_inc(pre_read, 1)

            ve.wait_ge(in_pos, 16)
            now(v.tensor_copy(pos_f[:, :], pos_i[:, :]))
            ve.wait_ge(const_ready, 2)
            for t in range(NT):
                ins = v.tensor_scalar(ang[:, t, :], freq[:, :], pos_f[:, t:t + 1], None, ALU.mult)
            now(ins)
            magic = 1.5 * 2 ** 23
            now(v.tensor_scalar(turns[:, :, :], ang[:, :, :], 1 / (2 * math.pi), magic, ALU.mult, ALU.add))
            now(v.tensor_scalar(turns[:, :, :], turns[:, :, :], -magic, None, ALU.add))
            c1 = 6.28125
            c2 = float(np.float32(math.floor((2 * math.pi - c1) * 2 ** 20) / 2 ** 20))
            c3 = 2 * math.pi - c1 - c2
            for c in (c1, c2, c3):
                now(v.scalar_tensor_tensor(ang[:, :, :], turns[:, :, :], -c, ang[:, :, :], ALU.mult, ALU.add))
            v.tensor_scalar(ang[:, :, :], ang[:, :, :], 3.1415925, -3.1415925, ALU.min, ALU.max).then_inc(pre_vec, 1)
            ve.wait_ge(in_lam, 16)
            pairs = lam_in[:, :, :, :].rearrange("p l (a b) d -> p (l a) b d", b=2)
            now(v.tensor_tensor(lam_prod[:, :, :], pairs[:, :, 0, :], pairs[:, :, 1, :], ALU.mult))
            v.tensor_reduce(lam_sum[:, :], lam_prod[:, :, :], AX.X, ALU.add).then_inc(pre_vec, 1)
            ve.wait_ge(pre_act, 1)
            now(v.tensor_tensor(cos_t[:, :, :], half_t[:, :, :], half_t[:, :, :], ALU.mult))
            v.tensor_scalar(neg_t[:, :, :], sin_t[:, :, :], -1.0, None, ALU.mult)
            now(v.tensor_scalar(cos_t[:, :, :], cos_t[:, :, :], -2.0, 1.0, ALU.mult, ALU.add))
            for c0, half, f0, kind in ((0, 8, 0, 0), (64, 8, 0, 0), (64, 16, 8, 2)):
                f = slice(f0, f0 + half)
                a, b = slice(c0, c0 + half), slice(c0 + half, c0 + 2 * half)
                v.tensor_copy(rope_t[:, kind, :, a], cos_t[:, :, f])
                v.tensor_copy(rope_t[:, kind, :, b], cos_t[:, :, f])
                v.tensor_copy(rope_t[:, kind + 1, :, a], neg_t[:, :, f])
                ins = v.tensor_copy(rope_t[:, kind + 1, :, b], sin_t[:, :, f])
            ins.then_inc(rope_ready, 1)
            ve.wait_ge(pre_full, 1)
            v.tensor_copy(gains[:, :], flip[0][:, 0:P]).then_inc(pre_read, 1)
            ve.wait_ge(pre_read, 1)

            def x_low(k):
                ve.wait_ge(pair_hi.sem, k + 2)
                v.tensor_tensor(h_lo[:, k, :], pair[:, k % 2, :], h_hi[:, k, :].bitcast(F32), ALU.subtract).then_inc(pair_lo.sem, 1)
                ve.wait_ge(sq_done.sem, k + 2)
                ve.wait_ge(sq_added.sem, k + 1)
                v.tensor_tensor(x_sum[:, :], x_sum[:, :], x_sq[:, k % 2, :], ALU.add).then_inc(sq_added.sem, 1)
            for k in range(KD):
                ve.wait_ge(x_copied, k + 1)
                if k >= 2:
                    ve.wait_ge(pair_lo.sem, k)
                v.tensor_scalar(pair[:, k % 2, :], xT[:, k, :], gains[:, k:k + 1], None, ALU.mult).then_inc(pair_ready.sem, 1)
                if k:
                    x_low(k - 1)
            x_low(KD - 1)
            ve.wait_ge(pre_act, 2)
            for l in range(DEPTH):
                lam_init = 0.8 - 0.6 * math.exp(-0.3 * l)
                sub = gains[:, l * G_N + G_SUB:l * G_N + G_SUB + 1]
                lam = gains[:, l * G_N + G_LAM:l * G_N + G_LAM + 1]
                now(v.tensor_tensor(lam, lam_exp[:, 2 * l + 1:2 * l + 2], lam_exp[:, 2 * l:2 * l + 1], ALU.subtract))
                v.tensor_scalar(lam, lam, -lam_init, None, ALU.add)
                now(v.tensor_scalar(sub, sub, 1.0 - lam_init, None, ALU.mult))
            for kind, t in enumerate((cos_d, sin_d, cos_m, sin_m)):
                fill(1 + KD + kind, t[:, :])
            ve.wait_ge(pre_act, NM + 4)
            for t in range(NM):
                v.tensor_scalar(mem_in[:, t, :], mem_in[:, t, :], mem_rstd[:, t:t + 1], None, ALU.mult).then_inc(mem_scaled, 1)
            for f in range(KD // 2):
                fill(1 + KD + 4 + f, mem_n[:, 2 * f:2 * f + 2, :].rearrange("p k n -> p (k n)"))

            with ve.Fori(0, DEPTH) as l:
                begin(l, "N1")
                v.tensor_copy(gl[:, :], gains[:, bass.ds(l * G_N, G_N)]).then_inc(gl_ready.sem, 1)
                ve.wait_ge(gl_ready.sem, gl_ready.at(l, "N1", 0, 1))
                for k in range(KD):
                    ve.wait_ge(memh_hi.sem, memh_hi.at(l, "N1", 0, k + 1))
                    v.scalar_tensor_tensor(mem_lo[:, k, :], mem_n[:, k, :], gl[:, G_MEM + k:G_MEM + k + 1],
                                           mem_hi[:, k, :].bitcast(F32), ALU.mult, ALU.subtract).then_inc(memh_lo.sem, 1)
                rms(l, "N1", 0)
                newton(rstd_x)
                chain(v.memset(q_sum[:, :], 0.0))
                end("N1")
                out_xq(l, 0)
                ve.wait_ge(mem_loaded.sem, mem_loaded.at(l, "H"))
                ve.wait_ge(mem_stored, 32)
                v.tensor_tensor(cos_d, cos_d, rstd_x[:, :], ALU.mult)
                v.tensor_tensor(sin_d, sin_d, rstd_x[:, :], ALU.mult)
                out_cq(l, 0)
                memory_low(l, 0)
                with ve.Fori(0, CROSS - 1) as i:
                    begin(l, "C", i)
                    cross_prob(l, i)
                    out_xq(l, i + 1)
                    cross_low(l, i)
                    cross_out(l, i)
                    out_cq(l, i + 1)
                    memory_low(l, i + 1)
                    end("C")
                i = CROSS - 1
                begin(l, "C", i)
                cross_prob(l, i)
                end("C")
                begin(l, "A")

                def out_ckv(j):
                    ve.wait_ge(slot_done.sem, slot_done.at(l, "A", 0, j + 1))
                    v.tensor_tensor(ckv_raw[:, j, :], proj[j][:, :], rstd_x[:, :], ALU.mult).then_inc(ckv_copied.sem, 1)
                out_ckv(0)
                cross_low(l, i)
                rms(l, "A", 0)
                out_ckv(1)
                norm(l, "A", 0, cq_raw, G_Q, QT, cq_hi, cq_lo)
                cross_out(l, i)
                ve.wait_ge(slot_done.sem, slot_done.at(l, "A", 0, 4))
                chain(rope(mkT, proj[0], slice(64, 96), cos_m, sin_m, SHUF_M, (pair_lo, pair_lo.at(l, "A", 0, QT))))
                v.tensor_tensor(mkT[64:96, :], mkT[64:96, :], rstd_x[64:96, :], ALU.mult).then_inc(mla_ready.sem, 1)
                ve.wait_ge(mla_ready.sem, mla_ready.at(l, "A", 0, 1))
                rms(l, "A", 1)
                ve.wait_ge(ckv_squared.sem, ckv_squared.at(l, "A", 0, 2))
                norm(l, "A", QT, ckv_raw, G_KV, KVT, ckv_hi, ckv_lo)
                end("A")
                begin(l, "P")
                out_v(l, 0)
                out_latent(l, 0, (pair_lo, pair_lo.at(l, "A", 0, QT + KVT)))
                out_qk(l, 0, 2, 1, qT)
                out_qk(l, 0, 3, 0, kT)
                maxima(l, "B", 0, 0, "m", MLA_SCALE)
                values_low(l, 0)
                end("P")
                with ve.Fori(0, HEADS // 2 - 1) as hp:
                    for e in range(2):
                        head(l, hp * 2 + e, hp * 2 + (e + 1))
                head(l, HEADS - 2, HEADS - 1)
                head(l, HEADS - 1, None)
                for k in range(16):
                    ve.wait_ge(outs_split_hi.sem, outs_split_hi.at(l, "E", 0, k + 1))
                    v.tensor_tensor(outs_lo[:, k, :], outs[:, k, :], outs_hi[:, k, :].bitcast(F32), ALU.subtract).then_inc(outs_split.sem, 1)
                with ve.Fori(0, 2) as jj:
                    begin(l, "E", jj)
                    for e in range(4):
                        ve.wait_ge(mix_ready.sem, mix_ready.at(l, "E", jj, e))
                        for g in range(3):
                            ve.wait_ge(slot_done.sem, slot_done.at(l, "E", jj, 5 * e + g + 1))
                            v.tensor_tensor(sig[:, g, :], proj[g % 2][:, :], rstd_x[:, :], ALU.mult).then_inc(gate_out.sem, 1)
                        ve.wait_ge(sig_ready.sem, sig_ready.at(l, "E", jj, 3 * e + 3))
                        ve.wait_ge(slot_done.sem, slot_done.at(l, "E", jj, 5 * e + 4))
                        ve.wait_ge(mix_split.sem, mix_split.at(l, "E", jj, e))
                        v.tensor_tensor(mix[:, :], proj[1][:, :], sig[:, 0, :], ALU.mult).then_inc(od_used.sem, 1)
                        ve.wait_ge(om_done.sem, om_done.at(l, "E", jj, e + 1))
                        v.tensor_tensor(sig[:, 1, :], proj[0][:, :], sig[:, 1, :], ALU.mult).then_inc(om_used.sem, 1)
                        ve.wait_ge(om_used.sem, om_used.at(l, "E", jj, e + 1))
                        chain(v.tensor_tensor(mix[:, :], mix[:, :], sig[:, 1, :], ALU.add))
                        ve.wait_ge(slot_done.sem, slot_done.at(l, "E", jj, 5 * e + 5))
                        v.tensor_tensor(sig[:, 2, :], proj[1][:, :], sig[:, 2, :], ALU.mult).then_inc(oc_used.sem, 1)
                        ve.wait_ge(oc_used.sem, oc_used.at(l, "E", jj, e + 1))
                        v.tensor_tensor(mix[:, :], mix[:, :], sig[:, 2, :], ALU.add).then_inc(mix_ready.sem, 1)
                        ve.wait_ge(mix_split_hi.sem, mix_split_hi.at(l, "E", jj, e + 1))
                        tile = jj * 4 + e
                        v.tensor_tensor(one(mix_lo, tile), mix[:, :], one(mix_hi, tile).bitcast(F32), ALU.subtract).then_inc(mix_split.sem, 1)
                    end("E")
                v.memset(x_sum[:, :], 0.0)
                with ve.Fori(0, 2) as jj:
                    for e in range(4):
                        out_residual(l, "F", jj, e, e + 1, e % 2, jj * 4 + e, l * G_N + G_FFN)
                begin(l, "N2")
                rms(l, "N2", 0)
                newton(rstd)
                v.memset(x_sum[:, :], 0.0)
                end("N2")

                def gate_up(t):
                    begin(l, "G", t)
                    for e in range(2):
                        ve.wait_ge(slot_done.sem, slot_done.at(l, "G", t, 2 * e + 1))
                        ve.wait_ge(gate_used.sem, gate_used.at(l, "G", t, e))
                        v.tensor_tensor(gate_n[:, :], proj[0][:, :], rstd[:, :], ALU.mult).then_inc(gate_read.sem, 1)
                        ve.wait_ge(silu_sig.sem, silu_sig.at(l, "G", t, e + 1))
                        ve.wait_ge(hid_split.sem, hid_split.at(l, "G", t, e))
                        v.tensor_tensor(gated[:, :], gate_n[:, :], sig_f[:, e, :], ALU.mult).then_inc(gate_used.sem, 1)
                        ve.wait_ge(gate_used.sem, gate_used.at(l, "G", t, e + 1))
                        chain(v.tensor_tensor(gated[:, :], gated[:, :], rstd[:, :], ALU.mult))
                        ve.wait_ge(slot_done.sem, slot_done.at(l, "G", t, 2 * e + 2))
                        v.tensor_tensor(hid[:, e, :], proj[1][:, :], gated[:, :], ALU.mult).then_inc(hid_ready.sem, 1)
                        ve.wait_ge(hid_split_hi.sem, hid_split_hi.at(l, "G", t, e + 1))
                        tile = t * 2 + e
                        v.tensor_tensor(one(hid_lo, tile), hid[:, e, :], one(hid_hi, tile).bitcast(F32), ALU.subtract).then_inc(hid_split.sem, 1)
                    end("G")
                gate_up(0)
                with ve.Fori(0, FT // 2 - 1) as t:
                    gate_up(t + 1)
                with ve.Fori(0, 4) as jj:
                    for e in range(2):
                        out_residual(l, "H", jj, e, 4 * e + 4, e, jj * 2 + e, (l + 1) * G_N + G_ATTN)
            ve.wait_ge(rms_ready.sem, rms_ready.end(DEPTH) + 1)
            for k in range(KD):
                c = DEPTH * G_N + k
                v.scalar_tensor_tensor(y_T[:, k, :], xT[:, k, :], gains[:, c:c + 1], rstd[:, :], ALU.mult, ALU.mult).then_inc(y_ready, 1)
            for n in range(0, 2 * NT, 2):
                ve.wait_ge(y_flipped, n + 1)
                ve.wait_ge(y_copied, n)
                v.tensor_copy(y_out[:, n // 2, 0:512], flip[0][:, :]).then_inc(y_copied, 1)


def kernel(**inputs):
    import concourse.bacc as bacc
    from concourse.bass_utils import run_bass_kernel_spmd

    names = ["x", "mem", "positions", "attn_norm_w", "w_in", "diff_lambda", "diff_subln_w", "w_o_diff", "mla_q_norm_w",
             "mla_w_uq", "mla_kv_norm_w", "mla_w_ukv", "w_o_mla", "mem_norm_w", "w_mem_kv", "w_o_cross", "w_out",
             "ffn_norm_w", "w_gate_up", "w_down", "final_norm_w"]
    nc = bacc.Bacc("TRN2", target_bir_lowering=False, num_devices=1)
    arrays, args = {}, []
    for name in names:
        a = np.ascontiguousarray(inputs[name])
        arrays[f"in_{name}"] = a
        args.append(nc.dram_tensor(f"in_{name}", a.shape, mybir.dt.from_np(a.dtype), kind="ExternalInput").ap())
    args.append(nc.dram_tensor("out", (1, SEQ, D), F32, kind="ExternalOutput").ap())
    args.append(nc.dram_tensor("mem_scratch", (P, KD, MEM), F32, kind="Internal").ap())
    args.append(nc.dram_tensor("table_scratch", (P, 2, SEQ), F32, kind="Internal").ap())
    build_trunk(nc, *args)
    r = run_bass_kernel_spmd(nc, [arrays], core_ids=[0])
    return r.results[0]["out"]
```

```python
import math
from contextlib import ExitStack

import numpy as np
import concourse.bass as bass
from concourse import mybir

F32 = mybir.dt.float32
F32R = mybir.dt.float32r
BF16 = mybir.dt.bfloat16
I32 = mybir.dt.int32
ACT = mybir.ActivationFunctionType
ALU = mybir.AluOpType
AX = mybir.AxisListType

P = 128
D = 1024
SEQ = 512
MEM = 256
DEPTH = 2
EPS = 1e-6
THETA = 500000.0
KD = D // P
NT = SEQ // P
NM = MEM // P
HEADS = 8
CROSS = 4
ROT_D, ROT_M = 16, 32
Q_LORA, KV_LORA = 512, 256
QT, KVT = Q_LORA // P, KV_LORA // P
FFN = 2816
FT = FFN // P
DOWN = (6, 6, 5, 5)
DIFF_SCALE = 64 ** -0.5
MLA_SCALE = 96 ** -0.5
CROSS_SCALE = 128 ** -0.5
C_DQ, C_DK, C_DV, C_CQ, C_CKV, C_KR, C_XQ, C_GATE = 0, 1024, 2048, 3072, 3584, 3840, 3872, 4384
MASKED = -3.0e38
LN_EXP = "natural_log_exp_and_others"
EARLY = 7
AHEAD = 3
CAUSAL = NT * (NT + 1) // 2 * P
G_ATTN, G_FFN, G_MEM, G_Q, G_KV, G_SUB, G_LAM, G_N = 0, 8, 16, 24, 28, 30, 31, 32


def q_off(t):
    return P * t * (t + 1) // 2


def k_off(j):
    return P * (NT * j - j * (j - 1) // 2)


class Tally:

    def __init__(self, sem, by, before=1, **stages):
        self.sem, self.by, self.start, total = sem, by, {}, 0
        for name, (per, steps) in stages.items():
            self.start[name] = (total, per)
            total += per * steps
        self.total, self.before = total, before

    def at(self, layer, stage, step=0, k=0):
        base, per = self.start[stage]
        return layer * self.total + step * per + (self.before + base + k)

    def index(self, layer, stage, step=0, k=0):
        base, per = self.start[stage]
        return layer * self.total + step * per + (base + k)

    def end(self, layers):
        return self.before + layers * self.total


def build_trunk(nc, x, mem, positions, attn_norm_w, w_in, diff_lambda, diff_subln_w, w_o_diff,
                mla_q_norm_w, mla_w_uq, mla_kv_norm_w, mla_w_ukv, w_o_mla, mem_norm_w, w_mem_kv,
                w_o_cross, w_out, ffn_norm_w, w_gate_up, w_down, final_norm_w, out, mem_scratch, table_scratch, x_scratch):
    ctx = ExitStack()
    with ctx:
        def sem(name):
            return ctx.enter_context(nc.semaphore(name))

        def bank(name):
            return ctx.enter_context(nc.psum_tensor(name, [P, 512], F32))

        cursor = [(nc.sbuf_base + 31) // 32 * 32]

        def here(name, shape, dt=F32):
            t = nc.alloc_sbuf_tensor_at(name, shape, dt, offset=cursor[0])
            size = int(np.prod(shape[1:])) * (2 if dt == BF16 else 4)
            cursor[0] += (size + 31) // 32 * 32
            return t

        x_at = cursor[0]
        xT = here("xT", [P, KD, SEQ])

        def over_x(name, n, dt=F32R):
            return nc.alloc_sbuf_tensor_at(name, [P, SEQ], dt, offset=x_at + n * SEQ * 4)

        q1, q2 = over_x("q1_hi_lo", 0), over_x("q2_lo_hi", 1)
        k1, k2 = over_x("k1_hi_hi", 2), over_x("k2_hi_hi", 3)
        k_lo = over_x("k_lo", 4)
        h_hi = here("h_hi", [P, KD, SEQ], F32R)
        h_lo = here("h_lo", [P, KD, SEQ], F32R)
        raw = [here(f"raw{s}", [P, KD * P]) for s in range(2)]
        w_hi = [here(f"w_hi{s}", [P, KD * P], F32R) for s in range(4)]
        w_lo = [here(f"w_lo{s}", [P, KD * P], F32R) for s in range(4)]
        tables_d = here("tables_d", [P, 2, SEQ])
        cos_d, sin_d = tables_d[:, 0, :], tables_d[:, 1, :]
        cos_m, sin_m = (here(n, [P, SEQ]) for n in ("cos_m", "sin_m"))
        ident = here("ident", [P, P])
        ident_b = here("ident_b", [P, P], BF16)
        mask_b = here("mask_b", [P, P], BF16)
        ones = here("ones", [P, P])
        gains = here("gains", [P, P])
        gl = here("gl", [P, G_N])
        stat = {k: [here(f"{n}_{k}", [P, NT]) for n in ("top", "bias", "total", "inv")]
                for k in ("m", "d1", "d2")}
        lam_scale = here("lam_scale", [P, NT])
        warm = here("warm", [P, 1])
        eps = here("eps", [P, 1])
        pool_mark = here("pool_mark", [P, 4])
        x_sum_at = cursor[0]
        x_sum = here("x_sum", [P, SEQ])
        rstd_x = nc.alloc_sbuf_tensor_at("rstd_x", [P, SEQ], F32, offset=x_sum_at)
        square = here("square", [P, SEQ])
        rstd_at = cursor[0]
        rstd = here("rstd", [P, SEQ])

        base = cursor[0]

        def at(name, offset, shape, dt=F32):
            return nc.alloc_sbuf_tensor_at(name, shape, dt, offset=base + offset)

        KB = 1024
        outs = at("outs", 0, [P, 16, SEQ])
        outs_lo = at("outs_lo", 0, [P, 16, SEQ], F32R)
        mem_hi = at("mem_hi", 0, [P, KD, MEM], F32R)
        mem_lo = at("mem_lo", 8 * KB, [P, KD, MEM], F32R)
        ckv_raw = at("ckv_raw", 0, [P, KVT, SEQ])
        ckv_sq = at("ckv_sq", 4 * KB, [P, KVT, SEQ])
        cq_raw = at("cq_raw", 16 * KB, [P, QT, SEQ])
        q_sum = nc.alloc_sbuf_tensor_at("q_sum", [P, SEQ], F32, offset=rstd_at)
        mem_n = at("mem_n", 88 * KB, [P, KD, MEM])
        cq_hi = at("cq_hi", 32 * KB, [P, QT, SEQ], F32R)
        cq_lo = at("cq_lo", 40 * KB, [P, QT, SEQ], F32R)
        ckv_hi = at("ckv_hi", 48 * KB, [P, KVT, SEQ], F32R)
        ckv_lo = at("ckv_lo", 52 * KB, [P, KVT, SEQ], F32R)
        T = 56 * KB
        p_a = at("p_a", T, [P, CAUSAL])
        p_b = at("p_b", T + 5 * KB, [P, CAUSAL])
        pt_hi = at("pt_hi", T + 10 * KB, [P, CAUSAL], F32R)
        pt_lo = at("pt_lo", T + 15 * KB, [P, CAUSAL], F32R)
        v_hi = at("v_hi", T + 20 * KB, [P, NT, P], F32R)
        v_lo = at("v_lo", T + 22 * KB, [P, NT, P], F32R)
        mv_hi = at("mv_hi", T + 24 * KB, [P, NT, P], F32R)
        mv_lo = at("mv_lo", T + 26 * KB, [P, NT, P], F32R)
        qT = at("qT", T + 28 * KB, [P, SEQ])
        kT = at("kT", T + 30 * KB, [P, SEQ])
        mqT = at("mqT", T + 32 * KB, [P, SEQ])
        mkT = at("mkT", T + 34 * KB, [P, SEQ])
        vT = at("vT", T + 36 * KB, [P, SEQ])
        kvT = at("kvT", T + 38 * KB, [P, SEQ])
        a_sq = at("a_sq", T + 40 * KB, [P, SEQ])
        rot = at("rot", T + 42 * KB, [P, SEQ])
        mid = at("mid", T + 44 * KB, [P, SEQ])
        pair = at("pair", T + 42 * KB, [P, 2, SEQ])
        outs_hi = at("outs_hi", 32 * KB, [P, 16, SEQ], F32R)
        mix_hi = at("mix_hi", 64 * KB, [P, KD, SEQ], F32R)
        mix_lo = at("mix_lo", 80 * KB, [P, KD, SEQ], F32R)
        sig = at("sig", 96 * KB, [P, 3, SEQ])
        mix = nc.alloc_sbuf_tensor_at("mix", [P, SEQ], F32, offset=rstd_at)
        hid_hi = at("hid_hi", 0, [P, FT, SEQ], F32R)
        hid_lo = at("hid_lo", 44 * KB, [P, FT, SEQ], F32R)
        sig_f = at("sig_f", 88 * KB, [P, 2, SEQ])
        gated = at("gated", 92 * KB, [P, SEQ])
        hid = at("hid", 94 * KB, [P, 2, SEQ])
        gate_n = at("gate_n", 98 * KB, [P, SEQ])
        x_in = at("x_in", 0, [P, NT, D])
        mem_in = at("mem_in", 16 * KB, [P, NM, D])
        gain_rows = at("gain_rows", 32 * KB, [P, P])
        lam_in = at("lam_in", 33 * KB, [P, DEPTH, 4, 64])
        lam_prod = at("lam_prod", 35 * KB, [P, DEPTH * 2, 64])
        lam_sum = at("lam_sum", 36 * KB, [P, DEPTH * 2])
        lam_exp = at("lam_exp", 36 * KB + 64, [P, DEPTH * 2])
        mem_ss = at("mem_ss", 36 * KB + 128, [P, NM])
        mem_rstd = at("mem_rstd", 36 * KB + 192, [P, NM])
        pos_i = at("pos_i", 36 * KB + 256, [P, NT], I32)
        pos_f = at("pos_f", 36 * KB + 320, [P, NT])
        freq = at("freq", 36 * KB + 384, [P, 24])
        ang = at("ang", 37 * KB, [P, NT, 24])
        turns = at("turns", 38 * KB, [P, NT, 24])
        sin_t = at("sin_t", 39 * KB, [P, NT, 24])
        cos_t = at("cos_t", 40 * KB, [P, NT, 24])
        half_t = at("half_t", 41 * KB, [P, NT, 24])
        neg_t = at("neg_t", 42 * KB, [P, NT, 24])
        rope_t = at("rope_t", 44 * KB, [P, 4, NT, P])
        mem_sq = at("mem_sq", 52 * KB, [P, NM, D])
        x_sq = at("x_sq", 60 * KB, [P, 2, SEQ])
        y_T = at("y_T", 16 * KB, [P, KD, SEQ])
        y_out = at("y_out", 0, [P, NT, D])
        assert base + 102 * KB <= nc.sbuf_usable_end, (base, nc.sbuf_usable_end)

        proj = [bank("proj0"), bank("proj1")]
        score = [bank("score0"), bank("score1"), bank("score2")]
        flip = [bank("flip0"), bank("flip1")]
        att = bank("att")
        last_score = [proj[0], proj[1], att]
        ssq = score[2]

        raw_full = [sem("raw_full0"), sem("raw_full1")]
        SLOTS = dict(C=(4, CROSS), A=(4, 1), B=(4, HEADS), E=(20, 2), F=(4, 2), G=(4, FT // 2), H=(8, 4))
        slot_hi = Tally(sem("slot_hi"), "act", **SLOTS)
        slot_lo = Tally(sem("slot_lo"), "pool", 2, **SLOTS)
        slot_done = Tally(sem("slot_done"), "pe", **SLOTS)
        mq_done = Tally(sem("mq_done"), "pe", B=(1, HEADS))
        om_done = Tally(sem("om_done"), "pe", E=(4, 2))
        SETS = dict(C=(1, CROSS), B=(3, HEADS))
        score_full = Tally(sem("score_full"), "pe", C=(2, CROSS), B=(9, HEADS))
        bias_ready = Tally(sem("bias_ready"), "ve", **SETS)
        exp_done = Tally(sem("exp_done"), "act", C=(4, CROSS), B=(12, HEADS))
        prob_ready = Tally(sem("prob_ready"), "ve", C=(1, CROSS), B=(2, HEADS))
        FLIPS = dict(C=(4, CROSS), B=(8, HEADS))
        flip_full = Tally(sem("flip_full"), "pe", **FLIPS)
        flip_hi = Tally(sem("flip_hi"), "act", **FLIPS)
        flip_read = Tally(sem("flip_read"), "ve", **FLIPS)
        ATT = dict(C=(1, CROSS), B=(2, HEADS))
        att_full = Tally(sem("att_full"), "pe", **ATT)
        att_read = Tally(sem("att_read"), "ve", **ATT)
        kv_copied = Tally(sem("kv_copied"), "act", C=(2, CROSS), B=(1, HEADS))
        xq_copied = Tally(sem("xq_copied"), "ve", C=(1, CROSS))
        v_copied = Tally(sem("v_copied"), "ve", B=(1, HEADS))
        gate_out = Tally(sem("gate_out"), "ve", E=(12, 2))
        mla_ready = Tally(sem("mla_ready"), "ve", A=(1, 1), B=(2, HEADS))
        diff_ready = Tally(sem("diff_ready"), "ve", B=(2, HEADS))
        qk_hi = Tally(sem("qk_hi"), "act", B=(6, HEADS))
        qk_split = Tally(sem("qk_split"), "ve", B=(2, HEADS))
        x_stored = Tally(sem("x_stored"), "act", N1=(16, 1))
        x_loaded = Tally(sem("x_loaded"), "act", E=(16, 1))
        SSQ = dict(N1=(1, 1), A=(2, 1), B=(1, HEADS), N2=(1, 1))
        ssq_full = Tally(sem("ssq_full"), "pe", **SSQ)
        ssq_read = Tally(sem("ssq_read"), "act", **SSQ)
        rms_ready = Tally(sem("rms_ready"), "act", **SSQ)
        SQ = dict(C=(1, CROSS), F=(4, 2), H=(2, 4))
        tile_ready = Tally(sem("tile_ready"), "ve", **SQ)
        sq_done = Tally(sem("sq_done"), "act", KD + 1, **SQ)
        sq_added = Tally(sem("sq_added"), "ve", KD + 1, **SQ)
        ckv_copied = Tally(sem("ckv_copied"), "ve", A=(2, 1))
        ckv_squared = Tally(sem("ckv_squared"), "act", A=(2, 1))
        a_squared = Tally(sem("a_squared"), "act", B=(1, HEADS))
        NORM = dict(A=(QT + KVT, 1), F=(4, 2), H=(2, 4))
        pair_ready = Tally(sem("pair_ready"), "ve", KD + 1, **NORM)
        pair_hi = Tally(sem("pair_hi"), "act", KD + 1, **NORM)
        pair_lo = Tally(sem("pair_lo"), "ve", KD + 1, **NORM)
        gl_ready = Tally(sem("gl_ready"), "ve", N1=(1, 1))
        mem_loaded = Tally(sem("mem_loaded"), "act", H=(32, 1))
        memh_hi = Tally(sem("memh_hi"), "act", N1=(KD, 1))
        memh_lo = Tally(sem("memh_lo"), "ve", N1=(KD, 1))
        outs_split_hi = Tally(sem("outs_split_hi"), "act", E=(16, 1))
        outs_split = Tally(sem("outs_split"), "ve", E=(16, 1))
        sig_ready = Tally(sem("sig_ready"), "act", E=(12, 2))
        od_used = Tally(sem("od_used"), "ve", E=(4, 2))
        om_used = Tally(sem("om_used"), "ve", E=(4, 2))
        oc_used = Tally(sem("oc_used"), "ve", E=(4, 2))
        mix_ready = Tally(sem("mix_ready"), "ve", E=(4, 2))
        mix_split_hi = Tally(sem("mix_split_hi"), "act", E=(4, 2))
        mix_split = Tally(sem("mix_split"), "ve", E=(4, 2))
        HID = dict(G=(2, FT // 2))
        gate_read = Tally(sem("gate_read"), "ve", **HID)
        silu_sig = Tally(sem("silu_sig"), "act", **HID)
        gate_used = Tally(sem("gate_used"), "ve", **HID)
        hid_ready = Tally(sem("hid_ready"), "ve", **HID)
        hid_split_hi = Tally(sem("hid_split_hi"), "act", **HID)
        hid_split = Tally(sem("hid_split"), "ve", **HID)
        const_step, const_ready = sem("const_step"), sem("const_ready")
        in_gain, in_mem, in_pos, in_lam = (sem(n) for n in ("in_gain", "in_mem", "in_pos", "in_lam"))
        in_x = [sem(f"in_x{quarter}") for quarter in range(4)]
        pre_full, pre_read, pre_act = sem("pre_full"), sem("pre_read"), sem("pre_act")
        pre_chain = sem("pre_chain")
        pre_vec, mem_stored, mem_scaled, rope_ready, x_copied = (sem(n) for n in ("pre_vec", "mem_stored", "mem_scaled", "rope_ready", "x_copied"))
        y_ready, y_flipped, stored = sem("y_ready"), sem("y_flipped"), sem("stored")
        y_copied = [sem("y_copied0"), sem("y_copied1")]
        vec_step = Tally(sem("vec_step"), "ve", N1=(5, 1), C=(2, CROSS), A=(3, 1), P=(7, 1), B=(14, HEADS - 1), L=(7, 1),
                         E=(4, 2), N2=(4, 1), G=(2, FT // 2))

        tallies = [
            sq_done, sq_added, slot_hi, slot_done, mq_done, om_done, score_full, bias_ready,
            exp_done, prob_ready, flip_full, flip_hi, flip_read, att_full, att_read, kv_copied,
            mla_ready, diff_ready, qk_hi, qk_split, x_stored, x_loaded, mem_loaded, xq_copied, v_copied, gate_out, ssq_full, ssq_read, rms_ready, tile_ready, ckv_copied,
            ckv_squared, a_squared, pair_ready, pair_hi, pair_lo, gl_ready, memh_hi, memh_lo,
            outs_split_hi, outs_split, sig_ready, od_used, om_used, oc_used, mix_ready,
            mix_split_hi, mix_split, gate_read, silu_sig, gate_used, hid_ready, hid_split_hi, hid_split,
            vec_step,
        ]

        def start_counts(engine, by):
            for t in tallies:
                if t.by == by:
                    engine.sem_inc(t.sem, 1)

        def load_gains(engine, l):
            for row, w, n in ((G_ATTN, attn_norm_w, KD), (G_FFN, ffn_norm_w, KD), (G_MEM, mem_norm_w, KD),
                              (G_Q, mla_q_norm_w, QT), (G_KV, mla_kv_norm_w, KVT), (G_SUB, diff_subln_w, 1)):
                engine.dma_start(gain_rows[l * G_N + row:l * G_N + row + n, :],
                                 w[l, :].rearrange("(k p) -> k p", p=P)).then_inc(in_gain, 16)

        block = ctx.enter_context(nc.Block())

        @block.sync
        def _(sp):
            sp.wait_ge(const_ready, 1)
            load_gains(sp, 0)
            sp.dma_start(gain_rows[DEPTH * G_N:DEPTH * G_N + KD, :],
                         final_norm_w.rearrange("(k p) -> k p", p=P)).then_inc(in_gain, 16)
            xv = x[0, :, :].rearrange("(t p) d -> p t d", p=P)
            for quarter in range(4):
                c = slice(quarter * (D // 4), (quarter + 1) * (D // 4))
                sp.dma_start(x_in[:, :, c], xv[:, :, c]).then_inc(in_x[quarter], 16)

            def slot(l, stage, step, s, *parts):
                sp.wait_ge(slot_lo.sem, slot_lo.at(l, stage, step, s - 1))
                assert len(parts) == 2
                for col, src in parts:
                    n, width = src.shape[1], src.shape[2]
                    sp.dma_start(raw[s % 2][:, col:col + n * width].rearrange("p (k n) -> p k n", k=n),
                                 src).then_inc(raw_full[s % 2], 16)

            def tiles(w, l, k0, k1, col, width=P):
                v = w.rearrange("l (k p) n -> l p k n", p=P)
                v = v[l:l + 1] if isinstance(l, int) else v[bass.ds(l, 1)]
                v = v[:, :, k0:k1, bass.ds(col, width)]
                return v.rearrange("a p k n -> (a p) k n")

            def whole(w, l, col):
                return (0, tiles(w, l, 0, 4, col)), (4 * P, tiles(w, l, 4, 8, col))

            def cross_slots(l, i):
                slot(l, "C", i, 0, *whole(w_in, l, C_XQ + i * P))
                slot(l, "C", i, 1, *whole(w_mem_kv, l, i * P))
                slot(l, "C", i, 2, *whole(w_mem_kv, l, 512 + i * P))
                slot(l, "C", i, 3, *whole(w_in, l, C_CQ + i * P))

            def latent(l, h):
                return ((0, tiles(mla_w_uq, l, 0, QT, h * 96, 96)), (QT * 96, tiles(mla_w_ukv, l, 0, KVT, h * P)))

            def head_slots(l, h):
                slot(l, "B", h, 0, *whole(w_in, l, C_DV + h * P))
                slot(l, "B", h, 1, *latent(l, h))
                slot(l, "B", h, 2, *whole(w_in, l, C_DQ + h * P))
                slot(l, "B", h, 3, *whole(w_in, l, C_DK + h * P))

            with sp.Fori(0, DEPTH) as l:
                slot(l, "C", 0, 0, *whole(w_in, l, C_XQ))
                slot(l, "C", 0, 1, *whole(w_in, l, C_CQ))
                slot(l, "C", 0, 2, *whole(w_mem_kv, l, 0))
                slot(l, "C", 0, 3, *whole(w_mem_kv, l, 512))
                with sp.Fori(0, CROSS - 1) as i:
                    cross_slots(l, i + 1)
                slot(l, "A", 0, 0, *whole(w_in, l, C_CKV))
                slot(l, "A", 0, 1, *whole(w_in, l, C_CKV + P))
                slot(l, "A", 0, 2, (0, tiles(w_in, l, 0, 2, C_KR - 64, 96)), (2 * 96, tiles(w_in, l, 2, 4, C_KR - 64, 96)))
                slot(l, "A", 0, 3, (0, tiles(w_in, l, 4, 6, C_KR - 64, 96)), (2 * 96, tiles(w_in, l, 6, 8, C_KR - 64, 96)))
                slot(l, "B", 0, 0, *whole(w_in, l, C_DV))
                slot(l, "B", 0, 1, *reversed(whole(w_in, l, C_DQ)))
                slot(l, "B", 0, 2, *reversed(latent(l, 0)))
                slot(l, "B", 0, 3, *whole(w_in, l, C_DK))
                with sp.Fori(1, HEADS) as h:
                    head_slots(l, h)
                with sp.Fori(0, 2) as jj:
                    for e in range(4):
                        j = jj * (4 * P) + e * P
                        for g in range(3):
                            slot(l, "E", jj, 5 * e + g, *whole(w_in, l, j + (C_GATE + g * D)))
                        slot(l, "E", jj, 5 * e + 3, *whole(w_o_diff, l, j))
                        slot(l, "E", jj, 5 * e + 4, (0, tiles(w_o_mla, l, 0, 4, j)), (4 * P, tiles(w_o_cross, l, 0, 4, j)))
                with sp.Fori(0, 2) as jj:
                    for e in range(4):
                        slot(l, "F", jj, e, *whole(w_out, l, jj * (4 * P) + e * P))
                with sp.Fori(0, FT // 2) as t:
                    for e in range(2):
                        slot(l, "G", t, 2 * e, *whole(w_gate_up, l, t * (2 * P) + e * P))
                        slot(l, "G", t, 2 * e + 1, *whole(w_gate_up, l, t * (2 * P) + (e * P + FFN)))
                with sp.Fori(0, 4) as jj:
                    for e in range(2):
                        k = 0
                        for c, n in enumerate(DOWN):
                            slot(l, "H", jj, 4 * e + c, (0, tiles(w_down, l, k, k + 3, jj * (2 * P) + e * P)),
                                 (3 * P, tiles(w_down, l, k + 3, k + n, jj * (2 * P) + e * P)))
                            k += n
            for s in range(AHEAD + 1):
                sp.wait_ge(slot_lo.sem, slot_lo.end(DEPTH) + s - 1)
                for half in range(2):
                    sp.dma_start(raw[s % 2][:, half * 512:(half + 1) * 512], w_out[0, 0:P, 0:512]).then_inc(raw_full[s % 2], 16)
            for n in range(2 * NT):
                half, t = n // NT, n % NT
                sp.wait_ge(y_copied[n % 2], n // 2 + 1)
                sp.dma_start(out[0, t * P:(t + 1) * P, half * 512:(half + 1) * 512],
                             y_out[:, t, half * 512:(half + 1) * 512]).then_inc(stored, 16)
            sp.wait_ge(stored, 16 * 2 * NT)
            sp.wait_ge(mem_stored, 32)

        @block.gpsimd
        def _(pool):
            g = nc.gpsimd
            n = [0]

            def step(ins):
                n[0] += 1
                ins.then_inc(const_step, 1)
                pool.wait_ge(const_step, n[0])

            step(g.memset(gain_rows[:, :], 0.0))
            g.memset(warm[:, :], 0.0).then_inc(const_ready, 1)
            g.memset(ones[:, :], 1.0)
            g.memset(eps[:, :], EPS)
            step(g.memset(ident[:, :], 0.0))
            step(g.affine_select(out=ident[:, :], in_=ident[:, :], compare_op=ALU.not_equal, fill=1.0,
                                 base=0, pattern=[[-1, P]], channel_multiplier=1))
            step(g.memset(ident_b[:, :], 0.0))
            step(g.affine_select(out=ident_b[:, :], in_=ident_b[:, :], compare_op=ALU.not_equal, fill=1.0,
                                 base=0, pattern=[[-1, P]], channel_multiplier=1))
            step(g.memset(mask_b[:, :], 0.0))
            step(g.affine_select(out=mask_b[:, :], in_=mask_b[:, :], compare_op=ALU.is_ge, fill=MASKED,
                                 base=0, pattern=[[-1, P]], channel_multiplier=1))
            g.memset(x_sum[:, :], 0.0)
            for r, rot_dim in ((0, ROT_D), (ROT_D // 2, ROT_M)):
                for i in range(rot_dim // 2):
                    f = np.float32(THETA) ** (-np.float32(i) * np.float32(2.0) / np.float32(rot_dim))
                    g.memset(freq[:, r + i:r + i + 1], float(f))
            for kind in range(4):
                step(g.memset(rope_t[:, kind, :, :], 1.0 - kind % 2))
            g.memset(pool_mark[:, 2:3], 0.0).then_inc(const_ready, 1)
            for b in range(2):
                g.memset(pool_mark[:, b:b + 1], 0.0).then_inc(slot_lo.sem, 1)
            total = slot_lo.total * DEPTH
            with pool.Fori(0, total // 4) as r:
                for s in range(4):
                    pool.wait_ge(slot_hi.sem, r * 4 + (slot_hi.before + s + 1))
                    g.tensor_tensor(w_lo[s][:, :], raw[s % 2][:, :], w_hi[s][:, :].bitcast(F32),
                                    ALU.subtract).then_inc(slot_lo.sem, 1)
            for s in range(AHEAD + 1):
                pool.wait_ge(slot_hi.sem, slot_hi.before + total + s + 1)
                g.tensor_tensor(w_lo[s][:, :], raw[s % 2][:, :], w_hi[s][:, :].bitcast(F32),
                                ALU.subtract).then_inc(slot_lo.sem, 1)

        @block.tensor
        def _(pe):
            mm = nc.tensor.matmul
            start_counts(pe, "pe")

            def product(pieces):
                last = len(pieces) - 1
                for n, (o, sh, sl, mh, ml) in enumerate(pieces):
                    mm(o, sh, mh, start=n == 0, stop=False)
                    mm(o, sh, ml, start=False, stop=False)
                    ins = mm(o, sl, mh, start=False, stop=n == last)
                return ins

            def unit(l, stage, step, s, b, free, n, rhs, width=P, cols=SEQ, first=0, before=None, start=True, stop=True):
                pe.wait_ge(slot_lo.sem, slot_lo.at(l, stage, step, s + 1))
                if free:
                    pe.wait_ge(free[0].sem, free[1])
                hi, lo = w_hi[s % 4], w_lo[s % 4]
                for k in range(n):
                    if before:
                        before(k)
                    c = first + k * width
                    rh, rl = rhs(k)
                    o = proj[b][0:width, 0:cols]
                    mm(o, hi[:, c:c + width], rh, start=start and k == 0, stop=False)
                    mm(o, hi[:, c:c + width], rl, start=False, stop=False)
                    ins = mm(o, lo[:, c:c + width], rh, start=False, stop=stop and k == n - 1)
                return ins

            def h_rhs(k):
                return h_hi[:, k, :], h_lo[:, k, :]

            def sum_squares(l, stage, k, *tiles):
                pe.wait_ge(ssq_read.sem, ssq_read.at(l, stage, 0, k))
                for n, t in enumerate(tiles):
                    ins = mm(ssq[:, :], ones[:, :], t, start=n == 0, stop=n == len(tiles) - 1)
                ins.then_inc(ssq_full.sem, 1)

            def flip_bank(l, stage, step, k):
                pe.wait_ge(flip_read.sem, flip_read.at(l, stage, step, k - 1) if stage == "B" or k else flip_read.at(l, stage, step, 0))
                return flip[k % 2]

            def causal_scores(l, h, n, banks=score, read=None, free=(None, None, None)):
                pe.wait_ge(exp_done.sem, exp_done.at(l, "B", h, 4 * n if read is None else read))
                for b, group in enumerate(((3,), (2, 0), (1,))):
                    if free[b]:
                        pe.wait_ge(free[b][0].sem, free[b][1])
                    for t in group:
                        o = banks[b][:, 384 * (t == 0):384 * (t == 0) + (t + 1) * P]
                        cols = slice(t * P, (t + 1) * P)
                        if n == 0:
                            mm(o, mqT[0:96, cols], mkT[0:96, 0:(t + 1) * P], start=True, stop=False)
                        else:
                            q, k, rows = ((q1, k1, slice(0, 64)), (q2, k2, slice(64, P)))[n - 1]
                            mm(o, q[:, cols], k[:, 0:(t + 1) * P], start=True, stop=False)
                            mm(o, q[rows, cols], k_lo[rows, 0:(t + 1) * P], start=False, stop=False)
                        ins = mm(o[:, t * P:(t + 1) * P], ident_b[:, :], mask_b[:, :], start=False, stop=True)
                    ins.then_inc(score_full.sem, 1)

            def causal_flip(l, h, n, part):
                p, k0 = (p_a, 2) if n == 0 else (p_b, 5)
                if part == 0:
                    pe.wait_ge(prob_ready.sem, prob_ready.at(l, "B", h, n + 1))
                fills = ((0,), (1,)) if part == 0 else ((2, 3),)
                for f, js in enumerate(fills):
                    k = k0 + 2 * part + f
                    b, col = flip_bank(l, "B", h, k), 0
                    for j in js:
                        for t in range(j, NT):
                            ins = nc.tensor.transpose(b[:, col:col + P], p[:, q_off(t) + j * P:q_off(t) + (j + 1) * P], ident[:, :])
                            col += P
                    ins.then_inc(flip_full.sem, 1)

            def causal_attend(l, h, n, vh, vl):
                pe.wait_ge(flip_read.sem, flip_read.at(l, "B", h, 5 + 3 * n))
                pe.wait_ge(att_read.sem, att_read.at(l, "B", h, n))
                product([(att[:, j * P:SEQ], vh[:, j, :], vl[:, j, :], pt_hi[:, k_off(j):k_off(j) + SEQ - j * P],
                          pt_lo[:, k_off(j):k_off(j) + SEQ - j * P]) for j in range(NT)]).then_inc(att_full.sem, 1)

            def flip_values(l, h):
                for k, (src, copied) in enumerate(((vT, v_copied), (kvT, kv_copied))):
                    pe.wait_ge(copied.sem, copied.at(l, "B", h, 1))
                    b = flip_bank(l, "B", h, k)
                    for j in range(NT):
                        ins = nc.tensor.transpose(b[:, j * P:(j + 1) * P], src[:, j * P:(j + 1) * P], ident[:, :])
                    ins.then_inc(flip_full.sem, 1)

            def project_v(l, h):
                unit(l, "B", h, 0, 0, (diff_ready, diff_ready.at(l, "B", h)), KD, h_rhs).then_inc(slot_done.sem, 1)

            def latent_units(l, h, s, free1, free0):
                unit(l, "B", h, s, 1, free1, QT, lambda k: (cq_hi[:, k, :], cq_lo[:, k, :]), width=96).then_inc(mq_done.sem, 1)
                unit(l, "B", h, s, 0, free0, KVT, lambda k: (ckv_hi[:, k, :], ckv_lo[:, k, :]), first=QT * 96).then_inc(slot_done.sem, 1)

            def project_latent(l, h):
                latent_units(l, h, 1, (diff_ready, diff_ready.at(l, "B", h)), (v_copied, v_copied.at(l, "B", h, 1)))

            def project_q(l, h):
                unit(l, "B", h, 2, 1, (mla_ready, mla_ready.at(l, "B", h, 1)), KD, h_rhs).then_inc(slot_done.sem, 1)

            def project_k(l, h, half=None):
                if half != 1:
                    ins = unit(l, "B", h, 3, 0, (kv_copied, kv_copied.at(l, "B", h, 1)), KD if half is None else 4, h_rhs, stop=half is None)
                if half == 1:
                    ins = unit(l, "B", h, 3, 0, None, 4, lambda k: h_rhs(k + 4), first=4 * P, start=False)
                if half != 0:
                    ins.then_inc(slot_done.sem, 1)

            def latent_scores(l, h):
                pe.wait_ge(mla_ready.sem, mla_ready.at(l, "B", h, 2))
                causal_scores(l, h, 0)

            def head(l, h, n):
                if n is not None:
                    project_v(l, n)
                pe.wait_ge(qk_split.sem, qk_split.at(l, "B", h, 2))
                if n is not None:
                    causal_scores(l, h, 1)
                else:
                    causal_scores(l, h, 1, last_score, 0, (None, (ssq_read, ssq_read.at(l, "B", h)), (att_read, att_read.at(l, "B", h))))
                    causal_scores(l, h, 2, score, 4)
                causal_flip(l, h, 0, 0)
                if n is not None:
                    pe.wait_ge(ssq_read.sem, ssq_read.at(l, "B", h))
                    project_latent(l, n)
                causal_flip(l, h, 0, 1)
                if n is not None:
                    causal_scores(l, h, 2)
                    project_q(l, n)
                else:
                    pe.wait_ge(exp_done.sem, exp_done.at(l, "B", h, 8))
                causal_attend(l, h, 0, mv_hi, mv_lo)
                if n is not None:
                    project_k(l, n, 0)
                causal_flip(l, h, 1, 0)
                if n is not None:
                    project_k(l, n, 1)
                causal_flip(l, h, 1, 1)
                if n is not None:
                    latent_scores(l, n)
                causal_attend(l, h, 1, v_hi, v_lo)
                if n is not None:
                    flip_values(l, n)
                pe.wait_ge(a_squared.sem, a_squared.at(l, "B", h, 1))
                pe.wait_ge(diff_ready.sem, diff_ready.at(l, "B", h + 1 if n is None else n, 0 if n is None else 1))
                mm(proj[1][:, :], ones[:, :], a_sq[:, :], start=True, stop=True).then_inc(ssq_full.sem, 1)

            def cross_scores(l, i):
                pe.wait_ge(kv_copied.sem, kv_copied.at(l, "C", i, 2))
                pe.wait_ge(xq_copied.sem, xq_copied.at(l, "C", i, 1))
                pe.wait_ge(exp_done.sem, exp_done.at(l, "C", i))
                for b in range(2):
                    for t in (2 * b, 2 * b + 1):
                        ins = mm(score[b][:, (t % 2) * MEM:(t % 2 + 1) * MEM], qT[:, t * P:(t + 1) * P], kT[:, 0:MEM], start=True, stop=True)
                    ins.then_inc(score_full.sem, 1)

            def cross_flip(l, i):
                pe.wait_ge(prob_ready.sem, prob_ready.at(l, "C", i, 1))
                for j in range(NM):
                    b = flip_bank(l, "C", i, 2 + j)
                    for t in range(NT):
                        ins = nc.tensor.transpose(b[:, t * P:(t + 1) * P], p_a[:, t * MEM + j * P:t * MEM + (j + 1) * P], ident[:, :])
                    ins.then_inc(flip_full.sem, 1)

            def cross_attend(l, i):
                pe.wait_ge(flip_read.sem, flip_read.at(l, "C", i, 4))
                pe.wait_ge(att_read.sem, att_read.at(l, "C", i))
                product([(att[:, :], v_hi[:, j, :], v_lo[:, j, :], pt_hi[:, j * SEQ:(j + 1) * SEQ], pt_lo[:, j * SEQ:(j + 1) * SEQ])
                         for j in range(NM)]).then_inc(att_full.sem, 1)

            def flip_memory(l, i):
                pe.wait_ge(kv_copied.sem, kv_copied.at(l, "C", i, 2))
                for j in range(NM):
                    b = flip_bank(l, "C", i, j)
                    nc.tensor.transpose(b[:, 0:P], vT[:, j * P:(j + 1) * P], ident[:, :]).then_inc(flip_full.sem, 1)

            def project_xq(l, i, before=None):
                unit(l, "C", i, 0, 0, (kv_copied, kv_copied.at(l, "C", i)), KD, h_rhs, before=before).then_inc(slot_done.sem, 1)

            def project_mem(l, i, s, b, free):
                unit(l, "C", i, s, b, free, KD, lambda k: (mem_hi[:, k, :], mem_lo[:, k, :]), cols=MEM).then_inc(slot_done.sem, 1)

            def project_cq(l, i):
                unit(l, "C", i, 3, 1, (kv_copied, kv_copied.at(l, "C", i, 1)), KD, h_rhs).then_inc(slot_done.sem, 1)

            fills = []
            fills.append(((in_gain, 16 * (6 * DEPTH + 1)), [(0, gain_rows[:, :])], [(pre_read, 1)]))
            for k in range(KD):
                fills.append(((in_x[k // (KD // 4)], 16), [(t, x_in[:, t, k * P:(k + 1) * P]) for t in range(NT)],
                              [(x_copied, k + 1)]))
            for f in range(KD // 2):
                fills.append(((mem_scaled, NM),
                              [(2 * e + t, mem_in[:, t, (2 * f + e) * P:(2 * f + e + 1) * P]) for e in range(2) for t in range(NM)],
                              [(pre_read, 2 + f)]))
            for kind in range(4):
                fills.append(((rope_ready, 1), [(t, rope_t[:, kind, t, :]) for t in range(NT)], [(pre_read, 2 + KD // 2 + kind)]))
            pe.wait_ge(const_ready, 2)
            for n, ((loaded, count), blocks, _) in enumerate(fills):
                pe.wait_ge(loaded, count)
                if n >= 2:
                    for reader, reads in fills[n - 2][2]:
                        pe.wait_ge(reader, reads)
                for c, src in blocks:
                    ins = nc.tensor.transpose(flip[n % 2][:, c * P:(c + 1) * P], src, ident[:, :])
                ins.then_inc(pre_full, 1)
            pe.wait_ge(pre_read, 5 + KD // 2)

            with pe.Fori(0, DEPTH) as l:
                project_xq(l, 0, before=lambda k: pe.wait_ge(pair_lo.sem, pair_lo.at(l, "A", 0, k + 1 - KD)))
                pe.wait_ge(sq_added.sem, sq_added.at(l, "C"))
                sum_squares(l, "N1", 0, x_sum[:, :])
                unit(l, "C", 0, 1, 1, (tile_ready, tile_ready.at(l, "C")), KD, h_rhs).then_inc(slot_done.sem, 1)
                pe.wait_ge(memh_lo.sem, memh_lo.at(l, "N1", 0, KD))
                project_mem(l, 0, 2, 0, (xq_copied, xq_copied.at(l, "C", 0, 1)))
                project_mem(l, 0, 3, 1, (tile_ready, tile_ready.at(l, "C", 0, 1)))
                flip_memory(l, 0)
                with pe.Fori(0, CROSS - 1) as i:
                    cross_scores(l, i)
                    project_xq(l, i + 1)
                    project_mem(l, i + 1, 1, 1, (tile_ready, tile_ready.at(l, "C", i + 1)))
                    cross_flip(l, i)
                    project_mem(l, i + 1, 2, 0, (xq_copied, xq_copied.at(l, "C", i + 1, 1)))
                    cross_attend(l, i)
                    project_cq(l, i + 1)
                    flip_memory(l, i + 1)
                i = CROSS - 1
                cross_scores(l, i)
                unit(l, "A", 0, 0, 0, (kv_copied, kv_copied.at(l, "C", CROSS)), KD, h_rhs).then_inc(slot_done.sem, 1)
                pe.wait_ge(sq_added.sem, sq_added.at(l, "F"))
                sum_squares(l, "A", 0, q_sum[:, :])
                cross_flip(l, i)
                unit(l, "A", 0, 1, 1, (tile_ready, tile_ready.at(l, "C", CROSS)), KD, h_rhs).then_inc(slot_done.sem, 1)
                cross_attend(l, i)
                unit(l, "A", 0, 2, 0, (ckv_copied, ckv_copied.at(l, "A", 0, 1)), 4, h_rhs, width=96, stop=False).then_inc(slot_done.sem, 1)
                unit(l, "A", 0, 3, 0, None, 4, lambda k: h_rhs(k + 4), width=96, start=False).then_inc(slot_done.sem, 1)
                unit(l, "B", 0, 0, 1, (ckv_copied, ckv_copied.at(l, "A", 0, 2)), KD, h_rhs).then_inc(slot_done.sem, 1)
                pe.wait_ge(ckv_squared.sem, ckv_squared.at(l, "A", 0, 2))
                sum_squares(l, "A", 1, ckv_sq[:, 0, :], ckv_sq[:, 1, :])
                unit(l, "B", 0, 1, 0, (mla_ready, mla_ready.at(l, "B", 0)), KD, h_rhs).then_inc(slot_done.sem, 1)
                pe.wait_ge(pair_lo.sem, pair_lo.at(l, "A", 0, QT + KVT))
                latent_units(l, 0, 2, (v_copied, v_copied.at(l, "B", 0, 1)), (diff_ready, diff_ready.at(l, "B", 0, 1)))
                unit(l, "B", 0, 3, 0, (kv_copied, kv_copied.at(l, "B", 0, 1)), KD, h_rhs).then_inc(slot_done.sem, 1)
                pe.wait_ge(ssq_read.sem, ssq_read.at(l, "B", 0))
                latent_scores(l, 0)
                flip_values(l, 0)
                with pe.Fori(0, HEADS // 2 - 1) as hp:
                    for e in range(2):
                        head(l, hp * 2 + e, hp * 2 + (e + 1))
                head(l, HEADS - 2, HEADS - 1)
                head(l, HEADS - 1, None)
                with pe.Fori(0, 2) as jj:
                    for e in range(4):
                        s = 5 * e
                        unit(l, "E", jj, s, 0, (om_used, om_used.at(l, "E", jj, e)), KD, h_rhs).then_inc(slot_done.sem, 1)
                        if e == 0:
                            pe.wait_ge(ssq_read.sem, ssq_read.at(l, "B", HEADS))
                        unit(l, "E", jj, s + 1, 1, (oc_used, oc_used.at(l, "E", jj, e)), KD, h_rhs).then_inc(slot_done.sem, 1)
                        unit(l, "E", jj, s + 2, 0, (gate_out, gate_out.at(l, "E", jj, 3 * e + 1)), KD, h_rhs).then_inc(slot_done.sem, 1)

                        def split(k):
                            if e == 0:
                                pe.wait_ge(outs_split.sem, outs_split.at(l, "E", 0, k + 1))
                        unit(l, "E", jj, s + 3, 1, (gate_out, gate_out.at(l, "E", jj, 3 * e + 2)), KD,
                             lambda k: (outs_hi[:, k, :], outs_lo[:, k, :]), before=split).then_inc(slot_done.sem, 1)
                        unit(l, "E", jj, s + 4, 0, (gate_out, gate_out.at(l, "E", jj, 3 * e + 3)), 4,
                             lambda k: (outs_hi[:, 8 + k, :], outs_lo[:, 8 + k, :]), before=lambda k: split(8 + k)).then_inc(om_done.sem, 1)
                        unit(l, "E", jj, s + 4, 1, (od_used, od_used.at(l, "E", jj, e + 1)), 4,
                             lambda k: (outs_hi[:, 12 + k, :], outs_lo[:, 12 + k, :]), first=4 * P,
                             before=lambda k: split(12 + k)).then_inc(slot_done.sem, 1)
                with pe.Fori(0, 2) as jj:
                    for e in range(4):
                        def mixed(k):
                            if e == 0 and k == 0:
                                pe.wait_ge(om_used.sem, om_used.at(l, "E", 2))
                            if e == 0:
                                pe.wait_ge(mix_split.sem, mix_split.at(l, "E", 0, k + 1))
                        unit(l, "F", jj, e, e % 2, (tile_ready, tile_ready.at(l, "F", jj, e - 1)), KD,
                             lambda k: (mix_hi[:, k, :], mix_lo[:, k, :]), before=mixed).then_inc(slot_done.sem, 1)
                unit(l, "G", 0, 0, 0, (tile_ready, tile_ready.at(l, "F", 1, 3)), KD, h_rhs,
                     before=lambda k: pe.wait_ge(pair_lo.sem, pair_lo.at(l, "F", 0, k + 1))).then_inc(slot_done.sem, 1)
                pe.wait_ge(sq_added.sem, sq_added.at(l, "H"))
                sum_squares(l, "N2", 0, x_sum[:, :])
                unit(l, "G", 0, 1, 1, (tile_ready, tile_ready.at(l, "H")), KD, h_rhs).then_inc(slot_done.sem, 1)

                def gate_up(t, e):
                    unit(l, "G", t, 2 * e, 0, (gate_read, gate_read.at(l, "G", t, e)), KD, h_rhs).then_inc(slot_done.sem, 1)
                    unit(l, "G", t, 2 * e + 1, 1, (hid_ready, hid_ready.at(l, "G", t, e)), KD, h_rhs).then_inc(slot_done.sem, 1)
                gate_up(0, 1)
                with pe.Fori(0, FT // 2 - 1) as t:
                    gate_up(t + 1, 0)
                    gate_up(t + 1, 1)
                with pe.Fori(0, 4) as jj:
                    for e in range(2):
                        k = 0
                        for c, n in enumerate(DOWN):
                            if e == 0 and c == 0:
                                pe.wait_ge(gate_read.sem, gate_read.at(l, "G", FT // 2))
                            if e == 0:
                                pe.wait_ge(hid_split.sem, hid_split.at(l, "G", 0, k + n))
                            unit(l, "H", jj, 4 * e + c, e, (tile_ready, tile_ready.at(l, "H", jj, e - 1)) if c == 0 else None, n, lambda q, k=k: (hid_hi[:, k + q, :], hid_lo[:, k + q, :]),
                                 start=c == 0, stop=c == 3).then_inc(slot_done.sem, 1)
                            k += n
            pe.wait_ge(sq_added.sem, sq_added.end(DEPTH))
            pe.wait_ge(ssq_read.sem, ssq_read.end(DEPTH))
            for t in range(NT):
                ins = mm(ssq[:, t:t + 1], x_sum[:, t * P:(t + 1) * P], ones[:, 0:1], start=True, stop=True)
            ins.then_inc(ssq_full.sem, 1)
            for n in range(2 * NT):
                half, t = n // NT, n % NT
                pe.wait_ge(y_ready, 4 * (half + 1))
                if n >= 2:
                    pe.wait_ge(y_copied[n % 2], n // 2)
                for k in range(4):
                    ins = nc.tensor.transpose(flip[n % 2][:, k * P:(k + 1) * P], y_T[:, 4 * half + k, t * P:(t + 1) * P], ident[:, :])
                ins.then_inc(y_flipped, 1)

        @block.scalar
        def _(act):
            sc = nc.scalar
            act.dma_start(pos_i[:, :], positions[0, :].rearrange("(t p) -> p t", p=P),
                          allow_slow_non_contiguous=True).then_inc(in_pos, 16)
            act.wait_ge(const_ready, 1)
            for l in range(1, DEPTH):
                load_gains(act, l)
            act.dma_start(lam_in[:, :, :, :].rearrange("p l a d -> p (l a d)"),
                          diff_lambda.rearrange("l a d -> (l a d)").partition_broadcast(P)).then_inc(in_lam, 16)
            act.dma_start(mem_in[:, :, :], mem[0, :, :].rearrange("(t p) d -> p t d", p=P)).then_inc(in_mem, 16)
            start_counts(act, "act")

            def copy(out, in_):
                return sc.activation(out, in_, ACT.Copy)

            def split_ahead(l, stage, step, s):
                n = slot_hi.index(l, stage, step, s)
                act.wait_ge(slot_done.sem, slot_done.at(l, stage, step, s))
                q = s + AHEAD
                act.wait_ge(raw_full[q % 2], n * 16 + (AHEAD * 16 + (16 if q % 2 else 32)))
                copy(w_hi[q % 4][:, :], raw[q % 2][:, :]).then_inc(slot_hi.sem, 1)

            def exps(l, stage, step, n, k, p, scale, banks=score):
                _, bias, total, _ = stat[k]
                act.wait_ge(bias_ready.sem, bias_ready.at(l, stage, step, n + 1))
                for t in range(NT):
                    if stage == "C":
                        src, dst = score[t // 2][:, (t % 2) * MEM:(t % 2 + 1) * MEM], p[:, t * MEM:(t + 1) * MEM]
                    else:
                        b, c = {3: (0, 0), 2: (1, 0), 0: (1, 384), 1: (2, 0)}[t]
                        src, dst = banks[b][:, c:c + (t + 1) * P], p[:, q_off(t):q_off(t) + (t + 1) * P]
                    sc.activation(dst, src, ACT.Exp, bias=bias[:, t:t + 1], scale=scale,
                                  accum_out=total[:, t:t + 1]).then_inc(exp_done.sem, 1)

            def flip_high(l, stage, step, k, dst, src):
                act.wait_ge(flip_full.sem, flip_full.at(l, stage, step, k + 1))
                copy(dst, src).then_inc(flip_hi.sem, 1)

            def causal_high(l, h, n, part):
                if part == 0:
                    act.wait_ge(att_full.sem, att_full.at(l, "B", h, n))
                    flip_high(l, "B", h, 2 + 3 * n, pt_hi[:, 0:512], flip[n][:, :])
                    flip_high(l, "B", h, 3 + 3 * n, pt_hi[:, 512:896], flip[1 - n][:, 0:384])
                else:
                    flip_high(l, "B", h, 4 + 3 * n, pt_hi[:, 896:1280], flip[n][:, 0:384])

            def values_high(l, h):
                act.wait_ge(att_full.sem, att_full.at(l, "B", h))
                flip_high(l, "B", h, 0, v_hi[:, :, :].rearrange("p j d -> p (j d)"), flip[0][:, :])
                flip_high(l, "B", h, 1, mv_hi[:, :, :].rearrange("p j d -> p (j d)"), flip[1][:, :])

            def out_kv(l, h):
                act.wait_ge(slot_done.sem, slot_done.at(l, "B", h, 2))
                copy(kvT[:, :], proj[0][:, :]).then_inc(kv_copied.sem, 1)

            def squares(l, stage, step, k, src):
                act.wait_ge(tile_ready.sem, tile_ready.at(l, stage, step, k + 1))
                act.wait_ge(sq_added.sem, sq_added.at(l, stage, step, k))
                scale = (Q_LORA if stage == "C" else D) ** -0.5
                sc.activation(square[:, :], src, ACT.Square, scale=scale).then_inc(sq_done.sem, 1)

            def rms(l, stage, step, k, sums=ssq, r=rstd):
                act.wait_ge(ssq_full.sem, ssq_full.at(l, stage, step, k + 1))
                sc.activation(r[:, :], sums[:, :], ACT.Ln, bias=eps[:, 0:1]).then_inc(ssq_read.sem, 1)
                act.wait_ge(ssq_read.sem, ssq_read.at(l, stage, step, k + 1))
                sc.activation(r[:, :], r[:, :], ACT.Exp, scale=-0.5).then_inc(rms_ready.sem, 1)

            def pair_high(l, stage, k, dst, step=0):
                act.wait_ge(pair_ready.sem, pair_ready.at(l, stage, step, k + 1))
                copy(dst, pair[:, k % 2, :]).then_inc(pair_hi.sem, 1)

            def query_high(l, h):
                act.wait_ge(diff_ready.sem, diff_ready.at(l, "B", h, 1))
                copy(q1[0:64, :], mid[0:64, :]).then_inc(qk_hi.sem, 1)
                copy(q2[64:P, :], mid[64:P, :]).then_inc(qk_hi.sem, 1)

            def key_high(l, h):
                act.wait_ge(diff_ready.sem, diff_ready.at(l, "B", h, 2))
                copy(k1[0:64, :], mid[0:64, :]).then_inc(qk_hi.sem, 1)
                copy(k2[64:P, :], mid[64:P, :]).then_inc(qk_hi.sem, 1)
                copy(k1[64:P, :], mid[0:64, :]).then_inc(qk_hi.sem, 1)
                copy(k2[0:64, :], mid[64:P, :]).then_inc(qk_hi.sem, 1)

            def head(l, h, n, e):
                exps(l, "B", h, 0, "m", p_a, MLA_SCALE)
                if n is not None:
                    split_ahead(l, "B", n, 0)
                if n is not None:
                    causal_high(l, h, 0, 0)
                act.wait_ge(flip_full.sem, flip_full.at(l, "B", h))
                exps(l, "B", h, 1, "d1", p_b, DIFF_SCALE, score if n is not None else last_score)
                if n is None:
                    causal_high(l, h, 0, 0)
                if n is not None:
                    split_ahead(l, "B", n, 1)
                if n is None:
                    for k in range(2):
                        copy(outs_hi[:, k, :], outs[:, k, :]).then_inc(outs_split_hi.sem, 1)
                causal_high(l, h, 0, 1)
                if n is not None:
                    out_kv(l, n)
                act.wait_ge(flip_full.sem, flip_full.at(l, "B", h, 5))
                exps(l, "B", h, 2, "d2", p_a, DIFF_SCALE)
                if n is not None:
                    split_ahead(l, "B", n, 2)
                if n is None:
                    for k in range(2, EARLY):
                        copy(outs_hi[:, k, :], outs[:, k, :]).then_inc(outs_split_hi.sem, 1)
                act.wait_ge(att_full.sem, att_full.at(l, "B", h, 1))
                o = outs[64 * e:64 * e + 64, 8 + h // 2, :] if isinstance(h, int) else \
                    outs[64 * e:64 * e + 64, bass.ds(n_pair(h) + 8, 1), :].rearrange("p a n -> p (a n)")
                copy(o, att[64:128, :]).then_inc(att_read.sem, 1)
                causal_high(l, h, 1, 0)
                if n is not None:
                    split_ahead(l, "B", n, 3)
                    query_high(l, n)
                causal_high(l, h, 1, 1)
                act.wait_ge(att_full.sem, att_full.at(l, "B", h, 2))
                act.wait_ge(ssq_full.sem, ssq_full.at(l, "B", h))
                sc.activation(a_sq[:, :], att[:, :], ACT.Square, scale=float(P) ** -0.5).then_inc(a_squared.sem, 1)
                if n is not None:
                    key_high(l, n)
                    values_high(l, n)
                act.wait_ge(att_read.sem, att_read.at(l, "B", h))
                rms(l, "B", h, 0, proj[1])

            pair_of = [None]

            def n_pair(h):
                return pair_of[0]

            def cross_step(l, i):
                exps(l, "C", i, 0, "m", p_a, CROSS_SCALE)

            def cross_high(l, i):
                act.wait_ge(att_full.sem, att_full.at(l, "C", i))
                for j in range(NM):
                    flip_high(l, "C", i, 2 + j, pt_hi[:, j * SEQ:(j + 1) * SEQ], flip[j][:, :])

            def memory_high(l, i):
                act.wait_ge(att_full.sem, att_full.at(l, "C", i))
                for j in range(NM):
                    flip_high(l, "C", i, j, v_hi[:, j, :], flip[j][:, 0:P])

            def out_cross(l, i, s, b, dst, cols):
                act.wait_ge(slot_done.sem, slot_done.at(l, "C", i, s + 1))
                copy(dst, proj[b][:, 0:cols]).then_inc(kv_copied.sem, 1)

            act.wait_ge(const_ready, 2)
            act.wait_ge(pre_vec, 1)
            sc.activation(sin_t[:, :, :], ang[:, :, :], ACT.Sin)
            sc.activation(half_t[:, :, :], ang[:, :, :], ACT.Sin, scale=0.5).then_inc(pre_act, 1)
            act.wait_ge(pre_vec, 2)
            sc.preload_act_table_set(LN_EXP)
            sc.activation(lam_exp[:, :], lam_sum[:, :], ACT.Exp).then_inc(pre_act, 1)

            def first_slot(s):
                act.wait_ge(raw_full[s % 2], 32 * (s // 2 + 1))
                copy(w_hi[s][:, :], raw[s % 2][:, :]).then_inc(slot_hi.sem, 1)
            for k in range(KD):
                act.wait_ge(pre_full, k + 2)
                copy(xT[:, k, :], flip[(1 + k) % 2][:, :]).then_inc(x_copied, 1)
                act.wait_ge(x_copied, k + 1)
                if k >= 2:
                    act.wait_ge(sq_added.sem, k)
                sc.activation(x_sq[:, k % 2, :], xT[:, k, :], ACT.Square, scale=float(D) ** -0.5).then_inc(sq_done.sem, 1)
                act.wait_ge(pair_ready.sem, k + 2)
                copy(h_hi[:, k, :], pair[:, k % 2, :]).then_inc(pair_hi.sem, 1)
                if k == 2:
                    act.wait_ge(in_mem, 16)
                if k in (2, 3):
                    t = k - 2
                    sc.activation(mem_sq[:, t, :], mem_in[:, t, :], ACT.Square, scale=float(D) ** -0.5,
                                  accum_out=mem_ss[:, t:t + 1]).then_inc(pre_act, 1)
                if k == 4:
                    act.wait_ge(pre_act, NM + 2)
                    sc.activation(mem_rstd[:, :], mem_ss[:, :], ACT.Ln, bias=eps[:, 0:1]).then_inc(pre_act, 1)
                    act.wait_ge(pre_act, NM + 3)
                    sc.activation(mem_rstd[:, :], mem_rstd[:, :], ACT.Exp, scale=-0.5).then_inc(pre_act, 1)
            for s in range(AHEAD + 1):
                first_slot(s)
            act.wait_ge(pre_read, 5 + KD // 2)
            act.dma_start(mem_scratch[:, :, :], mem_n[:, :, :]).then_inc(mem_stored, 16)
            act.dma_start(table_scratch[:, :, :], tables_d[:, :, :]).then_inc(mem_stored, 16)

            act.wait_ge(x_copied, KD)
            with act.Fori(0, DEPTH) as l:
                act.wait_ge(slot_done.sem, slot_done.at(l, "C"))
                act.wait_ge(tile_ready.sem, tile_ready.at(l, "C"))
                act.dma_start(x_scratch[:, :, :], xT[:, :, :]).then_inc(x_stored.sem, 16)
                act.wait_ge(mem_loaded.sem, mem_loaded.at(l, "H"))
                for k in range(KD):
                    sc.activation(mem_hi[:, k, :], mem_n[:, k, :], ACT.Copy, scale=gains[:, bass.ds(l * G_N + (G_MEM + k), 1)]).then_inc(memh_hi.sem, 1)
                rms(l, "N1", 0, 0, r=rstd_x)
                split_ahead(l, "C", 0, 1)
                split_ahead(l, "C", 0, 2)
                squares(l, "C", 0, 0, cq_raw[:, 0, :])
                out_cross(l, 0, 2, 0, kT[:, 0:MEM], MEM)
                act.wait_ge(mem_stored, 32)
                out_cross(l, 0, 3, 1, vT[:, 0:MEM], MEM)
                split_ahead(l, "C", 0, 3)
                memory_high(l, 0)
                with act.Fori(0, CROSS - 1) as i:
                    cross_step(l, i)
                    split_ahead(l, "C", i + 1, 0)
                    split_ahead(l, "C", i + 1, 1)
                    out_cross(l, i + 1, 1, 1, kT[:, 0:MEM], MEM)
                    cross_high(l, i)
                    split_ahead(l, "C", i + 1, 2)
                    out_cross(l, i + 1, 2, 0, vT[:, 0:MEM], MEM)
                    split_ahead(l, "C", i + 1, 3)
                    squares(l, "C", i + 1, 0, cq_raw[:, bass.ds(i + 1, 1), :].rearrange("p a n -> p (a n)"))
                    memory_high(l, i + 1)
                i = CROSS - 1
                cross_step(l, i)
                split_ahead(l, "A", 0, 0)
                for j in range(KVT):
                    act.wait_ge(ckv_copied.sem, ckv_copied.at(l, "A", 0, j + 1))
                    sc.activation(ckv_sq[:, j, :], ckv_raw[:, j, :], ACT.Square, scale=float(KV_LORA) ** -0.5).then_inc(ckv_squared.sem, 1)
                    if j == 0:
                        cross_high(l, i)
                        rms(l, "A", 0, 0)
                        split_ahead(l, "A", 0, 1)
                        for k in range(QT):
                            pair_high(l, "A", k, cq_hi[:, k, :])
                        split_ahead(l, "A", 0, 2)
                split_ahead(l, "A", 0, 3)
                split_ahead(l, "B", 0, 0)
                rms(l, "A", 0, 1)
                for k in range(KVT):
                    pair_high(l, "A", QT + k, ckv_hi[:, k, :])
                split_ahead(l, "B", 0, 1)
                act.wait_ge(x_stored.sem, x_stored.at(l, "N1", 0, 16))
                split_ahead(l, "B", 0, 2)
                query_high(l, 0)
                act.wait_ge(slot_done.sem, slot_done.at(l, "B", 0, 3))
                copy(kvT[:, :], proj[0][:, :]).then_inc(kv_copied.sem, 1)
                split_ahead(l, "B", 0, 3)
                key_high(l, 0)
                values_high(l, 0)
                with act.Fori(0, HEADS // 2 - 1) as hp:
                    pair_of[0] = hp
                    for e in range(2):
                        head(l, hp * 2 + e, hp * 2 + (e + 1), e)
                head(l, HEADS - 2, HEADS - 1, 0)
                head(l, HEADS - 1, None, 1)
                sc.activation(warm[:, :], eps[:, :], ACT.Sigmoid)
                act.wait_ge(att_read.sem, att_read.at(l, "B", HEADS))
                act.dma_start(xT[:, :, :], x_scratch[:, :, :]).then_inc(x_loaded.sem, 16)
                split_ahead(l, "E", 0, 0)
                for k in range(EARLY, 16):
                    copy(outs_hi[:, k, :], outs[:, k, :]).then_inc(outs_split_hi.sem, 1)
                with act.Fori(0, 2) as jj:
                    for e in range(4):
                        for g in range(3):
                            s = 5 * e + g
                            if s:
                                split_ahead(l, "E", jj, s)
                            act.wait_ge(gate_out.sem, gate_out.at(l, "E", jj, 3 * e + g + 1))
                            sc.activation(sig[:, g, :], sig[:, g, :], ACT.Sigmoid).then_inc(sig_ready.sem, 1)
                        split_ahead(l, "E", jj, 5 * e + 3)
                        split_ahead(l, "E", jj, 5 * e + 4)
                        if e == 3:
                            split_ahead(l, "E", jj, 20)
                        act.wait_ge(mix_ready.sem, mix_ready.at(l, "E", jj, e + 1))
                        copy(mix_hi[:, bass.ds(jj * 4 + e, 1), :].rearrange("p a n -> p (a n)"), mix[:, :]).then_inc(mix_split_hi.sem, 1)
                sc.preload_act_table_set(LN_EXP)
                with act.Fori(0, 2) as jj:
                    for e in range(4):
                        if e:
                            split_ahead(l, "F", jj, e)
                        pair_high(l, "F", e, h_hi[:, bass.ds(jj * 4 + e, 1), :].rearrange("p a n -> p (a n)"), jj)
                        squares(l, "F", jj, e, xT[:, bass.ds(jj * 4 + e, 1), :].rearrange("p a n -> p (a n)"))
                        if e == 3:
                            split_ahead(l, "F", jj, 4)
                rms(l, "N2", 0, 0)
                sc.activation(warm[:, :], eps[:, :], ACT.Sigmoid)
                def gate_up(t):
                    for e in range(2):
                        if e:
                            split_ahead(l, "G", t, 2)
                        act.wait_ge(gate_read.sem, gate_read.at(l, "G", t, e + 1))
                        act.wait_ge(gate_used.sem, gate_used.at(l, "G", t))
                        sc.activation(sig_f[:, e, :], gate_n[:, :], ACT.Sigmoid).then_inc(silu_sig.sem, 1)
                        split_ahead(l, "G", t, 2 * e + 1)
                        act.wait_ge(hid_ready.sem, hid_ready.at(l, "G", t, e + 1))
                        copy(hid_hi[:, bass.ds(t * 2 + e, 1), :].rearrange("p a n -> p (a n)"), hid[:, e, :]).then_inc(hid_split_hi.sem, 1)
                    split_ahead(l, "G", t, 4)
                gate_up(0)
                with act.Fori(0, FT // 2 - 1) as t:
                    gate_up(t + 1)
                sc.preload_act_table_set(LN_EXP)
                act.wait_ge(hid_split.sem, hid_split.at(l, "G", FT // 2))
                act.dma_start(mem_n[:, :, :], mem_scratch[:, :, :]).then_inc(mem_loaded.sem, 16)
                act.dma_start(tables_d[:, :, :], table_scratch[:, :, :]).then_inc(mem_loaded.sem, 16)
                with act.Fori(0, 4) as jj:
                    for e in range(2):
                        for c in range(4):
                            if e or c:
                                split_ahead(l, "H", jj, 4 * e + c)
                        pair_high(l, "H", e, h_hi[:, bass.ds(jj * 2 + e, 1), :].rearrange("p a n -> p (a n)"), jj)
                        squares(l, "H", jj, e, xT[:, bass.ds(jj * 2 + e, 1), :].rearrange("p a n -> p (a n)"))
                        if e:
                            split_ahead(l, "H", jj, 8)
            act.wait_ge(mem_loaded.sem, mem_loaded.end(DEPTH))
            act.wait_ge(ssq_full.sem, ssq_full.end(DEPTH) + 1)
            sc.activation(rstd[:, 0:NT], ssq[:, 0:NT], ACT.Ln, bias=eps[:, 0:1]).then_inc(ssq_read.sem, 1)
            act.wait_ge(ssq_read.sem, ssq_read.end(DEPTH) + 1)
            sc.activation(rstd[:, 0:NT], rstd[:, 0:NT], ACT.Exp, scale=-0.5).then_inc(rms_ready.sem, 1)
            act.wait_ge(y_ready, KD + 1)
            for n in range(1, 2 * NT, 2):
                half, t = n // NT, n % NT
                act.wait_ge(y_flipped, n + 1)
                sc.activation(y_out[:, t, half * 512:(half + 1) * 512], flip[1][:, :], ACT.Copy, scale=rstd[:, t:t + 1]).then_inc(y_copied[1], 1)

        @block.vector
        def _(ve):
            v = nc.vector
            start_counts(ve, "ve")
            state = {"origin": 0, "n": 0}

            def begin(l, stage, step=0):
                state["origin"], state["n"] = vec_step.at(l, stage, step), 0

            def end(stage):
                assert state["n"] == vec_step.start[stage][1], (stage, state["n"])

            def chain(ins):
                state["n"] += 1
                ins.then_inc(vec_step.sem, 1)
                ve.wait_ge(vec_step.sem, state["origin"] + state["n"])

            def one(t, i):
                return t[:, bass.ds(i, 1), :].rearrange("p a n -> p (a n)") if not isinstance(i, int) else t[:, i, :]

            SHUF_D = [(i + 8) % 16 if i < 16 else i for i in range(32)]
            SHUF_M = [(i + 16) % 32 for i in range(32)]

            def rope(dst, src, rows, cos, sin, mask, last):
                ve.wait_ge(last[0].sem, last[1])
                v.tensor_tensor(mid[rows, :], src[rows, :], cos[rows, :], ALU.mult)
                chain(v.stream_shuffle(rot[rows, :], src[rows, :], mask))
                chain(v.tensor_tensor(rot[rows, :], rot[rows, :], sin[rows, :], ALU.mult))
                return v.tensor_tensor(dst[rows, :], mid[rows, :], rot[rows, :], ALU.add)

            def query_low(l, h):
                for k, (q, hi, lo) in enumerate(((q1, slice(0, 64), slice(64, P)), (q2, slice(64, P), slice(0, 64)))):
                    ve.wait_ge(qk_hi.sem, qk_hi.at(l, "B", h, k + 1))
                    ins = v.tensor_tensor(q[lo, :], mid[hi, :], q[hi, :].bitcast(F32), ALU.subtract)
                ins.then_inc(qk_split.sem, 1)

            def key_low(l, h):
                for n, (k, rows) in enumerate(((k1, slice(0, 64)), (k2, slice(64, P)))):
                    ve.wait_ge(qk_hi.sem, qk_hi.at(l, "B", h, 3 if n == 0 else 6))
                    ins = v.tensor_tensor(k_lo[rows, :], mid[rows, :], k[rows, :].bitcast(F32), ALU.subtract)
                ins.then_inc(qk_split.sem, 1)

            def maxima(l, stage, step, n, k, scale, banks=score):
                top, bias, _, _ = stat[k]
                for t in (range(NT) if stage == "C" else (3, 2, 0, 1)):
                    if stage == "C":
                        full, src = t // 2 + 1, score[t // 2][:, (t % 2) * MEM:(t % 2 + 1) * MEM]
                    else:
                        b, c = {3: (0, 0), 2: (1, 0), 0: (1, 384), 1: (2, 0)}[t]
                        full, src = b + 1, banks[b][:, c:c + (t + 1) * P]
                    if stage == "C" and t % 2 == 0 or stage == "B" and t != 0:
                        ve.wait_ge(score_full.sem, score_full.at(l, stage, step, 3 * n + full))
                    ins = v.tensor_reduce(top[:, t:t + 1], src, AX.X, ALU.max)
                chain(ins)
                v.tensor_scalar(bias[:, :], top[:, :], -scale, None, ALU.mult).then_inc(bias_ready.sem, 1)

            def invert(l, stage, step, n, k):
                _, _, total, inv = stat[k]
                ve.wait_ge(exp_done.sem, exp_done.at(l, stage, step, 4 * (n + 1)))
                chain(v.reciprocal(inv[:, :], total[:, :]))

            def normalise(p, inv, off, size):
                for t in range(NT):
                    s = p[:, off(t):off(t) + size(t)]
                    ins = v.tensor_scalar(s, s, inv[:, t:t + 1], None, ALU.mult)
                return ins

            def flip_low(l, stage, step, k, dst, src, hi):
                ve.wait_ge(flip_hi.sem, flip_hi.at(l, stage, step, k + 1))
                v.tensor_tensor(dst, src, hi.bitcast(F32), ALU.subtract).then_inc(flip_read.sem, 1)

            def causal_low(l, h, n, part):
                if part == 0:
                    flip_low(l, "B", h, 2 + 3 * n, pt_lo[:, 0:512], flip[n][:, :], pt_hi[:, 0:512])
                    flip_low(l, "B", h, 3 + 3 * n, pt_lo[:, 512:896], flip[1 - n][:, 0:384], pt_hi[:, 512:896])
                else:
                    flip_low(l, "B", h, 4 + 3 * n, pt_lo[:, 896:1280], flip[n][:, 0:384], pt_hi[:, 896:1280])

            def values_low(l, h):
                for k, (lo, hi) in enumerate(((v_lo, v_hi), (mv_lo, mv_hi))):
                    flip_low(l, "B", h, k, lo[:, :, :].rearrange("p j d -> p (j d)"), flip[k][:, :],
                             hi[:, :, :].rearrange("p j d -> p (j d)"))

            def out_latent(l, h, last=None):
                ve.wait_ge(mq_done.sem, mq_done.at(l, "B", h, 1))
                last = last or (qk_split, qk_split.at(l, "B", h))
                rope(mqT, proj[1], slice(0, 96), cos_m, sin_m, SHUF_M, last).then_inc(mla_ready.sem, 1)
                ve.wait_ge(kv_copied.sem, kv_copied.at(l, "B", h, 1))
                v.tensor_copy(mkT[0:64, :], kvT[0:64, :]).then_inc(mla_ready.sem, 1)

            def out_qk(l, h, s, b, last=None):
                ve.wait_ge(slot_done.sem, slot_done.at(l, "B", h, s + 1))
                last = last or ((qk_split, qk_split.at(l, "B", h, 1)) if s == 3 else (mla_ready, mla_ready.at(l, "B", h, 1)))
                rope(mid, proj[b], slice(0, P), cos_d, sin_d, SHUF_D, last).then_inc(diff_ready.sem, 1)

            def rms(l, stage, k):
                ve.wait_ge(rms_ready.sem, rms_ready.at(l, stage, 0, k + 1))

            def newton(r, cols=SEQ):
                w = square[:, 0:cols]
                chain(v.tensor_tensor(w, r[:, 0:cols], r[:, 0:cols], ALU.mult))
                chain(v.scalar_tensor_tensor(w, ssq[:, 0:cols], EPS, w, ALU.add, ALU.mult))
                chain(v.tensor_scalar(w, w, -0.5, 1.5, ALU.mult, ALU.add))
                return v.tensor_tensor(r[:, 0:cols], r[:, 0:cols], w, ALU.mult)

            def norm(l, stage, k0, src, gain, n, hi, lo):
                def low(k):
                    ve.wait_ge(pair_hi.sem, pair_hi.at(l, stage, 0, k0 + k + 1))
                    v.tensor_tensor(lo[:, k, :], pair[:, (k0 + k) % 2, :], hi[:, k, :].bitcast(F32), ALU.subtract).then_inc(pair_lo.sem, 1)
                for k in range(n):
                    if k >= 2:
                        ve.wait_ge(pair_lo.sem, pair_lo.at(l, stage, 0, k0 + k - 1))
                    v.scalar_tensor_tensor(pair[:, (k0 + k) % 2, :], src[:, k, :], gl[:, gain + k:gain + k + 1], rstd[:, :],
                                           ALU.mult, ALU.mult).then_inc(pair_ready.sem, 1)
                    if k:
                        low(k - 1)
                low(n - 1)

            def add_square(l, stage, step, k, acc):
                ve.wait_ge(sq_done.sem, sq_done.at(l, stage, step, k + 1))
                v.tensor_tensor(acc[:, :], acc[:, :], square[:, :], ALU.add).then_inc(sq_added.sem, 1)
                ve.wait_ge(sq_added.sem, sq_added.at(l, stage, step, k + 1))

            def outs_low(l, k):
                ve.wait_ge(outs_split_hi.sem, outs_split_hi.at(l, "E", 0, k + 1))
                v.tensor_tensor(outs_lo[:, k, :], outs[:, k, :], outs_hi[:, k, :].bitcast(F32), ALU.subtract).then_inc(outs_split.sem, 1)

            def head(l, h, n):
                begin(l, "B" if n is not None else "L", h if n is not None else 0)
                invert(l, "B", h, 0, "m")
                normalise(p_a, stat["m"][3], q_off, lambda t: (t + 1) * P).then_inc(prob_ready.sem, 1)
                if n is not None:
                    out_v(l, n)
                maxima(l, "B", h, 1, "d1", DIFF_SCALE, score if n is not None else last_score)
                if n is None:
                    maxima(l, "B", h, 2, "d2", DIFF_SCALE)
                causal_low(l, h, 0, 0)
                if n is not None:
                    out_latent(l, n)
                causal_low(l, h, 0, 1)
                invert(l, "B", h, 1, "d1")
                chain(normalise(p_b, stat["d1"][3], q_off, lambda t: (t + 1) * P))
                if n is not None:
                    maxima(l, "B", h, 2, "d2", DIFF_SCALE)
                invert(l, "B", h, 2, "d2")
                chain(v.tensor_scalar(lam_scale[:, :], stat["d2"][3][:, :], gl[:, G_LAM:G_LAM + 1], None, ALU.mult))
                for t in range(NT):
                    s = slice(q_off(t), q_off(t) + (t + 1) * P)
                    ins = v.scalar_tensor_tensor(p_b[:, s], p_a[:, s], lam_scale[:, t:t + 1], p_b[:, s], ALU.mult, ALU.add)
                ins.then_inc(prob_ready.sem, 1)
                if n is not None:
                    out_qk(l, n, 2, 1)
                causal_low(l, h, 1, 0)
                causal_low(l, h, 1, 1)
                if n is not None:
                    query_low(l, n)
                    out_qk(l, n, 3, 0)
                    if n is HEADS - 1:
                        key_low(l, n)
                    maxima(l, "B", n, 0, "m", MLA_SCALE)
                    if n is not HEADS - 1:
                        key_low(l, n)
                    values_low(l, n)
                if n is None:
                    for k in range(EARLY):
                        outs_low(l, k)
                ve.wait_ge(rms_ready.sem, rms_ready.at(l, "B", h, 1))
                v.scalar_tensor_tensor(one(outs, h), att[:, :], gl[:, G_SUB:G_SUB + 1], rstd[:, :], ALU.mult, ALU.mult).then_inc(att_read.sem, 1)

                end("B" if n is not None else "L")

            def cross_prob(l, i):
                maxima(l, "C", i, 0, "m", CROSS_SCALE)
                invert(l, "C", i, 0, "m")
                normalise(p_a, stat["m"][3], lambda t: t * MEM, lambda t: MEM).then_inc(prob_ready.sem, 1)

            def cross_low(l, i):
                for j in range(NM):
                    s = slice(j * SEQ, (j + 1) * SEQ)
                    flip_low(l, "C", i, 2 + j, pt_lo[:, s], flip[j][:, :], pt_hi[:, s])

            def memory_low(l, i):
                for j in range(NM):
                    flip_low(l, "C", i, j, v_lo[:, j, :], flip[j][:, 0:P], v_hi[:, j, :])

            def cross_out(l, i):
                ve.wait_ge(att_full.sem, att_full.at(l, "C", i, 1))
                v.tensor_copy(one(outs, i + 12), att[:, :]).then_inc(att_read.sem, 1)

            def out_xq(l, i):
                ve.wait_ge(slot_done.sem, slot_done.at(l, "C", i, 1))
                v.tensor_tensor(qT[:, :], proj[0][:, :], rstd_x[:, :], ALU.mult).then_inc(xq_copied.sem, 1)

            def out_v(l, h, b=0):
                ve.wait_ge(slot_done.sem, slot_done.at(l, "B", h, 1))
                v.tensor_tensor(vT[:, :], proj[b][:, :], rstd_x[:, :], ALU.mult).then_inc(v_copied.sem, 1)

            def out_cq(l, i, done=4):
                ve.wait_ge(slot_done.sem, slot_done.at(l, "C", i, done))
                v.tensor_tensor(one(cq_raw, i), proj[1][:, :], rstd_x[:, :], ALU.mult).then_inc(tile_ready.sem, 1)
                add_square(l, "C", i, 0, q_sum)

            def out_residual(l, stage, step, k, s, b, tile, gain):
                ve.wait_ge(slot_done.sem, slot_done.at(l, stage, step, s))
                v.tensor_tensor(one(xT, tile), one(xT, tile), proj[b][:, :], ALU.add).then_inc(tile_ready.sem, 1)
                ve.wait_ge(tile_ready.sem, tile_ready.at(l, stage, step, k + 1))
                ve.wait_ge(pair_lo.sem, pair_lo.at(l, stage, step, k - 1))
                v.tensor_scalar(pair[:, k % 2, :], one(xT, tile), gains[:, bass.ds(tile + gain, 1)], None, ALU.mult).then_inc(pair_ready.sem, 1)
                ve.wait_ge(pair_hi.sem, pair_hi.at(l, stage, step, k + 1))
                v.tensor_tensor(one(h_lo, tile), pair[:, k % 2, :], one(h_hi, tile).bitcast(F32), ALU.subtract).then_inc(pair_lo.sem, 1)
                add_square(l, stage, step, k, x_sum)

            pre = [0]

            def now(ins):
                pre[0] += 1
                ins.then_inc(pre_chain, 1)
                ve.wait_ge(pre_chain, pre[0])

            def fill(n, dst, cols=512):
                ve.wait_ge(pre_full, n + 1)
                v.tensor_copy(dst, flip[n % 2][:, 0:cols]).then_inc(pre_read, 1)

            ve.wait_ge(in_pos, 16)
            now(v.tensor_copy(pos_f[:, :], pos_i[:, :]))
            ve.wait_ge(const_ready, 2)
            for t in range(NT):
                ins = v.tensor_scalar(ang[:, t, :], freq[:, :], pos_f[:, t:t + 1], None, ALU.mult)
            now(ins)
            magic = 1.5 * 2 ** 23
            now(v.tensor_scalar(turns[:, :, :], ang[:, :, :], 1 / (2 * math.pi), magic, ALU.mult, ALU.add))
            now(v.tensor_scalar(turns[:, :, :], turns[:, :, :], -magic, None, ALU.add))
            c1 = 6.28125
            c2 = float(np.float32(math.floor((2 * math.pi - c1) * 2 ** 20) / 2 ** 20))
            c3 = 2 * math.pi - c1 - c2
            for c in (c1, c2, c3):
                now(v.scalar_tensor_tensor(ang[:, :, :], turns[:, :, :], -c, ang[:, :, :], ALU.mult, ALU.add))
            v.tensor_scalar(ang[:, :, :], ang[:, :, :], 3.1415925, -3.1415925, ALU.min, ALU.max).then_inc(pre_vec, 1)
            ve.wait_ge(in_lam, 16)
            pairs = lam_in[:, :, :, :].rearrange("p l (a b) d -> p (l a) b d", b=2)
            now(v.tensor_tensor(lam_prod[:, :, :], pairs[:, :, 0, :], pairs[:, :, 1, :], ALU.mult))
            v.tensor_reduce(lam_sum[:, :], lam_prod[:, :, :], AX.X, ALU.add).then_inc(pre_vec, 1)
            ve.wait_ge(pre_act, 1)
            now(v.tensor_tensor(cos_t[:, :, :], half_t[:, :, :], half_t[:, :, :], ALU.mult))
            v.tensor_scalar(neg_t[:, :, :], sin_t[:, :, :], -1.0, None, ALU.mult)
            now(v.tensor_scalar(cos_t[:, :, :], cos_t[:, :, :], -2.0, 1.0, ALU.mult, ALU.add))
            for c0, half, f0, kind in ((0, 8, 0, 0), (64, 8, 0, 0), (64, 16, 8, 2)):
                f = slice(f0, f0 + half)
                a, b = slice(c0, c0 + half), slice(c0 + half, c0 + 2 * half)
                v.tensor_copy(rope_t[:, kind, :, a], cos_t[:, :, f])
                v.tensor_copy(rope_t[:, kind, :, b], cos_t[:, :, f])
                v.tensor_copy(rope_t[:, kind + 1, :, a], neg_t[:, :, f])
                ins = v.tensor_copy(rope_t[:, kind + 1, :, b], sin_t[:, :, f])
            ins.then_inc(rope_ready, 1)
            ve.wait_ge(pre_full, 1)
            v.tensor_copy(gains[:, :], flip[0][:, 0:P]).then_inc(pre_read, 1)
            ve.wait_ge(pre_read, 1)

            def x_low(k):
                ve.wait_ge(pair_hi.sem, k + 2)
                v.tensor_tensor(h_lo[:, k, :], pair[:, k % 2, :], h_hi[:, k, :].bitcast(F32), ALU.subtract).then_inc(pair_lo.sem, 1)
                ve.wait_ge(sq_done.sem, k + 2)
                ve.wait_ge(sq_added.sem, k + 1)
                v.tensor_tensor(x_sum[:, :], x_sum[:, :], x_sq[:, k % 2, :], ALU.add).then_inc(sq_added.sem, 1)
            for k in range(KD):
                ve.wait_ge(x_copied, k + 1)
                if k >= 2:
                    ve.wait_ge(pair_lo.sem, k)
                v.tensor_scalar(pair[:, k % 2, :], xT[:, k, :], gains[:, k:k + 1], None, ALU.mult).then_inc(pair_ready.sem, 1)
                if k:
                    x_low(k - 1)
            x_low(KD - 1)
            ve.wait_ge(pre_act, NM + 4)
            for t in range(NM):
                v.tensor_scalar(mem_in[:, t, :], mem_in[:, t, :], mem_rstd[:, t:t + 1], None, ALU.mult).then_inc(mem_scaled, 1)
            for f in range(KD // 2):
                fill(1 + KD + f, mem_n[:, 2 * f:2 * f + 2, :].rearrange("p k n -> p (k n)"))
            ve.wait_ge(pre_act, 2)
            for l in range(DEPTH):
                lam_init = 0.8 - 0.6 * math.exp(-0.3 * l)
                sub = gains[:, l * G_N + G_SUB:l * G_N + G_SUB + 1]
                lam = gains[:, l * G_N + G_LAM:l * G_N + G_LAM + 1]
                now(v.tensor_tensor(lam, lam_exp[:, 2 * l + 1:2 * l + 2], lam_exp[:, 2 * l:2 * l + 1], ALU.subtract))
                v.tensor_scalar(lam, lam, -lam_init, None, ALU.add)
                now(v.tensor_scalar(sub, sub, 1.0 - lam_init, None, ALU.mult))
            for kind, t in enumerate((cos_d, sin_d, cos_m, sin_m)):
                fill(1 + KD + KD // 2 + kind, t[:, :])

            with ve.Fori(0, DEPTH) as l:
                begin(l, "N1")
                v.tensor_copy(gl[:, :], gains[:, bass.ds(l * G_N, G_N)]).then_inc(gl_ready.sem, 1)
                ve.wait_ge(gl_ready.sem, gl_ready.at(l, "N1", 0, 1))
                for k in range(KD):
                    ve.wait_ge(memh_hi.sem, memh_hi.at(l, "N1", 0, k + 1))
                    v.scalar_tensor_tensor(mem_lo[:, k, :], mem_n[:, k, :], gl[:, G_MEM + k:G_MEM + k + 1],
                                           mem_hi[:, k, :].bitcast(F32), ALU.mult, ALU.subtract).then_inc(memh_lo.sem, 1)
                rms(l, "N1", 0)
                chain(newton(rstd_x))
                chain(v.memset(q_sum[:, :], 0.0))
                end("N1")
                out_xq(l, 0)
                ve.wait_ge(mem_loaded.sem, mem_loaded.at(l, "H"))
                ve.wait_ge(mem_stored, 32)
                v.tensor_tensor(cos_d, cos_d, rstd_x[:, :], ALU.mult)
                v.tensor_tensor(sin_d, sin_d, rstd_x[:, :], ALU.mult)
                out_cq(l, 0, 2)
                memory_low(l, 0)
                with ve.Fori(0, CROSS - 1) as i:
                    begin(l, "C", i)
                    cross_prob(l, i)
                    out_xq(l, i + 1)
                    cross_low(l, i)
                    cross_out(l, i)
                    out_cq(l, i + 1)
                    memory_low(l, i + 1)
                    end("C")
                i = CROSS - 1
                begin(l, "C", i)
                cross_prob(l, i)
                end("C")
                begin(l, "A")

                def out_ckv(j):
                    ve.wait_ge(slot_done.sem, slot_done.at(l, "A", 0, j + 1))
                    v.tensor_tensor(ckv_raw[:, j, :], proj[j][:, :], rstd_x[:, :], ALU.mult).then_inc(ckv_copied.sem, 1)
                out_ckv(0)
                cross_low(l, i)
                rms(l, "A", 0)
                out_ckv(1)
                norm(l, "A", 0, cq_raw, G_Q, QT, cq_hi, cq_lo)
                cross_out(l, i)
                ve.wait_ge(slot_done.sem, slot_done.at(l, "A", 0, 4))
                chain(rope(mkT, proj[0], slice(64, 96), cos_m, sin_m, SHUF_M, (pair_lo, pair_lo.at(l, "A", 0, QT))))
                v.tensor_tensor(mkT[64:96, :], mkT[64:96, :], rstd_x[64:96, :], ALU.mult).then_inc(mla_ready.sem, 1)
                out_v(l, 0, 1)
                ve.wait_ge(mla_ready.sem, mla_ready.at(l, "A", 0, 1))
                rms(l, "A", 1)
                ve.wait_ge(ckv_squared.sem, ckv_squared.at(l, "A", 0, 2))
                norm(l, "A", QT, ckv_raw, G_KV, KVT, ckv_hi, ckv_lo)
                end("A")
                begin(l, "P")
                out_qk(l, 0, 1, 0, (pair_lo, pair_lo.at(l, "A", 0, QT + KVT)))
                query_low(l, 0)
                out_latent(l, 0, (qk_split, qk_split.at(l, "B", 0, 1)))
                out_qk(l, 0, 3, 0, (mla_ready, mla_ready.at(l, "B", 0, 1)))
                maxima(l, "B", 0, 0, "m", MLA_SCALE)
                key_low(l, 0)
                values_low(l, 0)
                end("P")
                with ve.Fori(0, HEADS // 2 - 1) as hp:
                    for e in range(2):
                        head(l, hp * 2 + e, hp * 2 + (e + 1))
                head(l, HEADS - 2, HEADS - 1)
                head(l, HEADS - 1, None)
                for k in range(EARLY, 16):
                    outs_low(l, k)
                with ve.Fori(0, 2) as jj:
                    begin(l, "E", jj)
                    for e in range(4):
                        ve.wait_ge(mix_ready.sem, mix_ready.at(l, "E", jj, e))
                        for g in range(3):
                            ve.wait_ge(slot_done.sem, slot_done.at(l, "E", jj, 5 * e + g + 1))
                            v.tensor_tensor(sig[:, g, :], proj[g % 2][:, :], rstd_x[:, :], ALU.mult).then_inc(gate_out.sem, 1)
                        ve.wait_ge(sig_ready.sem, sig_ready.at(l, "E", jj, 3 * e + 3))
                        ve.wait_ge(slot_done.sem, slot_done.at(l, "E", jj, 5 * e + 4))
                        ve.wait_ge(mix_split.sem, mix_split.at(l, "E", jj, e))
                        v.tensor_tensor(mix[:, :], proj[1][:, :], sig[:, 0, :], ALU.mult).then_inc(od_used.sem, 1)
                        ve.wait_ge(om_done.sem, om_done.at(l, "E", jj, e + 1))
                        v.tensor_tensor(sig[:, 1, :], proj[0][:, :], sig[:, 1, :], ALU.mult).then_inc(om_used.sem, 1)
                        ve.wait_ge(om_used.sem, om_used.at(l, "E", jj, e + 1))
                        chain(v.tensor_tensor(mix[:, :], mix[:, :], sig[:, 1, :], ALU.add))
                        ve.wait_ge(slot_done.sem, slot_done.at(l, "E", jj, 5 * e + 5))
                        v.tensor_tensor(sig[:, 2, :], proj[1][:, :], sig[:, 2, :], ALU.mult).then_inc(oc_used.sem, 1)
                        ve.wait_ge(oc_used.sem, oc_used.at(l, "E", jj, e + 1))
                        v.tensor_tensor(mix[:, :], mix[:, :], sig[:, 2, :], ALU.add).then_inc(mix_ready.sem, 1)
                        ve.wait_ge(mix_split_hi.sem, mix_split_hi.at(l, "E", jj, e + 1))
                        tile = jj * 4 + e
                        v.tensor_tensor(one(mix_lo, tile), mix[:, :], one(mix_hi, tile).bitcast(F32), ALU.subtract).then_inc(mix_split.sem, 1)
                    end("E")
                ve.wait_ge(x_loaded.sem, x_loaded.at(l, "E", 0, 16))
                v.memset(x_sum[:, :], 0.0)
                with ve.Fori(0, 2) as jj:
                    for e in range(4):
                        out_residual(l, "F", jj, e, e + 1, e % 2, jj * 4 + e, l * G_N + G_FFN)
                begin(l, "N2")
                rms(l, "N2", 0)
                chain(newton(rstd))
                v.memset(x_sum[:, :], 0.0)
                end("N2")

                def gate_up(t):
                    begin(l, "G", t)
                    for e in range(2):
                        ve.wait_ge(slot_done.sem, slot_done.at(l, "G", t, 2 * e + 1))
                        ve.wait_ge(gate_used.sem, gate_used.at(l, "G", t, e))
                        v.tensor_tensor(gate_n[:, :], proj[0][:, :], rstd[:, :], ALU.mult).then_inc(gate_read.sem, 1)
                        ve.wait_ge(silu_sig.sem, silu_sig.at(l, "G", t, e + 1))
                        ve.wait_ge(hid_split.sem, hid_split.at(l, "G", t, e))
                        v.tensor_tensor(gated[:, :], gate_n[:, :], sig_f[:, e, :], ALU.mult).then_inc(gate_used.sem, 1)
                        ve.wait_ge(gate_used.sem, gate_used.at(l, "G", t, e + 1))
                        chain(v.tensor_tensor(gated[:, :], gated[:, :], rstd[:, :], ALU.mult))
                        ve.wait_ge(slot_done.sem, slot_done.at(l, "G", t, 2 * e + 2))
                        v.tensor_tensor(hid[:, e, :], proj[1][:, :], gated[:, :], ALU.mult).then_inc(hid_ready.sem, 1)
                        ve.wait_ge(hid_split_hi.sem, hid_split_hi.at(l, "G", t, e + 1))
                        tile = t * 2 + e
                        v.tensor_tensor(one(hid_lo, tile), hid[:, e, :], one(hid_hi, tile).bitcast(F32), ALU.subtract).then_inc(hid_split.sem, 1)
                    end("G")
                gate_up(0)
                with ve.Fori(0, FT // 2 - 1) as t:
                    gate_up(t + 1)
                with ve.Fori(0, 4) as jj:
                    for e in range(2):
                        out_residual(l, "H", jj, e, 4 * e + 4, e, jj * 2 + e, (l + 1) * G_N + G_ATTN)
            for k in range(KD):
                c = DEPTH * G_N + k
                v.tensor_scalar(y_T[:, k, :], xT[:, k, :], gains[:, c:c + 1], None, ALU.mult).then_inc(y_ready, 1)
            ve.wait_ge(rms_ready.sem, rms_ready.end(DEPTH) + 1)
            state["origin"], state["n"] = vec_step.end(DEPTH), 0
            newton(rstd, NT).then_inc(y_ready, 1)
            ve.wait_ge(y_ready, KD + 1)
            for n in range(0, 2 * NT, 2):
                half, t = n // NT, n % NT
                ve.wait_ge(y_flipped, n + 1)
                v.tensor_scalar(y_out[:, t, half * 512:(half + 1) * 512], flip[0][:, :], rstd[:, t:t + 1], None, ALU.mult).then_inc(y_copied[0], 1)


def kernel(**inputs):
    import concourse.bacc as bacc
    from concourse.bass_utils import run_bass_kernel_spmd

    names = ["x", "mem", "positions", "attn_norm_w", "w_in", "diff_lambda", "diff_subln_w", "w_o_diff", "mla_q_norm_w",
             "mla_w_uq", "mla_kv_norm_w", "mla_w_ukv", "w_o_mla", "mem_norm_w", "w_mem_kv", "w_o_cross", "w_out",
             "ffn_norm_w", "w_gate_up", "w_down", "final_norm_w"]
    nc = bacc.Bacc("TRN2", target_bir_lowering=False, num_devices=1)
    arrays, args = {}, []
    for name in names:
        a = np.ascontiguousarray(inputs[name])
        arrays[f"in_{name}"] = a
        args.append(nc.dram_tensor(f"in_{name}", a.shape, mybir.dt.from_np(a.dtype), kind="ExternalInput").ap())
    args.append(nc.dram_tensor("out", (1, SEQ, D), F32, kind="ExternalOutput").ap())
    args.append(nc.dram_tensor("mem_scratch", (P, KD, MEM), F32, kind="Internal").ap())
    args.append(nc.dram_tensor("table_scratch", (P, 2, SEQ), F32, kind="Internal").ap())
    args.append(nc.dram_tensor("x_scratch", (P, KD, SEQ), F32, kind="Internal").ap())
    build_trunk(nc, *args)
    r = run_bass_kernel_spmd(nc, [arrays], core_ids=[0])
    return r.results[0]["out"]
```
